# Optimizing a Trainium2 kernel written in Bass

```python
import jax, jax.numpy as jnp
from jax import lax
import numpy as np

D_MODEL = 1024
BATCH = 1
SEQ = 256
DEPTH = 1

N_META = 16
CHUNK = 64
N_PAD = CHUNK - N_META
GLA_HEADS = 4
GLA_DK = 128
GLA_DV = 256
GLA_KEY = GLA_HEADS * GLA_DK
GLA_VAL = GLA_HEADS * GLA_DV
GATE_RANK = 16
GATE_TAU = 16.0
SSM_WIDTH = D_MODEL
SSM_GROUP = 16
SSM_GROUPS = SSM_WIDTH // SSM_GROUP
SSM_STATE = 64
D_FF = 4 * D_MODEL
EPS = 1e-6

Q_END = GLA_KEY
K_END = Q_END + GLA_KEY
V_END = K_END + GLA_VAL
R_END = V_END + GLA_VAL
A_END = R_END + GATE_RANK
U_END = A_END + SSM_WIDTH
G1_END = U_END + D_MODEL
IN_WIDTH = G1_END + D_MODEL


def rmsnorm(x, g):
    xf = x.astype(jnp.float32)
    ms = jnp.mean(xf * xf, axis=-1, keepdims=True)
    return (xf * lax.rsqrt(ms + EPS) * g.astype(jnp.float32)).astype(x.dtype)

def gla_chunked(q, k, v, log_a):
    bsz, p, h, dk = q.shape
    dv = v.shape[-1]
    nc = p // CHUNK

    def to_chunks(t):
        return t.reshape(bsz, nc, CHUNK, h, t.shape[-1]).transpose(1, 0, 3, 2, 4)

    qc, kc, vc = to_chunks(q), to_chunks(k), to_chunks(v)
    b = jnp.cumsum(to_chunks(log_a).astype(jnp.float32), axis=3)
    b_ref = b[:, :, :, CHUNK // 2:CHUNK // 2 + 1, :]
    q_in = qc * jnp.exp(b - b_ref)
    k_in = kc * jnp.exp(b_ref - b)
    mask = jnp.tril(jnp.ones((CHUNK, CHUNK), dtype=bool))
    scores = jnp.where(mask, jnp.einsum('nbhid,nbhjd->nbhij', q_in, k_in), 0.0)
    o_intra = jnp.einsum('nbhij,nbhjv->nbhiv', scores, vc.astype(jnp.float32))

    b_last = b[:, :, :, -1:, :]
    q_inter = qc * jnp.exp(b)
    k_state = kc * jnp.exp(b_last - b)
    decay_chunk = jnp.exp(b_last[:, :, :, 0, :])

    def step(state, inp):
        qi, ks, vv, dc = inp
        o = jnp.einsum('bhid,bhdv->bhiv', qi, state)
        new_state = dc[..., None] * state + jnp.einsum('bhjd,bhjv->bhdv', ks, vv.astype(jnp.float32))
        return new_state, o

    s0 = jnp.zeros((bsz, h, dk, dv), jnp.float32)
    _, o_inter = lax.scan(step, s0, (q_inter, k_state, vc, decay_chunk))
    o = (o_intra + o_inter).transpose(1, 0, 3, 2, 4).reshape(bsz, p, h, dv)
    return o.astype(v.dtype)

def _complex_combine(e1, e2):
    a1r, a1i, b1r, b1i = e1
    a2r, a2i, b2r, b2i = e2
    return (a2r * a1r - a2i * a1i,
            a2r * a1i + a2i * a1r,
            a2r * b1r - a2i * b1i + b2r,
            a2r * b1i + a2i * b1r + b2i)

def s5_ssm(u, a_re, a_im, log_step, b_re, b_im, c_re, c_im, d_skip):
    bsz, p, _ = u.shape
    g, n, hg = SSM_GROUPS, SSM_STATE, SSM_GROUP
    ar = a_re.astype(jnp.float32)
    ai = a_im.astype(jnp.float32)
    dt = jnp.exp(log_step.astype(jnp.float32))[:, None]
    mag = jnp.exp(ar * dt)
    lam_re, lam_im = mag * jnp.cos(ai * dt), mag * jnp.sin(ai * dt)
    zr, zi = lam_re - 1.0, lam_im
    den = ar * ar + ai * ai
    fr = (zr * ar + zi * ai) / den
    fi = (zi * ar - zr * ai) / den
    br, bi = b_re.astype(jnp.float32), b_im.astype(jnp.float32)
    bb_re = fr[..., None] * br - fi[..., None] * bi
    bb_im = fr[..., None] * bi + fi[..., None] * br
    cr, ci = c_re.astype(jnp.float32), c_im.astype(jnp.float32)

    nc = p // CHUNK
    uc = u.reshape(bsz, nc, CHUNK, g, hg).transpose(1, 0, 2, 3, 4)
    lam_b_re = jnp.broadcast_to(lam_re, (bsz, CHUNK, g, n))
    lam_b_im = jnp.broadcast_to(lam_im, (bsz, CHUNK, g, n))

    def step(carry, u_blk):
        h_re, h_im = carry
        uf = u_blk.astype(jnp.float32)
        bu_re = jnp.einsum('bcgh,gnh->bcgn', uf, bb_re)
        bu_im = jnp.einsum('bcgh,gnh->bcgn', uf, bb_im)
        acc_re, acc_im, x_re, x_im = lax.associative_scan(
            _complex_combine, (lam_b_re, lam_b_im, bu_re, bu_im), axis=1)
        s_re = x_re + acc_re * h_re[:, None] - acc_im * h_im[:, None]
        s_im = x_im + acc_re * h_im[:, None] + acc_im * h_re[:, None]
        y = jnp.einsum('bcgn,ghn->bcgh', s_re, cr) - jnp.einsum('bcgn,ghn->bcgh', s_im, ci)
        return (s_re[:, -1], s_im[:, -1]), y

    carry0 = (jnp.zeros((bsz, g, n), jnp.float32), jnp.zeros((bsz, g, n), jnp.float32))
    _, y = lax.scan(step, carry0, uc)
    y = y.transpose(1, 0, 2, 3, 4).reshape(bsz, p, g * hg)
    return (y + d_skip.astype(jnp.float32) * u.astype(jnp.float32)).astype(u.dtype)

def first_inputs(seed: int = 0) -> dict:
    key = jax.random.key(seed)
    ks = jax.random.split(key, 24)
    nrm = lambda k, shape, s: jax.random.normal(k, shape, jnp.float32) * s
    gain = lambda k, shape: 1.0 + 0.05 * jax.random.normal(k, shape, jnp.float32)
    L = DEPTH
    x = jax.random.normal(ks[0], (BATCH, SEQ, D_MODEL), jnp.float32)
    meta_tokens = nrm(ks[1], (N_META, D_MODEL), 1.0)
    g_mix_pre = gain(ks[2], (L, D_MODEL))
    w_in = nrm(ks[3], (L, D_MODEL, IN_WIDTH), D_MODEL ** -0.5)
    w_gate_up = nrm(ks[4], (L, GATE_RANK, GLA_KEY), GATE_RANK ** -0.5)
    b_gate = 1.0 + 0.5 * jax.random.normal(ks[5], (L, GLA_KEY), jnp.float32)
    gla_norm_g = gain(ks[6], (L, GLA_HEADS, GLA_DV))
    w_o_gla = nrm(ks[7], (L, GLA_VAL, D_MODEL), GLA_VAL ** -0.5)
    n_idx = jnp.arange(SSM_STATE, dtype=jnp.float32)
    a_re = -0.5 + 0.01 * jax.random.normal(ks[8], (L, SSM_GROUPS, SSM_STATE), jnp.float32)
    a_im = jnp.broadcast_to(jnp.pi * n_idx, (L, SSM_GROUPS, SSM_STATE)) + 0.0
    log_step = jax.random.uniform(ks[9], (L, SSM_GROUPS), jnp.float32,
                                  minval=float(np.log(1e-3)), maxval=float(np.log(1e-1)))
    b_re = nrm(ks[10], (L, SSM_GROUPS, SSM_STATE, SSM_GROUP), (2 * SSM_GROUP) ** -0.5)
    b_im = nrm(ks[11], (L, SSM_GROUPS, SSM_STATE, SSM_GROUP), (2 * SSM_GROUP) ** -0.5)
    c_re = nrm(ks[12], (L, SSM_GROUPS, SSM_GROUP, SSM_STATE), (2 * SSM_STATE) ** -0.5)
    c_im = nrm(ks[13], (L, SSM_GROUPS, SSM_GROUP, SSM_STATE), (2 * SSM_STATE) ** -0.5)
    d_skip = nrm(ks[14], (L, SSM_WIDTH), 1.0)
    w_glu = nrm(ks[15], (L, SSM_WIDTH, 2 * D_MODEL), SSM_WIDTH ** -0.5)
    b_glu = nrm(ks[16], (L, 2 * D_MODEL), 0.02)
    w_out = nrm(ks[17], (L, D_MODEL, D_MODEL), D_MODEL ** -0.5)
    g_mix_post = gain(ks[18], (L, D_MODEL))
    g_ffn_pre = gain(ks[19], (L, D_MODEL))
    w_ff1 = nrm(ks[20], (L, D_MODEL, D_FF), D_MODEL ** -0.5)
    w_ff2 = nrm(ks[21], (L, D_FF, D_MODEL), D_FF ** -0.5)
    g_ffn_post = gain(ks[22], (L, D_MODEL))
    return {"x": x, "meta_tokens": meta_tokens, "g_mix_pre": g_mix_pre, "w_in": w_in,
            "w_gate_up": w_gate_up, "b_gate": b_gate, "gla_norm_g": gla_norm_g, "w_o_gla": w_o_gla,
            "a_re": a_re, "a_im": a_im, "log_step": log_step, "b_re": b_re, "b_im": b_im,
            "c_re": c_re, "c_im": c_im, "d_skip": d_skip, "w_glu": w_glu, "b_glu": b_glu,
            "w_out": w_out, "g_mix_post": g_mix_post, "g_ffn_pre": g_ffn_pre, "w_ff1": w_ff1,
            "w_ff2": w_ff2, "g_ffn_post": g_ffn_post}

def first_block(x, meta_tokens, g_mix_pre, w_in, w_gate_up, b_gate, gla_norm_g, w_o_gla,
              a_re, a_im, log_step, b_re, b_im, c_re, c_im, d_skip, w_glu, b_glu,
              w_out, g_mix_post, g_ffn_pre, w_ff1, w_ff2, g_ffn_post):
    bsz, seq, dm = x.shape
    meta = jnp.broadcast_to(meta_tokens.astype(x.dtype)[None], (bsz, N_META, dm))
    h = jnp.concatenate([meta, x], axis=1)
    p = N_PAD + N_META + seq

    def pad(t):
        return jnp.pad(t, ((0, 0), (N_PAD, 0), (0, 0)))

    def heads(t, d):
        return t.reshape(bsz, p, GLA_HEADS, d)

    for l in range(DEPTH):
        xn = rmsnorm(h, g_mix_pre[l])
        proj = xn @ w_in[l]
        q = proj[..., :Q_END]
        k = proj[..., Q_END:K_END]
        v = proj[..., K_END:V_END]
        r = proj[..., V_END:R_END]
        a_low = proj[..., R_END:A_END]
        u = proj[..., A_END:U_END]
        z_gla = proj[..., U_END:G1_END]
        z_ssm = proj[..., G1_END:]

        log_a = jax.nn.log_sigmoid((a_low @ w_gate_up[l] + b_gate[l]).astype(jnp.float32)) / GATE_TAU
        o = gla_chunked(heads(pad(q), GLA_DK) * (GLA_DK ** -0.5), heads(pad(k), GLA_DK),
                        heads(pad(v), GLA_DV), heads(pad(log_a), GLA_DK))[:, N_PAD:]
        o = rmsnorm(o, gla_norm_g[l]).reshape(bsz, N_META + seq, GLA_VAL) * jax.nn.silu(r)
        y_gla = o @ w_o_gla[l]

        y_s = s5_ssm(pad(u), a_re[l], a_im[l], log_step[l], b_re[l], b_im[l],
                     c_re[l], c_im[l], d_skip[l])[:, N_PAD:]
        g_s = jax.nn.gelu(y_s)
        glu = g_s @ w_glu[l] + b_glu[l]
        y_ssm = glu[..., :D_MODEL] * jax.nn.sigmoid(glu[..., D_MODEL:])

        mixed = jax.nn.sigmoid(z_gla) * y_gla + jax.nn.sigmoid(z_ssm) * y_ssm
        h = h + rmsnorm(mixed @ w_out[l], g_mix_post[l])

        hn = rmsnorm(h, g_ffn_pre[l])
        f = jnp.square(jax.nn.relu(hn @ w_ff1[l])) @ w_ff2[l]
        h = h + rmsnorm(f, g_ffn_post[l])

    return h[:, N_META:]


MEM_LEN = 256

M_HEADS = 4
M_DV = D_MODEL // 8
M_DQK = M_DV // 2
M_CONV = 4
M_CHUNK = 64

A_HEADS = 8
A_KV_HEADS = 2
A_DH = 64
WINDOW = 128
A_BLOCK = 128

X_HEADS = 4
X_DH = D_MODEL // X_HEADS

P_HEADS = 8
P_NKEYS = 128
P_EXPERTS = P_NKEYS * P_NKEYS
P_KEY_DIM = 128
P_TOPK = 16
P_TOKEN_BLOCK = 128

IN_SIZES = (M_HEADS * M_DQK, M_HEADS * M_DQK, M_HEADS * M_DV, M_HEADS * M_DV, M_HEADS, M_HEADS,
            A_HEADS * A_DH, A_KV_HEADS * A_DH, A_KV_HEADS * A_DH)
P_IN = sum(IN_SIZES)
MIX_WIDTH = M_HEADS * M_DV + A_HEADS * A_DH


def rmsnorm_2(x, g):
    xf = x.astype(jnp.float32)
    y = xf * lax.rsqrt(jnp.mean(xf * xf, axis=-1, keepdims=True) + EPS)
    return (y * g.astype(jnp.float32)).astype(x.dtype)

def causal_depthwise_conv(x, w, b):
    y = lax.conv_general_dilated(
        x, w[:, None, :].astype(x.dtype), window_strides=(1,),
        padding=[(w.shape[0] - 1, 0)], dimension_numbers=('NWC', 'WIO', 'NWC'),
        feature_group_count=x.shape[-1])
    return y + b.astype(x.dtype)

def mlstm_chunkwise(q, k, v, i_pre, f_pre):
    B, S, H, _ = q.shape
    L = M_CHUNK
    nc = S // L
    f32 = jnp.float32

    def chunks(t):
        t = t.astype(f32).reshape((B, nc, L, H) + t.shape[3:])
        return jnp.moveaxis(t, (1, 3), (0, 2))

    qc = chunks(q) * (M_DQK ** -0.5)
    kc = chunks(k)
    vc = chunks(v)
    ic = chunks(i_pre)
    lfc = chunks(jax.nn.log_sigmoid(f_pre.astype(f32)))
    causal = jnp.tril(jnp.ones((L, L), dtype=bool))

    def step(carry, inp):
        C, n, m = carry
        qb, kb, vb, ib, lfb = inp
        b = jnp.cumsum(lfb, axis=-1)
        log_d = jnp.where(causal, b[..., :, None] - b[..., None, :] + ib[..., None, :], -jnp.inf)
        inter = b + m[..., None]
        m_t = jnp.maximum(inter, jnp.max(log_d, axis=-1))
        d = jnp.exp(log_d - m_t[..., None])
        s = jnp.einsum('bhtk,bhsk->bhts', qb, kb) * d
        w_inter = jnp.exp(inter - m_t)
        num = jnp.einsum('bhts,bhsv->bhtv', s, vb) + w_inter[..., None] * jnp.einsum('bhvk,bhtk->bhtv', C, qb)
        den = jnp.sum(s, axis=-1) + w_inter * jnp.einsum('bhk,bhtk->bht', n, qb)
        h = num / jnp.maximum(jnp.abs(den), jnp.exp(-m_t))[..., None]
        m_new = m_t[..., -1]
        w = jnp.exp(b[..., -1:] - b + ib - m_new[..., None])
        decay = jnp.exp(b[..., -1] + m - m_new)
        C_new = decay[..., None, None] * C + jnp.einsum('bhs,bhsv,bhsk->bhvk', w, vb, kb)
        n_new = decay[..., None] * n + jnp.einsum('bhs,bhsk->bhk', w, kb)
        return (C_new, n_new, m_new), h

    init = (jnp.zeros((B, H, M_DV, M_DQK), f32), jnp.zeros((B, H, M_DQK), f32), jnp.zeros((B, H), f32))
    _, h = lax.scan(step, init, (qc, kc, vc, ic, lfc))
    h = jnp.moveaxis(h, (0, 2), (1, 3)).reshape(B, S, H, M_DV)
    return h.astype(v.dtype)

def sliding_window_gqa_sinks(q, k, v, sinks):
    B, S, Hq, dh = q.shape
    Hkv = k.shape[2]
    G = Hq // Hkv
    nb = S // A_BLOCK
    f32 = jnp.float32
    qb = q.astype(f32).reshape(B, nb, A_BLOCK, Hkv, G, dh)

    def band_blocks(t):
        t = t.astype(f32)
        prev = jnp.concatenate([jnp.zeros_like(t[:, :A_BLOCK]), t[:, :S - A_BLOCK]], axis=1)
        return jnp.concatenate([prev.reshape(B, nb, A_BLOCK, Hkv, dh),
                                t.reshape(B, nb, A_BLOCK, Hkv, dh)], axis=2)

    kb = band_blocks(k)
    vb = band_blocks(v)
    qi = jnp.arange(A_BLOCK)[:, None]
    kj = jnp.arange(2 * A_BLOCK)[None, :]
    diff = qi - kj + A_BLOCK
    band = (diff >= 0) & (diff < WINDOW)
    exists = (jnp.arange(nb)[:, None, None] > 0) | (kj >= A_BLOCK)[None]
    mask = band[None] & exists

    scores = jnp.einsum('bnqhgd,bnkhd->bnhgqk', qb, kb) * (dh ** -0.5)
    scores = jnp.where(mask[None, :, None, None], scores, -jnp.inf)
    sink = sinks.astype(f32).reshape(Hkv, G)[None, None, :, :, None, None]
    mx = jnp.maximum(jnp.max(scores, axis=-1, keepdims=True), sink)
    p = jnp.exp(scores - mx)
    probs = p / (jnp.sum(p, axis=-1, keepdims=True) + jnp.exp(sink - mx))
    out = jnp.einsum('bnhgqk,bnkhd->bnqhgd', probs, vb)
    return out.reshape(B, S, Hq * dh).astype(q.dtype)

def memory_cross_attention(xn, memn, w_q, w_k, w_v, w_o):
    B, S, D = xn.shape
    M = memn.shape[1]
    f32 = jnp.float32
    q = (xn @ w_q).reshape(B, S, X_HEADS, X_DH).astype(f32)
    k = (memn @ w_k).reshape(B, M, X_HEADS, X_DH).astype(f32)
    v = (memn @ w_v).reshape(B, M, X_HEADS, X_DH).astype(f32)
    p = jax.nn.softmax(jnp.einsum('bshd,bmhd->bhsm', q, k) * (X_DH ** -0.5), axis=-1)
    o = jnp.einsum('bhsm,bmhd->bshd', p, v).reshape(B, S, X_HEADS * X_DH).astype(xn.dtype)
    return o @ w_o

def peer_ffn(xn, w_pq, sub_keys1, sub_keys2, expert_down, expert_up):
    B, S, D = xn.shape
    T = P_TOKEN_BLOCK
    xt = xn.reshape(-1, T, D)

    def block(xb):
        qh = (xb @ w_pq).reshape(T, P_HEADS, 2, P_KEY_DIM).astype(jnp.float32)
        s1 = jnp.einsum('thd,nd->thn', qh[:, :, 0], sub_keys1.astype(jnp.float32))
        s2 = jnp.einsum('thd,nd->thn', qh[:, :, 1], sub_keys2.astype(jnp.float32))
        v1, i1 = lax.top_k(s1, P_TOPK)
        v2, i2 = lax.top_k(s2, P_TOPK)
        cand_s = (v1[..., :, None] + v2[..., None, :]).reshape(T, P_HEADS, P_TOPK * P_TOPK)
        cand_i = (i1[..., :, None] * P_NKEYS + i2[..., None, :]).reshape(T, P_HEADS, P_TOPK * P_TOPK)
        top_s, pos = lax.top_k(cand_s, P_TOPK)
        eidx = jnp.take_along_axis(cand_i, pos, axis=-1)
        g = jax.nn.softmax(top_s, axis=-1)
        u = expert_down[eidx]
        a = jax.nn.gelu(jnp.einsum('thkd,td->thk', u, xb), approximate=False)
        coef = (g * a.astype(jnp.float32)).astype(xb.dtype)
        return jnp.einsum('thk,thkd->td', coef, expert_up[eidx])

    return lax.map(block, xt).reshape(B, S, D)

def second_inputs(seed: int = 0) -> dict:
    key = jax.random.key(seed)
    ks = jax.random.split(key, 24)
    f32 = jnp.float32

    def nrm(k, shape, scale):
        return jax.random.normal(k, shape, f32) * scale

    Dn = D_MODEL ** -0.5
    qk_ch = 2 * M_HEADS * M_DQK
    return {
        "x": nrm(ks[0], (BATCH, SEQ, D_MODEL), 1.0),
        "mem": nrm(ks[1], (BATCH, MEM_LEN, D_MODEL), 1.0),
        "g_mix": 1.0 + nrm(ks[2], (DEPTH, D_MODEL), 0.02),
        "w_in": nrm(ks[3], (DEPTH, D_MODEL, P_IN), Dn),
        "conv_w": nrm(ks[4], (DEPTH, M_CONV, qk_ch), M_CONV ** -0.5),
        "conv_b": nrm(ks[5], (DEPTH, qk_ch), 0.02),
        "b_igate": nrm(ks[6], (DEPTH, M_HEADS), 0.1),
        "b_fgate": jnp.linspace(3.0, 6.0, M_HEADS, dtype=f32)[None] + nrm(ks[7], (DEPTH, M_HEADS), 0.1),
        "g_mhead": 1.0 + nrm(ks[8], (DEPTH, M_HEADS * M_DV), 0.02),
        "sinks": nrm(ks[9], (DEPTH, A_HEADS), 0.5),
        "w_out": nrm(ks[10], (DEPTH, MIX_WIDTH, D_MODEL), MIX_WIDTH ** -0.5),
        "g_cross": 1.0 + nrm(ks[11], (DEPTH, D_MODEL), 0.02),
        "g_mem": 1.0 + nrm(ks[12], (DEPTH, D_MODEL), 0.02),
        "w_xq": nrm(ks[13], (DEPTH, D_MODEL, X_HEADS * X_DH), Dn),
        "w_xk": nrm(ks[14], (DEPTH, D_MODEL, X_HEADS * X_DH), Dn),
        "w_xv": nrm(ks[15], (DEPTH, D_MODEL, X_HEADS * X_DH), Dn),
        "w_xo": nrm(ks[16], (DEPTH, X_HEADS * X_DH, D_MODEL), (X_HEADS * X_DH) ** -0.5),
        "g_ffn": 1.0 + nrm(ks[17], (DEPTH, D_MODEL), 0.02),
        "w_pq": nrm(ks[18], (DEPTH, D_MODEL, P_HEADS * 2 * P_KEY_DIM), Dn),
        "sub_keys1": nrm(ks[19], (DEPTH, P_NKEYS, P_KEY_DIM), P_KEY_DIM ** -0.5),
        "sub_keys2": nrm(ks[20], (DEPTH, P_NKEYS, P_KEY_DIM), P_KEY_DIM ** -0.5),
        "expert_down": nrm(ks[21], (DEPTH, P_EXPERTS, D_MODEL), Dn),
        "expert_up": nrm(ks[22], (DEPTH, P_EXPERTS, D_MODEL), Dn),
        "g_final": 1.0 + nrm(ks[23], (D_MODEL,), 0.02),
    }

def second_block(x, mem, g_mix, w_in, conv_w, conv_b, b_igate, b_fgate, g_mhead, sinks, w_out,
              g_cross, g_mem, w_xq, w_xk, w_xv, w_xo, g_ffn, w_pq, sub_keys1, sub_keys2,
              expert_down, expert_up, g_final):
    B, S, _ = x.shape
    split_points = [int(c) for c in np.cumsum(IN_SIZES)[:-1]]
    h = x
    for l in range(DEPTH):
        xn = rmsnorm_2(h, g_mix[l])
        proj = xn @ w_in[l]
        mq, mk, mv, mo, mi, mf, aq, ak, av = jnp.split(proj, split_points, axis=-1)
        qk = jax.nn.silu(causal_depthwise_conv(jnp.concatenate([mq, mk], axis=-1), conv_w[l], conv_b[l]))
        mq, mk = jnp.split(qk, 2, axis=-1)
        hm = mlstm_chunkwise(mq.reshape(B, S, M_HEADS, M_DQK), mk.reshape(B, S, M_HEADS, M_DQK),
                             mv.reshape(B, S, M_HEADS, M_DV),
                             mi + b_igate[l].astype(mi.dtype), mf + b_fgate[l].astype(mf.dtype))
        hm = rmsnorm_2(hm, g_mhead[l].reshape(M_HEADS, M_DV)).reshape(B, S, M_HEADS * M_DV)
        hm = (jax.nn.sigmoid(mo) * hm).astype(x.dtype)
        ha = sliding_window_gqa_sinks(aq.reshape(B, S, A_HEADS, A_DH), ak.reshape(B, S, A_KV_HEADS, A_DH),
                                      av.reshape(B, S, A_KV_HEADS, A_DH), sinks[l])
        h = h + jnp.concatenate([hm, ha], axis=-1) @ w_out[l]
        h = h + memory_cross_attention(rmsnorm_2(h, g_cross[l]), rmsnorm_2(mem, g_mem[l]),
                                       w_xq[l], w_xk[l], w_xv[l], w_xo[l])
        h = h + peer_ffn(rmsnorm_2(h, g_ffn[l]), w_pq[l], sub_keys1[l], sub_keys2[l],
                         expert_down[l], expert_up[l])
    return rmsnorm_2(h, g_final)


def setup_inputs(seed=0):
    out = dict(first_inputs(seed))
    for name, value in second_inputs(seed + 1).items():
        if name != "x":
            out[name + "_2"] = value
    return out


def reference(
    x, meta_tokens, g_mix_pre, w_in, w_gate_up, b_gate, gla_norm_g, w_o_gla, a_re, a_im,
    log_step, b_re, b_im, c_re, c_im, d_skip, w_glu, b_glu, w_out, g_mix_post, g_ffn_pre, w_ff1,
    w_ff2, g_ffn_post, mem_2, g_mix_2, w_in_2, conv_w_2, conv_b_2, b_igate_2, b_fgate_2,
    g_mhead_2, sinks_2, w_out_2, g_cross_2, g_mem_2, w_xq_2, w_xk_2, w_xv_2, w_xo_2, g_ffn_2,
    w_pq_2, sub_keys1_2, sub_keys2_2, expert_down_2, expert_up_2, g_final_2,
):
    x = first_block(
        x, meta_tokens, g_mix_pre, w_in, w_gate_up, b_gate, gla_norm_g, w_o_gla, a_re, a_im,
        log_step, b_re, b_im, c_re, c_im, d_skip, w_glu, b_glu, w_out, g_mix_post, g_ffn_pre,
        w_ff1, w_ff2, g_ffn_post,
    )
    return second_block(
        x, mem_2, g_mix_2, w_in_2, conv_w_2, conv_b_2, b_igate_2, b_fgate_2, g_mhead_2, sinks_2,
        w_out_2, g_cross_2, g_mem_2, w_xq_2, w_xk_2, w_xv_2, w_xo_2, g_ffn_2, w_pq_2,
        sub_keys1_2, sub_keys2_2, expert_down_2, expert_up_2, g_final_2,
    )


_drawn_inputs = setup_inputs


def setup_inputs(seed=0):
    import zlib

    import numpy as np

    out = dict(_drawn_inputs(seed))
    spreads = {}
    factors = {'a_re': 8.0,
     'b_re': 3.515,
     'b_im': 3.522,
     'c_re': 3.534,
     'c_im': 3.562,
     'b_glu': 4.306,
     'g_mix_2': 7.583,
     'conv_b_2': 8.0,
     'b_igate_2': 200.0,
     'g_mhead_2': 8.0,
     'sinks_2': 8.0,
     'g_cross_2': 8.0,
     'g_mem_2': 8.0,
     'g_ffn_2': 8.0,
     'w_pq_2': 6.686,
     'sub_keys1_2': 6.816,
     'sub_keys2_2': 6.85,
     'expert_down_2': 7.399,
     'expert_up_2': 6.68,
     'g_final_2': 23.064}
    for name, (base, spread) in spreads.items():
        noise = np.random.default_rng([zlib.crc32(name.encode()), seed]).standard_normal(out[name].shape)
        drawn = base * np.exp(spread * noise) if base else spread * noise
        out[name] = __import__('jax').numpy.asarray(drawn.astype(out[name].dtype))
    for name, factor in factors.items():
        out[name] = (out[name] * factor).astype(out[name].dtype)
    return out
```

```python
from contextlib import ExitStack

import numpy as np
import concourse.bass as bass
from concourse import mybir

F32 = mybir.dt.float32
I32 = mybir.dt.int32
U32 = mybir.dt.uint32
ALU = mybir.AluOpType
ACT = mybir.ActivationFunctionType
AX = mybir.AxisListType

P = 128
D = 1024
KT = D // P
EPS = 1e-6
SEQ, META = 256, 16
T1 = META + SEQ
T2 = SEQ
CW = 256
RING = 4
FF = 4 * D
GH, GDK, GDV, GCH = 4, 128, 256, 64
GSTART = [0] + [META + GCH * i for i in range(SEQ // GCH)]
TOK1 = [(0, META), (META, P), (META + P, P)]
SG, SN, SHG = 64, 64, 16
ST = SG * SN // P
SHALF = 8
MH, MQK, MV = 4, 64, 128
AH, AKV, ADH = 8, 2, 64
XH, XD = 4, 256
PH, PK, PTOP, PEXP = 8, 128, 16, 128 * 128

MQK_SCALE = MQK ** -0.5
MAGIC = 1.5 * 2.0 ** 23
NEG = -1.0e30
MAXNEG = -3.0e38

COLS = {}
_n = 0
for _name, _w in [("g_mix_pre", 8), ("g_mix_post", 8), ("g_ffn_pre", 8), ("g_ffn_post", 8), ("b_gate", 4),
                  ("gla_norm_g", 8), ("d_skip", 8), ("b_glu", 16), ("g_mix_2", 8), ("conv_w_2", 16),
                  ("conv_b_2", 4), ("g_mhead_2", 4), ("g_cross_2", 8), ("g_mem_2", 8), ("g_ffn_2", 8),
                  ("b_igate_2", 1), ("b_fgate_2", 1), ("sinks_2", 8)]:
    COLS[_name] = (_n, _w)
    _n += _w
NCOLS = _n

STREAM = [("u", 4), ("qk", 4), ("r", 4), ("zg", 4), ("zs", 4), ("v", 4), ("w_glu", 8), ("w_o_gla", 4),
          ("w_out", 4), ("w_ff1", 16), ("w_ff2", 16),
          ("xk", 4), ("xv", 4), ("mqk_mo", 4), ("aq_mv", 4), ("w_out_2", 4), ("xq", 4), ("xo", 4), ("pq", 8)]
FIRST = {}
_n = 0
for _name, _w in STREAM:
    FIRST[_name] = _n
    _n += _w
NCHUNK = _n


def layout(x):
    c = np.ascontiguousarray
    w1, w2 = x["w_in"][0], x["w_in_2"][0]
    b = np.cumsum([0, 512, 512, 1024, 1024, 16, 1024, 1024, 1024])
    q, k, v, r, al, u, zg, zs = (w1[:, b[i]:b[i + 1]] for i in range(8))
    b2 = np.cumsum([0, 256, 256, 512, 512, 4, 4, 512, 128, 128])
    mq, mk, mv, mo, mi, mf, aq, ak, av = (w2[:, b2[i]:b2[i + 1]] for i in range(9))
    pair = np.arange(AH).reshape(2, 4).T.reshape(-1)
    aqp = aq.reshape(D, AH, ADH)[:, pair].reshape(D, -1)
    wo2 = x["w_out_2"][0]
    wo2 = np.concatenate([wo2[:512], wo2[512:].reshape(AH, ADH, D)[pair].reshape(-1, D)])

    def chunks(m):
        kk, n = m.shape
        return m.reshape(kk // D, KT, P, n // CW, CW).transpose(3, 0, 2, 1, 4).reshape(-1, P, KT * CW)
    g = {"u": u, "qk": np.concatenate([q, k], 1), "r": r, "zg": zg, "zs": zs, "v": v, "w_glu": x["w_glu"][0],
         "w_o_gla": x["w_o_gla"][0], "w_out": x["w_out"][0], "w_ff1": x["w_ff1"][0], "w_ff2": x["w_ff2"][0],
         "xk": x["w_xk_2"][0], "xv": x["w_xv_2"][0], "mqk_mo": np.concatenate([mq, mk, mo], 1),
         "aq_mv": np.concatenate([aqp, mv], 1), "w_out_2": wo2, "xq": x["w_xq_2"][0], "xo": x["w_xo_2"][0],
         "pq": x["w_pq_2"][0]}
    fm = lambda m: m.reshape(-1, KT, P).transpose(2, 1, 0)

    table = np.zeros((P, NCOLS), np.float32)
    for name, (at, n) in COLS.items():
        v0 = x[name].reshape(-1)
        if name == "conv_w_2":
            table[:, at:at + n] = x[name][0].reshape(4, 4, P).transpose(2, 1, 0).reshape(P, 16)
        elif name in ("b_igate_2", "b_fgate_2"):
            table[0:4, at] = v0
        elif name == "sinks_2":
            table[:, at:at + n] = v0[None, pair]
        else:
            table[:, at:at + n] = v0.reshape(n, P).T
    h = np.concatenate([x["meta_tokens"], x["x"][0]], 0)
    cre, cim = (x[n][0].reshape(ST, 2, SHG, SN) for n in ("c_re", "c_im"))

    def cmat(m):
        o = np.zeros((2, SN, ST, 2, SHG), np.float32)
        for i in range(2):
            o[i, :, :, i, :] = m[:, i].transpose(2, 0, 1)
        return o.reshape(P, ST, 2 * SHG)

    def bmat(m):
        m = m.reshape(8, 4, 2, SN, SHG)
        o = np.zeros((4, 2, SHG, 8, 2, SN), np.float32)
        for i in range(2):
            o[:, i, :, :, i, :] = m[:, :, i].transpose(1, 3, 0, 2)
        return o.reshape(P, 8, P)
    out = {
        "xT": fm(h), "w": np.concatenate([chunks(g[n]) for n, _ in STREAM]), "cols": table,
        "a_re": x["a_re"].reshape(ST, P), "a_im": x["a_im"].reshape(ST, P), "log_step": x["log_step"].reshape(ST, 2),
        "w_alow": al.reshape(KT, P, 16).transpose(1, 0, 2), "w_gate_up": x["w_gate_up"][0],
        "b_re": bmat(x["b_re"][0]), "b_im": bmat(x["b_im"][0]), "c_re": cmat(cre), "c_im": cmat(cim),
        "memT": fm(x["mem_2"][0]), "w_if": np.concatenate([mi, mf], 1).reshape(KT, P, 2 * MH).transpose(1, 0, 2),
        "w_akv": np.concatenate([ak, av], 1).reshape(KT, P, CW).transpose(1, 0, 2),
        "sub1": x["sub_keys1_2"][0].T, "sub2": x["sub_keys2_2"][0].T,
        "g_final": np.broadcast_to(x["g_final_2"][None], (P, D)),
        "expert_down": x["expert_down_2"][0], "expert_up": x["expert_up_2"][0],
    }
    return {n: c(v) for n, v in out.items()}


def build(nc, a):
    ctx = ExitStack()

    def sb(name, shape, dt=F32):
        return ctx.enter_context(nc.sbuf_tensor(name, shape, dt))

    def sem(name):
        return ctx.enter_context(nc.semaphore(name))

    ring = sb("ring", [P, RING, KT, CW])
    feat = sb("feat", [P, 10, 8, T1])
    H, XN, SQ, UU, YS, QK, RR, ZG, ZS, EX = (feat[:, i] for i in range(10))
    FFH = feat[:, 3:7].rearrange("p s k t -> p (s k) t")
    VT = sb("VT", [P, 3, D])
    arena = sb("arena", [P, 16384])
    cols = sb("cols", [P, NCOLS])
    ident = sb("ident", [P, P])
    ones = sb("ones", [P, P])
    cmask = sb("cmask", [P, P])
    rmask = sb("rmask", [P, GH * T1])
    epsc = sb("epsc", [P, 1])
    RT = sb("RT", [P, 2, T1])
    walow = sb("walow", [P, KT, 16])
    wgu = sb("wgu", [16, GH * GDK])
    wif = sb("wif", [P, KT, 2 * MH])
    alow = sb("alow", [16, T1])

    at = [0]

    def carve(shape):
        n = int(np.prod(shape))
        v = arena[:, at[0]:at[0] + n]
        at[0] += n
        assert at[0] <= 16384, at[0]
        if len(shape) == 2:
            v = v.rearrange("p (a b) -> p a b", a=shape[0])
        if len(shape) == 3:
            v = v.rearrange("p (a b c) -> p a b c", a=shape[0], b=shape[1])
        return v

    COS = carve([SHALF, T1])
    SIN = carve([SHALF, T1])
    BD = [carve([8, P]) for _ in range(2)]
    CM = [carve([ST, 2 * SHG]) for _ in range(3)]
    P1, P2, WW, ZZ, R1, R2 = ([carve([2, T1]) for _ in range(2)] for _ in range(6))
    s5_end = at[0]
    SEL = VT[:, 0].rearrange("p (q c) -> p q c", q=8)
    LT = carve([3, ST])
    at[0] = 0
    GA, GB, GC, GE, GF, GI, GK = (carve([GH, T1]) for _ in range(7))
    GS = carve([4, GH, GDV])
    KST = carve([3, GH, GDK])
    SCT = carve([3, GH, P])
    prm = RR[0:ST].rearrange("p k t -> p (k t)")

    psD = ctx.enter_context(nc.psum_tensor("psD", [P, 4, 512], F32))
    psB = ctx.enter_context(nc.psum_tensor("psB", [P, 2, 512], F32))
    psY = ctx.enter_context(nc.psum_tensor("psY", [P, 512], F32))
    psN = ctx.enter_context(nc.psum_tensor("psN", [P, 512], F32))

    s_w = [sem(f"s_w{j}") for j in range(RING)]
    s_chunk = sem("s_chunk")
    s_dev = sem("s_dev")
    s_x = sem("s_x")
    s_cols = sem("s_cols")
    s_small = sem("s_small")
    s_s5 = sem("s_s5")
    s_s5b = sem("s_s5b")
    s_s5c = sem("s_s5c")
    s_zero = sem("s_zero")
    s_const = sem("s_const")
    s_vconst = sem("s_vconst")
    s_v = sem("s_v")
    s_p = sem("s_p")
    s_a = sem("s_a")
    s_sqa, s_sqv, s_ms, s_rt, s_xn = (sem(n) for n in ("s_sqa", "s_sqv", "s_ms", "s_rt", "s_xn"))
    s_h = sem("s_h")
    s_prm, s_exp, s_lt, s_ltc, s_bd = (sem(n) for n in ("s_prm", "s_exp", "s_lt", "s_ltc", "s_bd"))
    s_cn = sem("s_cn")
    s_bu, s_p12, s_rot, s_scan, s_r1, s_r2, s_y, s_ye, s_gs, s_tab = (
        sem(n) for n in ("s_bu", "s_p12", "s_rot", "s_scan", "s_r1", "s_r2", "s_y", "s_ye", "s_gs", "s_tab"))
    s_al, s_alc, s_gz, s_gzc, s_ls = (sem(n) for n in ("s_al", "s_alc", "s_gz", "s_gzc", "s_ls"))

    def counter(eng, s):
        n = [0]

        def link(ins):
            n[0] += 1
            ins.then_inc(s, 1)
            eng.wait_ge(s, n[0])
        return link

    def repeat(eng, n, body):
        if n == 1:
            body(0)
        else:
            with eng.Fori(0, n, 1) as it:
                body(it)

    def col(name, k, n=1):
        c = COLS[name][0] + k
        return cols[:, c:c + n]

    block = ctx.enter_context(nc.Block())

    def norm_act(i, x, ready, n, T, width=D):
        nc.scalar.wait_ge(ready, n)
        nc.scalar.activation(SQ[:, 4:8, 0:T], x[:, 4:8], ACT.Square).then_inc(s_sqa, 1)
        nc.scalar.wait_ge(s_ms, i + 1)
        nc.scalar.activation(RT[:, 0, 0:T], psN[:, 0:T], ACT.Sqrt, bias=epsc[:, 0:1],
                             scale=1.0 / width).then_inc(s_rt, 1)

    def norm_pe(i, T):
        nc.tensor.wait_ge(s_sqa, i + 1)
        nc.tensor.wait_ge(s_sqv, i + 1)
        for k in range(KT):
            mm = nc.tensor.matmul(psN[:, 0:T], ones[:, :], SQ[:, k, 0:T], start=(k == 0), stop=(k == KT - 1))
        mm.then_inc(s_ms, 1)

    def norm_dve(i, x, ready, n, T, gain, out, link):
        nc.vector.wait_ge(ready, n)
        nc.vector.tensor_tensor(SQ[:, 0:4, 0:T], x[:, 0:4], x[:, 0:4], ALU.mult).then_inc(s_sqv, 1)
        nc.vector.wait_ge(s_rt, i + 1)
        link(nc.vector.reciprocal(RT[:, 1, 0:T], RT[:, 0, 0:T]))
        for k in range(KT):
            ins = nc.vector.scalar_tensor_tensor(out=out[:, k, 0:T], in0=x[:, k], scalar=col(gain, k),
                                                 in1=RT[:, 1, 0:T], op0=ALU.mult, op1=ALU.mult)
        ins.then_inc(s_xn, 1)

    def dense_pe(first, n, x, T, hook=None):
        def body(it):
            for j in range(RING):
                c = first + RING * it + j
                nc.tensor.wait_ge(s_w[j], (first // RING + it + 1) * 16)
                if first + j >= 2:
                    nc.tensor.wait_ge(s_dev, first + j - 1 + RING * it)
                for m in range(2):
                    for k in range(KT):
                        mm = nc.tensor.matmul(psD[:, 2 * (j % 2) + m, 0:T], ring[:, j, k, m * P:(m + 1) * P],
                                              x[:, k], start=(k == 0), stop=(k == KT - 1))
                mm.then_inc(s_chunk, 1)
                if hook:
                    hook(j)
        repeat(nc.tensor, n, body)

    def dense_act(first, n, T, out):
        def body(it):
            for j in range(RING):
                nc.scalar.wait_ge(s_chunk, first + j + 1 + RING * it)
                out(it, j, psD[:, 2 * (j % 2):2 * (j % 2) + 2, 0:T]).then_inc(s_dev, 1)
        repeat(nc.scalar, n, body)


    def region(i, n=P):
        return prm[:, i * P:i * P + n]

    def poly(out, x, coef, link):
        link(nc.vector.tensor_scalar(out, x, float(coef[-1]), None, ALU.mult))
        for c in coef[-2::-1]:
            link(nc.vector.scalar_tensor_tensor(out=out, in0=out, scalar=float(c), in1=x, op0=ALU.add, op1=ALU.mult))

    def exp_exact(out, x, n, r, q, link):
        link(nc.vector.tensor_scalar(n, x, float(1 / np.log(2)), MAGIC, ALU.mult, ALU.add))
        link(nc.vector.tensor_scalar(n, n, MAGIC, -126.0, ALU.subtract, ALU.max))
        link(nc.vector.tensor_scalar(n, n, 127.0, None, ALU.min))
        link(nc.vector.scalar_tensor_tensor(out=r, in0=n, scalar=-0.693359375, in1=x, op0=ALU.mult, op1=ALU.add))
        link(nc.vector.scalar_tensor_tensor(out=r, in0=n, scalar=2.12194440e-4, in1=r, op0=ALU.mult, op1=ALU.add))
        poly(q, r, [1.0 / float(np.prod(np.arange(1, k + 1))) for k in range(1, 9)], link)
        link(nc.vector.tensor_scalar(n.bitcast(I32), n, 127.0, None, ALU.add))
        link(nc.vector.tensor_scalar(n.bitcast(I32), n.bitcast(I32), 23, None, ALU.logical_shift_left))
        link(nc.vector.scalar_tensor_tensor(out=out, in0=q, scalar=1.0, in1=n, op0=ALU.add, op1=ALU.mult))

    AR, AI, X, NN, RE, Q, TH, S2, C2, MAG, LRE, LIM, TT, DEN = (region(i) for i in range(14))
    FRI = prm[:, 14 * P:16 * P]
    FR, FI = FRI[:, 0:P], FRI[:, P:2 * P]
    LST, DT, D1, D2, D3 = (prm[:, 16 * P + 2 * i:16 * P + 2 * i + 2] for i in range(5))
    BR, BI = (s[:, 0:4].rearrange("p k t -> p (k t)")[:, 0:8 * P].rearrange("p (q n) -> p q n", q=8) for s in (ZG, ZS))

    def s5_param_dve(link):
        tt = nc.vector.tensor_tensor
        nc.vector.wait_ge(s_s5, 48)
        exp_exact(DT, LST, D1, D2, D3, link)
        dtb = DT.unsqueeze(2).to_broadcast([ST, 2, SN])
        three = lambda v: v.rearrange("p (g n) -> p g n", g=2)
        link(tt(three(X), three(AR), dtb, ALU.mult))
        link(tt(three(TH), three(AI), dtb, ALU.mult))
        exp_exact(MAG, X, NN, RE, Q, link)
        c1 = 6.28125
        c2 = float(np.float32(np.round((2 * np.pi - c1) * 2 ** 22) / 2 ** 22))
        c3 = float(2 * np.pi - c1 - c2)
        link(nc.vector.tensor_scalar(NN, TH, float(1 / (2 * np.pi)), MAGIC, ALU.mult, ALU.add))
        link(nc.vector.tensor_scalar(NN, NN, MAGIC, None, ALU.subtract))
        link(nc.vector.scalar_tensor_tensor(out=RE, in0=NN, scalar=-c1, in1=TH, op0=ALU.mult, op1=ALU.add))
        link(nc.vector.scalar_tensor_tensor(out=RE, in0=NN, scalar=-c2, in1=RE, op0=ALU.mult, op1=ALU.add))
        link(nc.vector.scalar_tensor_tensor(out=RE, in0=NN, scalar=-c3, in1=RE, op0=ALU.mult, op1=ALU.add))
        link(nc.vector.tensor_scalar(RE, RE, 0.5, None, ALU.mult))
        link(tt(X, RE, RE, ALU.mult))
        fact = lambda k: float(np.prod(np.arange(1.0, k + 1)))
        poly(Q, X, [(-1) ** k / fact(2 * k + 1) for k in range(1, 8)], link)
        link(nc.vector.scalar_tensor_tensor(out=S2, in0=Q, scalar=1.0, in1=RE, op0=ALU.add, op1=ALU.mult))
        poly(Q, X, [(-1) ** k / fact(2 * k) for k in range(1, 8)], link)
        link(nc.vector.scalar_tensor_tensor(out=C2, in0=Q, scalar=1.0, in1=S2, op0=ALU.add, op1=ALU.mult))
        link(nc.vector.tensor_scalar(C2, C2, 2.0, None, ALU.mult))
        link(tt(S2, S2, S2, ALU.mult))
        link(nc.vector.tensor_scalar(S2, S2, -2.0, 1.0, ALU.mult, ALU.add))
        link(tt(LRE, MAG, S2, ALU.mult))
        link(tt(LIM, MAG, C2, ALU.mult))
        link(nc.vector.tensor_scalar(LRE, LRE, -1.0, None, ALU.add))
        link(tt(DEN, AR, AR, ALU.mult))
        link(tt(TT, AI, AI, ALU.mult))
        link(tt(DEN, DEN, TT, ALU.add))
        link(nc.vector.reciprocal(DEN, DEN))
        link(tt(FR, LRE, AR, ALU.mult))
        link(tt(TT, LIM, AI, ALU.mult))
        link(tt(FR, FR, TT, ALU.add))
        link(tt(FI, LIM, AR, ALU.mult))
        link(tt(TT, LRE, AI, ALU.mult))
        link(tt(FI, FI, TT, ALU.subtract))
        link(tt(FR, FR, DEN, ALU.mult))
        tt(FI, FI, DEN, ALU.mult).then_inc(s_prm, 1)
        nc.vector.wait_ge(s_lt, 1)
        nc.vector.tensor_copy(LT[:, :, :].rearrange("p a j -> p (a j)"), psN[:, 0:3 * ST]).then_inc(s_ltc, 1)
        nc.vector.wait_ge(s_s5b, 32)
        for half in range(2):
            nc.vector.wait_ge(s_exp, half + 1)
            f = psB[:, :, :].rearrange("p b (q c n) -> p (b q) c n", q=2, c=2)
            qs = slice(4 * half, 4 * half + 4)
            fr, fi = f[:, :, 0], f[:, :, 1]
            ta, tb = (WW[i][:, :, :].rearrange("p a t -> p (a t)")[:, 0:4 * P].rearrange("p (q n) -> p q n", q=4)
                      for i in range(2))
            for dst, (x1, x2), op in ((BD[0], (BR, BI), ALU.subtract), (BD[1], (BI, BR), ALU.add)):
                link(tt(ta, fr, x1[:, qs], ALU.mult))
                link(tt(tb, fi, x2[:, qs], ALU.mult))
                ins = tt(dst[:, qs], ta, tb, op)
                if dst is BD[0]:
                    link(ins)
            ins.then_inc(s_bd, 1)
            nc.vector.wait_ge(s_bd, half + 1)

    def s5_param_pe():
        nc.tensor.wait_ge(s_prm, 1)
        nc.tensor.wait_ge(s_const, 1)
        for i, v in enumerate((MAG, S2, C2)):
            mm = nc.tensor.transpose(psN[:, i * ST:(i + 1) * ST], v, ident[0:ST, 0:ST])
        mm.then_inc(s_lt, 1)
        for half in range(2):
            if half:
                nc.tensor.wait_ge(s_bd, half)
            for i in range(4):
                mm = nc.tensor.matmul(psB[:, i // 2, (i % 2) * 256:(i % 2) * 256 + 256],
                                      SEL[0:ST, 4 * half + i, :], FRI, start=True, stop=True)
            mm.then_inc(s_exp, 1)

    def s5_tables(g, link):
        tt = nc.vector.tensor_tensor
        js = slice(g * SHALF, (g + 1) * SHALF)
        ta, tb = (SQ[:, 4 * i:4 * i + 4].rearrange("p k t -> p (k t)")[:, 0:SHALF * P]
                  .rearrange("p (j t) -> p j t", j=SHALF) for i in range(2))
        if g:
            nc.vector.wait_ge(s_r2, g * SHALF)
            nc.vector.wait_ge(s_r1, g * SHALF)
        nc.vector.memset(COS[:, :, 0:1], 1.0)
        nc.vector.memset(SIN[:, :, 0:1], 0.0)
        nc.vector.tensor_copy(COS[:, :, 1:2], LT[:, 1, js].unsqueeze(2))
        link(nc.vector.tensor_copy(SIN[:, :, 1:2], LT[:, 2, js].unsqueeze(2)))
        known = 1
        while known < T1 - 1:
            n = min(known, T1 - 1 - known)
            c, s = COS[:, :, 1:1 + n], SIN[:, :, 1:1 + n]
            ck = COS[:, :, known:known + 1].to_broadcast([P, SHALF, n])
            sk = SIN[:, :, known:known + 1].to_broadcast([P, SHALF, n])
            new = slice(known + 1, known + 1 + n)
            tt(ta[:, :, 0:n], c, ck, ALU.mult)
            link(tt(tb[:, :, 0:n], s, sk, ALU.mult))
            link(tt(COS[:, :, new], ta[:, :, 0:n], tb[:, :, 0:n], ALU.subtract))
            tt(ta[:, :, 0:n], c, sk, ALU.mult)
            link(tt(tb[:, :, 0:n], s, ck, ALU.mult))
            link(tt(SIN[:, :, new], ta[:, :, 0:n], tb[:, :, 0:n], ALU.add))
            known += n

    def s5_bu(j):
        q, r = j // 4, j % 4
        if j == 0:
            nc.tensor.wait_ge(s_bd, 2)
            nc.tensor.wait_ge(s_dev, FIRST["u"] + 4)
        if j >= 1:
            nc.tensor.wait_ge(s_p12, j)
        for c in range(2):
            mm = nc.tensor.matmul(psB[:, c, 0:T1], BD[c][32 * r:32 * r + 32, q, :], UU[32 * r:32 * r + 32, q],
                                  start=True, stop=True, tile_position=(32 * r, 0))
        mm.then_inc(s_bu, 1)

    def s5_y(j):
        q, r = j // 4, j % 4
        if j == 0:
            nc.tensor.wait_ge(s_cn, 1)
        if r == 0 and q:
            nc.tensor.wait_ge(s_ye, q)
        nc.tensor.wait_ge(s_r1, j + 1)
        nc.tensor.wait_ge(s_r2, j + 1)
        b = j % 2
        terms = [(CM[0], R1[b][:, 0]), (CM[1], R2[b][:, 1]), (CM[2], R2[b][:, 0]), (CM[2], R1[b][:, 1])]
        for i, (c, x) in enumerate(terms):
            mm = nc.tensor.matmul(psY[32 * r:32 * r + 32, 0:T1], c[:, j, :], x, start=(i == 0), stop=(i == 3),
                                  tile_position=(0, 32 * r))
        mm.then_inc(s_y, 1)

    def bc(tab, j):
        return tab[:, j % SHALF].unsqueeze(1).to_broadcast([P, 2, T1])

    def s5_dve(link):
        def rotate_in(j):
            if j % SHALF == 0:
                s5_tables(j // SHALF, link)
            nc.vector.wait_ge(s_bu, j + 1)
            if j >= 2:
                nc.vector.wait_ge(s_rot, j - 1)
            nc.vector.tensor_tensor(P1[j % 2], psB[:, :, 0:T1], bc(COS, j), ALU.mult)
            nc.vector.tensor_tensor(P2[j % 2], psB[:, :, 0:T1], bc(SIN, j), ALU.mult).then_inc(s_p12, 1)

        def scan(j):
            b = j % 2
            nc.vector.wait_ge(s_rot, j + 1)
            if j >= 2:
                nc.vector.wait_ge(s_r2, j - 1)
            for c in range(2):
                m = LT[:, 0, j:j + 1].to_broadcast([P, T1])
                ins = nc.vector.tensor_tensor_scan(ZZ[b][:, c], m, WW[b][:, c], 0.0, ALU.mult, ALU.add)
            ins.then_inc(s_scan, 1)
            nc.vector.wait_ge(s_scan, j + 1)
            if j >= 2:
                nc.vector.wait_ge(s_y, j - 1)
            nc.vector.tensor_tensor(R1[b], ZZ[b], bc(COS, j), ALU.mult).then_inc(s_r1, 1)

        def skip(q):
            nc.vector.wait_ge(s_y, 4 * q + 4)
            nc.vector.scalar_tensor_tensor(out=YS[:, q], in0=UU[:, q], scalar=col("d_skip", q), in1=psY[:, 0:T1],
                                           op0=ALU.mult, op1=ALU.add).then_inc(s_ye, 1)

        for j in range(ST + 1):
            if j < ST:
                if j % SHALF == 0 and j:
                    scan(j - 1)
                    rotate_in(j)
                else:
                    rotate_in(j)
                    if j:
                        scan(j - 1)
            else:
                scan(j - 1)
            if j >= 6 and (j - 6) % 4 == 0:
                skip((j - 6) // 4)
        skip(ST // 4 - 1)

    def s5_pool():
        def back(j):
            b = j % 2
            nc.gpsimd.wait_ge(s_scan, j + 1)
            if j >= 2:
                nc.gpsimd.wait_ge(s_y, j - 1)
            nc.gpsimd.tensor_tensor(R2[b], ZZ[b], bc(SIN, j), ALU.mult).then_inc(s_r2, 1)

        for j in range(ST):
            b = j % 2
            if j % SHALF == 0 and j:
                back(j - 1)
            nc.gpsimd.wait_ge(s_p12, j + 1)
            if j >= 2:
                nc.gpsimd.wait_ge(s_scan, j - 1)
            nc.gpsimd.tensor_tensor(WW[b][:, 0], P1[b][:, 0], P2[b][:, 1], ALU.add)
            nc.gpsimd.tensor_tensor(WW[b][:, 1], P1[b][:, 1], P2[b][:, 0], ALU.subtract).then_inc(s_rot, 1)
            if j % SHALF:
                back(j - 1)
        back(ST - 1)

    LZ, LB = EX[:, 0:4], EX[:, 4:8]
    flat = lambda v: v.rearrange("p h t -> p (h t)")

    def gate_pe():
        nc.tensor.wait_ge(s_small, 48)
        for k in range(KT):
            mm = nc.tensor.matmul(psY[0:16, 0:T1], walow[:, k, :], XN[:, k], start=(k == 0), stop=(k == KT - 1))
        mm.then_inc(s_al, 1)
        nc.tensor.wait_ge(s_alc, 1)
        for h in range(GH):
            if h >= 2:
                nc.tensor.wait_ge(s_gzc, h - 1)
            (nc.tensor.matmul((psY, psN)[h % 2][:, 0:T1], wgu[:, h * P:(h + 1) * P], alow[:, :], start=True, stop=True)
             .then_inc(s_gz, 1))

    def gate_act(link):
        nc.scalar.wait_ge(s_al, 1)
        nc.scalar.activation(alow[:, :], psY[0:16, 0:T1], ACT.Identity).then_inc(s_alc, 1)
        for h in range(GH):
            nc.scalar.wait_ge(s_gz, h + 1)
            (nc.scalar.activation(LZ[:, h], (psY, psN)[h % 2][:, 0:T1], ACT.Identity, bias=col("b_gate", h))
             .then_inc(s_gzc, 1))
        nc.scalar.wait_ge(s_gzc, GH)
        link(nc.scalar.activation(LB, LZ, ACT.Abs))
        link(nc.scalar.activation(LB, LB, ACT.Exp, scale=-1.0))
        nc.scalar.activation(LB, LB, ACT.Ln, bias=1.0).then_inc(s_ls, 1)

    def gate_dve(link):
        nc.vector.wait_ge(s_ls, 1)
        link(nc.vector.scalar_tensor_tensor(out=LZ, in0=LZ, scalar=0.0, in1=LB, op0=ALU.min, op1=ALU.subtract))
        link(nc.vector.tensor_tensor_scan(flat(LB), rmask[:, :], flat(LZ), 0.0, ALU.mult, ALU.add))

    s_gd, s_ge, s_gq, s_kt, s_ktc, s_sc, s_scc, s_u, s_st, s_o, s_oc, s_hms, s_hrt, s_og = (sem(n) for n in (
        "s_gd", "s_ge", "s_gq", "s_kt", "s_ktc", "s_sc", "s_scc", "s_u", "s_st", "s_o", "s_oc", "s_hms", "s_hrt",
        "s_og"))
    inv = 1.0 / 16.0

    def gla_prep_dve(link):
        tt = nc.vector.tensor_tensor
        nc.vector.wait_ge(s_y, ST)
        nc.vector.wait_ge(s_r2, ST)
        body = lambda v: v[:, :, META:T1].rearrange("p h (c t) -> p h c t", t=GCH)
        wide = [P, GH, 4, GCH]
        nc.vector.memset(SCT[:, :, :, :], 0.0)
        for h in range(GH):
            tt(body(GA)[:, h], body(LB)[:, h], body(LB)[:, h, :, 32:33].to_broadcast([P, 4, GCH]), ALU.subtract)
            tt(body(GB)[:, h], body(LB)[:, h, :, 63:64].to_broadcast([P, 4, GCH]), body(LB)[:, h], ALU.subtract)
        nc.vector.tensor_copy(GA[:, :, 0:META], LB[:, :, 0:META])
        tt(GB[:, :, 0:META], LB[:, :, META - 1:META].to_broadcast([P, GH, META]), LB[:, :, 0:META],
           ALU.subtract).then_inc(s_gd, 1)
        nc.vector.wait_ge(s_ge, 1)
        nc.vector.wait_ge(s_dev, FIRST["qk"] + 4)
        sc = float(GDK) ** -0.5
        stt = nc.vector.scalar_tensor_tensor
        tt(GK, QK[:, 4:8], GB, ALU.mult).then_inc(s_gq, 1)
        tt(GI, QK[:, 4:8], GA, ALU.mult)
        link(stt(out=GF, in0=QK[:, 0:4], scalar=sc, in1=GC, op0=ALU.mult, op1=ALU.mult))
        stt(out=GC, in0=QK[:, 0:4], scalar=sc, in1=GE, op0=ALU.mult, op1=ALU.mult).then_inc(s_gq, 1)

    def gla_exp_act():
        nc.scalar.wait_ge(s_gd, 1)
        nc.scalar.activation(GC, GA, ACT.Exp, scale=inv)
        nc.scalar.activation(GE, LB, ACT.Exp, scale=inv)
        nc.scalar.activation(GB, GB, ACT.Exp, scale=inv)
        nc.scalar.activation(GA, GA, ACT.Exp, scale=-inv).then_inc(s_ge, 1)

    KTB = [psB[:, 0], psB[:, 1], psY]
    SCB = [psN, psB[:, 0], psB[:, 1]]

    def gla_pe_a():
        nc.tensor.wait_ge(s_gq, 1)
        nc.tensor.wait_ge(s_ye, 8)
        for g, (t0, n) in enumerate(TOK1):
            for h in range(GH):
                mm = nc.tensor.transpose(KTB[g][0:n, h * P:(h + 1) * P], GK[:, h, t0:t0 + n], ident[:, :])
            mm.then_inc(s_kt, 1)
        nc.tensor.wait_ge(s_gq, 2)
        for g, (t0, n) in enumerate(TOK1):
            if g:
                nc.tensor.wait_ge(s_ktc, g)
            for h in range(GH):
                mm = nc.tensor.matmul(SCB[g][0:n, h * P:h * P + n], GI[:, h, t0:t0 + n], GF[:, h, t0:t0 + n],
                                      start=True, stop=True)
            mm.then_inc(s_sc, 1)
        nc.tensor.wait_ge(s_dev, FIRST["v"] + 4)
        nc.tensor.wait_ge(s_ktc, 3)
        nc.tensor.wait_ge(s_scc, 3)
        rows = [(0, 0, META), (1, 0, 64), (1, 64, 64), (2, 0, 64)]
        for c, (g, r, n) in enumerate(rows):
            if c:
                nc.tensor.wait_ge(s_st, c)
            for h in range(GH):
                mm = nc.tensor.matmul(psB[:, h // 2, (h % 2) * GDV:(h % 2) * GDV + GDV],
                                      KST[r:r + n, g, h, :], VT[r:r + n, g, h * GDV:(h + 1) * GDV],
                                      start=True, stop=True, tile_position=(r, 0))
            mm.then_inc(s_u, 1)

    def gla_dve_a(link):
        for g, (t0, n) in enumerate(TOK1):
            nc.vector.wait_ge(s_kt, g + 1)
            (nc.vector.tensor_copy(KST[0:n, g].rearrange("p h d -> p (h d)"), KTB[g][0:n, :])
             .then_inc(s_ktc, 1))
        for g, (t0, n) in enumerate(TOK1):
            nc.vector.wait_ge(s_sc, g + 1)
            src = SCB[g][0:n, :].rearrange("p (h i) -> p h i", h=GH)[:, :, 0:n]
            mask = cmask[0:n, 0:n].bitcast(U32).unsqueeze(1).to_broadcast([n, GH, n])
            nc.vector.copy_predicated(SCT[0:n, g, :, 0:n], mask, src).then_inc(s_scc, 1)
        ends = [META - 1 + GCH * c for c in range(4)]
        for c in range(4):
            nc.vector.wait_ge(s_u, c + 1)
            if c == 0:
                ins = nc.vector.tensor_copy(GS[:, 0].rearrange("p (b h) v -> p b (h v)", b=2), psB[:, :, :])
            else:
                nc.vector.wait_ge(s_st, c)
                for h in range(GH):
                    ins = nc.vector.scalar_tensor_tensor(
                        out=GS[:, c, h], in0=GS[:, c - 1, h], scalar=GE[:, h, ends[c]:ends[c] + 1],
                        in1=psB[:, h // 2, (h % 2) * GDV:(h % 2) * GDV + GDV], op0=ALU.mult, op1=ALU.add)
            ins.then_inc(s_st, 1)

    def gla_pe_b():
        for g, (t0, n) in enumerate(TOK1):
            nc.tensor.wait_ge(s_st, 4)
            if g:
                nc.tensor.wait_ge(s_oc, g)
            for h in range(GH):
                for m in range(2):
                    i = 2 * h + m
                    o = psB[:, i // 4, (i % 4) * P:(i % 4) * P + n]
                    vcol = h * GDV + m * P
                    mm = nc.tensor.matmul(o, VT[0:n, g, vcol:vcol + P], SCT[0:n, g, h, 0:n], start=True,
                                          stop=(g == 0), skip_group_check=True)
                    for half in range(2 if g else 0):
                        c = 2 * g - 1 + half
                        q = GC[:, h, GSTART[c]:GSTART[c] + GCH]
                        mm = nc.tensor.matmul(o[:, half * GCH:half * GCH + GCH], GS[:, c - 1, h, m * P:(m + 1) * P], q,
                                              start=False, stop=True, skip_group_check=True)
            mm.then_inc(s_o, 1)

    def gla_act_b():
        for g, (t0, n) in enumerate(TOK1):
            nc.scalar.wait_ge(s_o, g + 1)
            src = psB[:, :, :].rearrange("p b (i t) -> p (b i) t", t=P)[:, :, 0:n]
            nc.scalar.activation(QK[:, :, t0:t0 + n], src, ACT.Identity).then_inc(s_oc, 1)
        nc.scalar.wait_ge(s_oc, 3)
        nc.scalar.activation(SQ[:, :, :], QK[:, :, :], ACT.Square).then_inc(s_oc, 1)
        for h in range(GH):
            nc.scalar.wait_ge(s_hms, h + 1)
            (nc.scalar.activation(GA[:, h], (psB[:, 0], psB[:, 1], psY, psN)[h][:, 0:T1], ACT.Sqrt,
                                  bias=epsc[:, 0:1], scale=1.0 / GDV).then_inc(s_hrt, 1))

    def gla_pe_norm():
        nc.tensor.wait_ge(s_oc, 4)
        for h in range(GH):
            for m in range(2):
                mm = nc.tensor.matmul((psB[:, 0], psB[:, 1], psY, psN)[h][:, 0:T1], ones[:, :], SQ[:, 2 * h + m],
                                      start=(m == 0), stop=(m == 1))
            mm.then_inc(s_hms, 1)

    def gla_dve_norm(link):
        nc.vector.wait_ge(s_hrt, 4)
        link(nc.vector.reciprocal(GB, GA))
        for k in range(8):
            ins = nc.vector.scalar_tensor_tensor(out=QK[:, k], in0=QK[:, k], scalar=col("gla_norm_g", k),
                                                 in1=GB[:, k // 2], op0=ALU.mult, op1=ALU.mult)
        link(ins)
        nc.vector.tensor_tensor(QK, QK, RR, ALU.mult).then_inc(s_og, 1)

    def v1_pe(j):
        c = FIRST["v"] + j
        nc.tensor.wait_ge(s_w[j], (c // RING + 1) * 16)
        nc.tensor.wait_ge(s_dev, c - 1)
        for g, (t0, n) in ((1, TOK1[1]), (2, TOK1[2]), (0, TOK1[0])):
            o = psD[0:n, 2 * (j % 2) + (g == 0), (g == 2) * CW:(g == 2) * CW + CW]
            for k in range(KT):
                mm = nc.tensor.matmul(o, XN[:, k, t0:t0 + n], ring[:, j, k, :], start=(k == 0), stop=(k == KT - 1))
        mm.then_inc(s_chunk, 1)

    def v1_act(j):
        nc.scalar.wait_ge(s_chunk, FIRST["v"] + j + 1)
        b = 2 * (j % 2)
        nc.scalar.activation(VT[:, 1:3, j * CW:(j + 1) * CW],
                             psD[:, b, :].rearrange("p (g n) -> p g n", g=2), ACT.Identity)
        nc.scalar.activation(VT[0:META, 0, j * CW:(j + 1) * CW], psD[0:META, b + 1, 0:CW],
                             ACT.Identity).then_inc(s_dev, 1)

    def chunk_pe(first, j, x, T):
        c = first + j
        nc.tensor.wait_ge(s_w[j % RING], (c // RING + 1) * 16)
        if c >= 2:
            nc.tensor.wait_ge(s_dev, c - 1)
        for m in range(2):
            for k in range(KT):
                mm = nc.tensor.matmul(psD[:, 2 * (c % 2) + m, 0:T], ring[:, j % RING, k, m * P:(m + 1) * P],
                                      x[:, k], start=(k == 0), stop=(k == KT - 1))
        mm.then_inc(s_chunk, 1)

    def evac(dst, func, base=0, T=T1):
        return lambda it, j, ps: nc.scalar.activation(dst[:, bass.ds(2 * j + 8 * it, 2), 0:T] if not isinstance(it, int)
                                                      else dst[:, 2 * j + 8 * it:2 * j + 8 * it + 2, 0:T], ps, func)

    s_mix, s_ffh, s_t, s_glu = sem("s_mix"), sem("s_ffh"), sem("s_t"), sem("s_glu")

    def glu_act(part):
        for j in range(RING):
            c = FIRST["w_glu"] + 4 * part + j
            nc.scalar.wait_ge(s_chunk, c + 1)
            for m in range(2):
                i = 2 * j + m
                dst = (UU, EX)[part][:, i]
                ins = nc.scalar.activation(dst, psD[:, 2 * (j % 2) + m, 0:T1], (ACT.Identity, ACT.Sigmoid)[part],
                                           bias=col("b_glu", 8 * part + i))
            ins.then_inc(s_dev, 1)

    def ff2_pe(x, T):
        first = FIRST["w_ff2"]

        def body(it):
            for half in range(2):
                for kg in range(RING):
                    nc.tensor.wait_ge(s_w[kg], (first // RING + 1 + half + 2 * it) * 16)
                    if kg == 0:
                        nc.tensor.wait_ge(s_dev, first + (4 * (2 * it + half) - 4) if not isinstance(it, int)
                                          else first + max(4 * (2 * it + half) - 4, half - 1))
                    for m in range(2):
                        for k in range(KT):
                            mm = nc.tensor.matmul(psD[:, 2 * half + m, 0:T], ring[:, kg, k, m * P:(m + 1) * P],
                                                  x[:, KT * kg + k], start=(kg == 0 and k == 0),
                                                  stop=(kg == RING - 1 and k == KT - 1))
                    mm.then_inc(s_chunk, 1)
        body(0)
        body(1)

    def ff2_act(dst, T):
        for mg in range(4):
            nc.scalar.wait_ge(s_chunk, FIRST["w_ff2"] + 4 * mg + 4)
            (nc.scalar.activation(dst[:, 2 * mg:2 * mg + 2, 0:T], psD[:, 2 * (mg % 2):2 * (mg % 2) + 2, 0:T],
                                  ACT.Identity).then_inc(s_dev, 4))

    H2 = H[:, :, META:T1]
    XN2 = XN[:, :, 0:T2]
    MEM = EX[:, :, 0:T2]
    KX = UU[:, :, 0:T2]
    XV = YS.rearrange("p k t -> p (k t)")[:, 0:2 * D].rearrange("p (s n) -> p s n", s=2)
    MQKP = QK[:, 0:4, :]
    MO = QK[:, 4:8, 0:T2]
    AQ = RR[:, 0:4, 0:T2]
    MVT = RR[:, 4:8].rearrange("p k t -> p (k t)")[:, 0:2 * 512].rearrange("p (s n) -> p s n", s=2)
    CAT = ZS[:, :, 0:T2]
    QX = EX[:, :, 0:T2]
    OX = QK[:, :, 0:T2]
    DEL = ZG[:, :, 0:T2]
    at[0] = 0
    WKV = carve([KT, CW])
    AK = carve([T2])
    AV = carve([2, P])
    MQK = carve([4, T2])
    NEGC = carve([P])
    MASK3 = carve([3, P])
    ROWS = carve([5, T2])
    SELH = carve([MH, P])
    ACOL = carve([2, MH])
    EXPM = carve([MH, T2])
    DTE = carve([MH, 3 * P])
    PTM = carve([MH, 3 * P])
    HM = carve([MH, T2])
    RH = carve([MH, T2])
    SB = carve([AH, 3 * P])
    at_swa = at[0]
    MX, NMX, SUM, ESK = (carve([2, AH]) for _ in range(4))
    at[0] = 0
    XP = carve([XH, 2, T2])
    XPT = carve([XH, 2, T2])
    XMX, XNM, XSM, XRC = (carve([XH, 2]) for _ in range(4))
    at[0] = 0
    QH = feat[:, 3:5].rearrange("p s k t -> p (s k) t")[:, :, 0:T2]
    SCO = feat[:, 5:7].rearrange("p s k t -> p (s k t)")[:, 0:4096].rearrange("p (t x n) -> p t x n", t=2, x=16)
    XTOK, HTOK, ACC = (feat[:, i].rearrange("p k t -> p (k t)")[:, 0:2 * D].rearrange("p (t d) -> p t d", t=2)
                       for i in (7, 8, 9))
    GB_ = ring[:, :, :, :].rearrange("p j k n -> p (j k n)").rearrange("p (b d) -> p b d", d=D)
    SKT = carve([2, PK])
    VAL = carve([16, PTOP])
    IDX = carve([16, PTOP]).bitcast(U32)
    IDF = carve([16, PTOP])
    CS = carve([PH, PTOP * PTOP])
    OH = carve([PH, PTOP, PTOP])
    TV = carve([2, PH, PTOP])
    POS = carve([PH, PTOP]).bitcast(U32)
    PA = carve([PH, PTOP]).bitcast(U32)
    PAF = carve([PH, PTOP])
    SEL1 = carve([PH, PTOP])
    SEL2 = carve([PH, PTOP])
    EID = carve([2, PH * PTOP]).bitcast(U32)
    IOTA = carve([PTOP])
    IOI = carve([PTOP]).bitcast(I32)
    GT = carve([2, PH, PTOP])
    GM = carve([PH])
    AD = carve([2, PH * PTOP])
    COEF = carve([2, PH * PTOP])
    ADB = carve([8])
    JUNK = carve([2, D])
    ACB = carve([D])
    GFIN = carve([D])
    FS = carve([2, 4])

    (s_mem, s_kv, s_c2, s_if, s_ifl, s_conv, s_silu, s_mrow, s_acol, s_acs, s_rb, s_em, s_dt, s_de, s_ms2, s_pt,
     s_num, s_hm, s_hsq, s_hs, s_hr, s_cat, s_akv, s_aks, s_ws, s_wsb, s_wmx, s_wex, s_wpn, s_wt, s_wtc, s_wo_,
     s_woc) = (sem(n) for n in (
         "s_mem", "s_kv", "s_c2", "s_if", "s_ifl", "s_conv", "s_silu", "s_mrow", "s_acol", "s_acs", "s_rb", "s_em",
         "s_dt", "s_de", "s_ms2", "s_pt", "s_num", "s_hm", "s_hsq", "s_hs", "s_hr", "s_cat", "s_akv", "s_aks",
         "s_ws", "s_wsb", "s_wmx", "s_wex", "s_wpn", "s_wt", "s_wtc", "s_wo_", "s_woc"))

    def tok_pe(first, j, x):
        c = first + j
        nc.tensor.wait_ge(s_w[c % RING], (c // RING + 1) * 16)
        nc.tensor.wait_ge(s_dev, c - 1)
        for g in range(2):
            for k in range(KT):
                mm = nc.tensor.matmul(psD[:, 2 * (c % 2) + g, 0:CW], x[:, k, g * P:(g + 1) * P], ring[:, c % RING, k, :],
                                      start=(k == 0), stop=(k == KT - 1))
        mm.then_inc(s_chunk, 1)

    def tok_act(first, j, dst):
        c = first + j
        nc.scalar.wait_ge(s_chunk, c + 1)
        (nc.scalar.activation(dst, psD[:, 2 * (c % 2):2 * (c % 2) + 2, 0:CW], ACT.Identity).then_inc(s_dev, 1))

    def pair_act(first, j, dst, func=ACT.Identity):
        c = first + j
        nc.scalar.wait_ge(s_chunk, c + 1)
        (nc.scalar.activation(dst, psD[:, 2 * (c % 2):2 * (c % 2) + 2, 0:T2], func).then_inc(s_dev, 1))

    def small2_pe():
        nc.tensor.wait_ge(s_kv, 16)
        for i in range(2):
            for k in range(KT):
                mm = nc.tensor.matmul(psY[0:MH, i * T2:(i + 1) * T2], wif[:, k, MH * i:MH * i + MH], XN2[:, k],
                                      start=(k == 0), stop=(k == KT - 1))
        mm.then_inc(s_if, 1)
        for k in range(KT):
            mm = nc.tensor.matmul(psB[:, 0, 0:T2], WKV[:, k, 0:P], XN2[:, k], start=(k == 0), stop=(k == KT - 1))
        for g in range(2):
            for k in range(KT):
                mm = nc.tensor.matmul(psB[:, 1, g * P:(g + 1) * P], XN2[:, k, g * P:(g + 1) * P], WKV[:, k, P:2 * P],
                                      start=(k == 0), stop=(k == KT - 1))
        mm.then_inc(s_akv, 1)

    def small2_act(link):
        nc.scalar.wait_ge(s_if, 1)
        r = ROWS[0:MH]
        nc.scalar.activation(r[:, 3], psY[0:MH, 0:T2], ACT.Identity, bias=col("b_igate_2", 0)[0:MH])
        link(nc.scalar.activation(r[:, 4], psY[0:MH, T2:2 * T2], ACT.Identity, bias=col("b_fgate_2", 0)[0:MH]))
        link(nc.scalar.activation(r[:, 0], r[:, 4], ACT.Abs))
        link(nc.scalar.activation(r[:, 0], r[:, 0], ACT.Exp, scale=-1.0))
        nc.scalar.activation(r[:, 0], r[:, 0], ACT.Ln, bias=1.0).then_inc(s_ifl, 1)
        nc.scalar.wait_ge(s_akv, 1)
        nc.scalar.activation(AK, psB[:, 0, 0:T2], ACT.Identity)
        nc.scalar.activation(AV[:, :, :], psB[:, 1, 0:2 * P].rearrange("p (g n) -> p g n", g=2),
                             ACT.Identity).then_inc(s_aks, 1)

    def conv_dve(link):
        for i in range(4):
            for k in range(4):
                x = MQKP[:, k, i:i + T2]
                if i == 0:
                    ins = nc.vector.tensor_scalar(MQK[:, k], x, col("conv_w_2", 4 * k), col("conv_b_2", k),
                                                  ALU.mult, ALU.add)
                else:
                    ins = nc.vector.scalar_tensor_tensor(out=MQK[:, k], in0=x, scalar=col("conv_w_2", 4 * k + i),
                                                         in1=MQK[:, k], op0=ALU.mult, op1=ALU.add)
            if i < 3:
                link(ins)
        ins.then_inc(s_conv, 1)

    def mrows_dve(link):
        r = ROWS[0:MH]
        nc.vector.wait_ge(s_ifl, 1)
        link(nc.vector.scalar_tensor_tensor(out=r[:, 4], in0=r[:, 4], scalar=0.0, in1=r[:, 0], op0=ALU.min,
                                            op1=ALU.subtract))
        nc.vector.tensor_tensor_scan(r[:, 2], r[:, 4], r[:, 3], 0.0, ALU.add, ALU.max)
        one = ones[0:MH, 0:1].to_broadcast([MH, T2])
        link(nc.vector.tensor_tensor_scan(r[:, 1], one, r[:, 4], 0.0, ALU.mult, ALU.add))
        link(nc.vector.tensor_tensor(r[:, 0], r[:, 3], r[:, 1], ALU.subtract))
        nc.vector.tensor_tensor(r[:, 1], r[:, 1], r[:, 2], ALU.subtract).then_inc(s_mrow, 1)
        nc.vector.wait_ge(s_acol, 1)
        (nc.vector.tensor_copy(ACOL.rearrange("p s h -> p (s h)"), psY[:, 0:2 * MH]).then_inc(s_acs, 1))

    RB = [psB[:, 0], psB[:, 1], psY[:, :], psN[:, :]]

    def mrows_pe():
        nc.tensor.wait_ge(s_mrow, 1)
        nc.tensor.wait_ge(s_ifl, 1)
        for s in range(2):
            mm = nc.tensor.transpose(psY[:, s * MH:(s + 1) * MH], ROWS[0:MH, 0, s * P:(s + 1) * P], ident[0:MH, 0:MH])
        mm.then_inc(s_acol, 1)
        nc.tensor.wait_ge(s_c2, 1)
        nc.tensor.wait_ge(s_aks, 1)
        nc.tensor.wait_ge(s_acs, 1)
        for h in range(MH):
            (nc.tensor.matmul(RB[h][:, :], SELH[0:MH, h, :], ROWS[0:MH, 1:3].rearrange("p a t -> p (a t)"),
                              start=True, stop=True).then_inc(s_rb, 1))

    def mdecay_act():
        for h in range(MH):
            nc.scalar.wait_ge(s_dt, h + 1)
            nc.scalar.activation(EXPM[:, h], RB[h][:, T2:2 * T2], ACT.Exp, scale=-1.0)
            nc.scalar.activation(DTE[:, h, P:2 * P], RB[h][:, P:2 * P], ACT.Exp, bias=ACOL[:, 0, h:h + 1])
            v = DTE[:, h].rearrange("p (a t) -> p a t", a=3)[:, 0:3:2]
            nc.scalar.activation(v, v, ACT.Exp).then_inc(s_de, 1)

    def mdecay_dve():
        nc.vector.wait_ge(s_c2, 1)
        for h in range(MH):
            nc.vector.wait_ge(s_rb, h + 1)
            for s in range(2):
                ins = nc.vector.scalar_tensor_tensor(out=DTE[:, h, 2 * s * P:2 * s * P + P], in0=RB[h][:, s * P:(s + 1) * P],
                                                     scalar=ACOL[:, s, h:h + 1], in1=NEGC, op0=ALU.add, op1=ALU.add)
            ins.then_inc(s_dt, 1)

    def mscore_pe():
        nc.tensor.wait_ge(s_silu, 1)
        nc.tensor.wait_ge(s_de, MH)
        for h in range(MH):
            r = 64 * (h % 2)
            q, k = MQK[r:r + 64, h // 2], MQK[r:r + 64, 2 + h // 2]
            nc.tensor.matmul(RB[h][:, 0:T2], k[:, 0:P], q, start=True, stop=True, tile_position=(r, 0))
            (nc.tensor.matmul(RB[h][:, T2:T2 + P], k[:, P:T2], q[:, P:T2], start=True, stop=True, tile_position=(r, 0))
             .then_inc(s_ms2, 1))

    def mprod_dve():
        for h in range(MH):
            nc.vector.wait_ge(s_ms2, h + 1)
            nc.vector.wait_ge(s_de, h + 1)
            (nc.vector.scalar_tensor_tensor(out=PTM[:, h], in0=RB[h][:, 0:3 * P], scalar=float(MQK_SCALE), in1=DTE[:, h],
                                            op0=ALU.mult, op1=ALU.mult).then_inc(s_pt, 1))

    def mnum_pe():
        nc.tensor.wait_ge(s_dev, FIRST["aq_mv"] + 4)
        for h in range(MH):
            nc.tensor.wait_ge(s_pt, h + 1)
            for i in range(2):
                w = [MVT[:, s, h * P:(h + 1) * P] if i == 0 else ones[:, :] for s in range(2)]
                o = i * T2
                nc.tensor.matmul(RB[h][:, o:o + T2], w[0], PTM[:, h, 0:T2], start=True, stop=False,
                                 skip_group_check=True)
                mm = nc.tensor.matmul(RB[h][:, o + P:o + T2], w[1], PTM[:, h, T2:T2 + P], start=False, stop=True,
                                      skip_group_check=True)
            mm.then_inc(s_num, 1)

    def mout_dve(link):
        for h in range(MH):
            nc.vector.wait_ge(s_num, h + 1)
            link(nc.vector.scalar_tensor_tensor(out=RH[:, h], in0=RB[h][:, T2:2 * T2], scalar=-1.0, in1=EXPM[:, h],
                                                op0=ALU.mult, op1=ALU.max))
            link(nc.vector.tensor_tensor(RH[:, h], RB[h][:, T2:2 * T2], RH[:, h], ALU.max))
            link(nc.vector.reciprocal(RH[:, h], RH[:, h]))
            nc.vector.tensor_tensor(HM[:, h], RB[h][:, 0:T2], RH[:, h], ALU.mult).then_inc(s_hm, 1)

    def mnorm_act():
        nc.scalar.wait_ge(s_hm, MH)
        nc.scalar.activation(SQ[:, 0:MH, 0:T2], HM[:, :, :], ACT.Square).then_inc(s_hsq, 1)
        nc.scalar.wait_ge(s_hs, 1)
        (nc.scalar.activation(RH[:, :, :], psB[:, :, :].rearrange("p b (h t) -> p (b h) t", h=2), ACT.Sqrt,
                              bias=epsc[:, 0:1], scale=1.0 / MV).then_inc(s_hr, 1))

    def mnorm_pe():
        nc.tensor.wait_ge(s_hsq, 1)
        for h in range(MH):
            mm = nc.tensor.matmul(psB[:, h // 2, (h % 2) * T2:(h % 2) * T2 + T2], ones[:, :], SQ[:, h, 0:T2],
                                  start=True, stop=True)
        mm.then_inc(s_hs, 1)

    def mnorm_dve(link):
        nc.vector.wait_ge(s_hr, 1)
        link(nc.vector.reciprocal(RH[:, :, :], RH[:, :, :]))
        for h in range(MH):
            ins = nc.vector.scalar_tensor_tensor(out=HM[:, h], in0=HM[:, h], scalar=col("g_mhead_2", h), in1=RH[:, h],
                                                 op0=ALU.mult, op1=ALU.mult)
        link(ins)
        nc.vector.tensor_tensor(CAT[:, 0:4], HM[:, :, :], MO, ALU.mult).then_inc(s_cat, 1)

    WB = [psD[:, i] for i in range(4)]

    def wscore_pe():
        nc.tensor.wait_ge(s_dev, FIRST["aq_mv"] + 4)
        nc.tensor.wait_ge(s_aks, 1)
        for i in range(AH):
            if i >= 4:
                nc.tensor.wait_ge(s_wsb, i - 3)
            r = 64 * (i % 2)
            q, k, o = AQ[r:r + 64, i // 2], AK[r:r + 64], WB[i % 4]
            nc.tensor.matmul(o[:, 0:P], q[:, 0:P], k[:, 0:P], start=True, stop=True, tile_position=(r, 0))
            (nc.tensor.matmul(o[:, P:3 * P], q[:, P:T2], k[:, 0:T2], start=True, stop=True, tile_position=(r, 0))
             .then_inc(s_ws, 1))

    def wsoft1_dve(link):
        nc.vector.wait_ge(s_c2, 1)
        for i in range(AH):
            nc.vector.wait_ge(s_ws, i + 1)
            (nc.vector.scalar_tensor_tensor(out=SB[:, i], in0=WB[i % 4][:, 0:3 * P], scalar=float(ADH) ** -0.5,
                                            in1=MASK3.rearrange("p a s -> p (a s)"), op0=ALU.mult, op1=ALU.add)
             .then_inc(s_wsb, 1))
        nc.vector.wait_ge(s_wsb, AH)
        nc.vector.tensor_reduce(MX[:, 0], SB[:, :, 0:P], AX.X, ALU.max)
        link(nc.vector.tensor_reduce(MX[:, 1], SB[:, :, P:3 * P], AX.X, ALU.max))
        sk = col("sinks_2", 0, AH).unsqueeze(1).to_broadcast([P, 2, AH])
        link(nc.vector.tensor_tensor(MX[:, :, :], MX[:, :, :], sk, ALU.max))
        nc.vector.tensor_scalar(NMX[:, :, :], MX[:, :, :], -1.0, None, ALU.mult).then_inc(s_wmx, 1)
        nc.vector.tensor_tensor(ESK[:, :, :], sk, MX[:, :, :], ALU.subtract).then_inc(s_wmx, 1)

    def wsoft2_dve(link):
        nc.vector.wait_ge(s_wex, 1)
        link(nc.vector.tensor_tensor(SUM[:, :, :], SUM[:, :, :], ESK[:, :, :], ALU.add))
        link(nc.vector.reciprocal(SUM[:, :, :], SUM[:, :, :]))
        nc.vector.tensor_tensor(SB[:, :, 0:P], SB[:, :, 0:P], SUM[:, 0].unsqueeze(2).to_broadcast([P, AH, P]), ALU.mult)
        (nc.vector.tensor_tensor(SB[:, :, P:3 * P], SB[:, :, P:3 * P], SUM[:, 1].unsqueeze(2).to_broadcast([P, AH, 2 * P]),
                                 ALU.mult).then_inc(s_wpn, 1))

    def wexp_act(link):
        nc.scalar.wait_ge(s_wmx, 1)
        for i in range(AH):
            nc.scalar.activation(SB[:, i, 0:P], SB[:, i, 0:P], ACT.Exp, bias=NMX[:, 0, i:i + 1],
                                 accum_out=SUM[:, 0, i:i + 1])
            nc.scalar.activation(SB[:, i, P:3 * P], SB[:, i, P:3 * P], ACT.Exp, bias=NMX[:, 1, i:i + 1],
                                 accum_out=SUM[:, 1, i:i + 1])
        nc.scalar.wait_ge(s_wmx, 2)
        nc.scalar.activation(ESK[:, :, :], ESK[:, :, :], ACT.Exp).then_inc(s_wex, 1)

    WPT = [DTE, PTM]

    def wout_pe():
        def turn(i):
            if i >= 4:
                nc.tensor.wait_ge(s_wtc, i - 3)
            for b, x in enumerate((0, 1, 2)):
                mm = nc.tensor.transpose(WB[i % 4][:, b * P:(b + 1) * P], SB[:, i, x * P:(x + 1) * P], ident[:, :])
            mm.then_inc(s_wt, 1)

        def product(i):
            r, p = 64 * (i % 2), WPT[i // 4][:, i % 4]
            o = RB[i // 2][r:r + 64]
            nc.tensor.wait_ge(s_wtc, i + 1)
            kv = slice(64 * (i % 2), 64 * (i % 2) + 64)
            nc.tensor.matmul(o[:, 0:T2], AV[:, 0, kv], p[:, 0:T2], start=True, stop=False, tile_position=(0, r),
                             skip_group_check=True)
            mm = nc.tensor.matmul(o[:, P:T2], AV[:, 1, kv], p[:, T2:3 * P], start=False, stop=True,
                                  tile_position=(0, r), skip_group_check=True)
            if i % 2:
                mm.then_inc(s_wo_, 1)
        nc.tensor.wait_ge(s_wpn, 1)
        nc.tensor.wait_ge(s_hr, 1)
        nc.tensor.wait_ge(s_hm, MH)
        for i in range(AH):
            turn(i)
            if i >= 2:
                product(i - 2)
        product(AH - 2)
        product(AH - 1)

    def wout_act():
        for i in range(AH):
            nc.scalar.wait_ge(s_wt, i + 1)
            nc.scalar.activation(WPT[i // 4][:, i % 4], WB[i % 4][:, 0:3 * P], ACT.Identity).then_inc(s_wtc, 1)
        for p in range(4):
            nc.scalar.wait_ge(s_wo_, p + 1)
            nc.scalar.activation(CAT[:, 4 + p], RB[p][:, 0:T2], ACT.Identity).then_inc(s_woc, 1)

    s_xs, s_xmx, s_xex, s_xpn, s_xt, s_xtc, s_xo, s_xoc = (sem(n) for n in (
        "s_xs", "s_xmx", "s_xex", "s_xpn", "s_xt", "s_xtc", "s_xo", "s_xoc"))

    def cross_pe():
        nc.tensor.wait_ge(s_dev, FIRST["xq"] + 4)
        for h in range(XH):
            for t in range(2):
                for m in range(2):
                    mm = nc.tensor.matmul(RB[h][:, t * T2:(t + 1) * T2], QX[:, 2 * h + m, t * P:(t + 1) * P],
                                          KX[:, 2 * h + m], start=(m == 0), stop=(m == 1))
            mm.then_inc(s_xs, 1)
        for h in range(XH):
            nc.tensor.wait_ge(s_xpn, h + 1)
            for t in range(2):
                for s in range(2):
                    mm = nc.tensor.transpose(WB[h][:, s * T2 + t * P:s * T2 + t * P + P],
                                             XP[:, h, t, s * P:(s + 1) * P], ident[:, :])
            mm.then_inc(s_xt, 1)
        for h in range(XH):
            nc.tensor.wait_ge(s_xtc, h + 1)
            for m in range(2):
                for s in range(2):
                    mm = nc.tensor.matmul(RB[h][:, m * T2:(m + 1) * T2], XV[:, s, h * XD + m * P:h * XD + (m + 1) * P],
                                          XPT[:, h, s], start=(s == 0), stop=(s == 1))
            mm.then_inc(s_xo, 1)

    def cross_dve(link):
        sc = float(XD) ** -0.5
        for h in range(XH):
            nc.vector.wait_ge(s_xs, h + 1)
            link(nc.vector.tensor_reduce(XMX[:, h], RB[h][:, :].rearrange("p (t s) -> p t s", t=2), AX.X, ALU.max))
            nc.vector.tensor_scalar(XNM[:, h], XMX[:, h], -sc, None, ALU.mult).then_inc(s_xmx, 1)
        for h in range(XH):
            nc.vector.wait_ge(s_xex, h + 1)
            link(nc.vector.reciprocal(XRC[:, h], XSM[:, h]))
            for t in range(2):
                ins = nc.vector.tensor_scalar(XP[:, h, t], XP[:, h, t], XRC[:, h, t:t + 1], None, ALU.mult)
            ins.then_inc(s_xpn, 1)
        for h in range(XH):
            nc.vector.wait_ge(s_xt, h + 1)
            nc.vector.tensor_copy(XPT[:, h].rearrange("p s t -> p (s t)"), WB[h]).then_inc(s_xtc, 1)

    def cross_act():
        sc = float(XD) ** -0.5
        for h in range(XH):
            nc.scalar.wait_ge(s_xmx, h + 1)
            for t in range(2):
                ins = nc.scalar.activation(XP[:, h, t], RB[h][:, t * T2:(t + 1) * T2], ACT.Exp, bias=XNM[:, h, t:t + 1],
                                           scale=sc, accum_out=XSM[:, h, t:t + 1])
            ins.then_inc(s_xex, 1)
        for h in range(XH):
            nc.scalar.wait_ge(s_xo, h + 1)
            (nc.scalar.activation(OX[:, 2 * h:2 * h + 2], RB[h][:, :].rearrange("p (m t) -> p m t", m=2), ACT.Identity)
             .then_inc(s_xoc, 1))

    (s_sk, s_ps, s_psc, s_tt, s_ttc, s_eid, s_gate, s_io, s_adn, s_gel, s_coef, s_use, s_fin, s_fsq, s_frt) = (
        sem(n) for n in (
            "s_sk", "s_ps", "s_psc", "s_tt", "s_ttc", "s_eid", "s_gate", "s_io", "s_adn", "s_gel", "s_coef", "s_use",
            "s_fin", "s_fsq", "s_frt"))
    NB = 8
    s_gb = [sem(f"s_gb{j}") for j in range(NB)]

    def peer_pe():
        nc.tensor.wait_ge(s_sk, 48)
        nc.tensor.wait_ge(s_dev, FIRST["pq"] + 8)
        for t in range(2):
            for h in range(4):
                b = 4 * t + h
                if b >= 4:
                    nc.tensor.wait_ge(s_psc, b - 3)
                for x in range(4):
                    i = 4 * h + x
                    mm = nc.tensor.matmul(WB[h][:, x * PK:(x + 1) * PK], QH[:, i, t * P:(t + 1) * P], SKT[:, i % 2],
                                          start=True, stop=True)
                mm.then_inc(s_ps, 1)
        for i, src in enumerate((XN2, XN2, H2, H2)):
            t = i % 2
            if i % 2 == 0 and i:
                nc.tensor.wait_ge(s_ttc, i)
            for k in range(KT):
                o = RB[2 * t + k // 4]
                mm = nc.tensor.transpose(o[:, (k % 4) * P:(k % 4) * P + P], src[:, k, t * P:(t + 1) * P], ident[:, :])
            mm.then_inc(s_tt, 1)

    def peer_act(link):
        for b in range(8):
            nc.scalar.wait_ge(s_ps, b + 1)
            (nc.scalar.activation(SCO[:, b // 4, 4 * (b % 4):4 * (b % 4) + 4], WB[b % 4].rearrange("p (x n) -> p x n", x=4),
                                  ACT.Identity).then_inc(s_psc, 1))
        for i, dst in enumerate((XTOK, XTOK, HTOK, HTOK)):
            t = i % 2
            nc.scalar.wait_ge(s_tt, i + 1)
            nc.scalar.activation(dst[:, t, 0:512], RB[2 * t], ACT.Identity)
            nc.scalar.activation(dst[:, t, 512:1024], RB[2 * t + 1], ACT.Identity).then_inc(s_ttc, 1)
        for t in range(2):
            nc.scalar.wait_ge(s_eid, 2 * t + 2)
            link(nc.scalar.activation(GT[:, t], GT[:, t], ACT.Exp))
            nc.scalar.sem_inc(s_gate, 1)
        for t in range(2):
            nc.scalar.wait_ge(s_adc, ROUNDS * (t + 1))
            nc.scalar.activation(AD[:, t], AD[:, t], ACT.Gelu).then_inc(s_gel, 1)
        for t in range(2):
            nc.scalar.wait_ge(s_fin, t + 1)
            nc.scalar.activation(JUNK[:, t], ACC[:, t], ACT.Square, accum_out=FS[:, t, 0:1]).then_inc(s_fsq, 1)
            nc.scalar.wait_ge(s_fsq, t + 1)
            (nc.scalar.activation(FS[:, t, 1:2], FS[:, t, 0:1], ACT.Sqrt, bias=epsc[:, 0:1], scale=1.0 / D)
             .then_inc(s_frt, 1))

    def top16(vals, idx, src, rows, link):
        for r in rows:
            ins = nc.vector.max(vals(r)[:, 0:8], src(r))
        link(ins)
        for r in rows:
            ins = nc.vector.max_index(idx(r)[:, 0:8], vals(r)[:, 0:8], src(r))
        for r in rows:
            ins = nc.vector.match_replace(src(r), vals(r)[:, 0:8], src(r), MAXNEG)
        link(ins)
        for r in rows:
            ins = nc.vector.max(vals(r)[:, 8:16], src(r))
        link(ins)
        for r in rows:
            ins = nc.vector.max_index(idx(r)[:, 8:16], vals(r)[:, 8:16], src(r))
        link(ins)

    def route_dve(t, link):
        tt = nc.vector.tensor_tensor
        nc.vector.wait_ge(s_psc, 4 * t + 4)
        top16(lambda r: VAL[:, r], lambda r: IDX[:, r], lambda r: SCO[:, t, r], range(16), link)
        v = VAL.rearrange("p (h c) k -> p h c k", c=2)
        cs4 = CS.rearrange("p h (a b) -> p h a b", a=PTOP)
        full = [P, PH, PTOP, PTOP]
        link(nc.vector.tensor_copy(IDF[:, :, :], IDX))
        for h in range(PH):
            ins = tt(cs4[:, h], v[:, h, 0].unsqueeze(2).to_broadcast([P, PTOP, PTOP]),
                     v[:, h, 1].unsqueeze(1).to_broadcast([P, PTOP, PTOP]), ALU.add)
        link(ins)
        top16(lambda r: TV[:, t, r], lambda r: POS[:, r], lambda r: CS[:, r], range(PH), link)
        link(tt(GT[:, t], TV[:, t], TV[:, t, :, 0:1].to_broadcast([P, PH, PTOP]), ALU.subtract))
        nc.vector.sem_inc(s_eid, 1)
        f = IDF.rearrange("p (h c) k -> p h c k", c=2)
        nc.vector.wait_ge(s_io, 2)
        for c, sel in ((0, SEL1), (1, SEL2)):
            if c == 0:
                link(nc.vector.tensor_scalar(PA, POS, 4, None, ALU.logical_shift_right))
            else:
                link(nc.vector.tensor_scalar(PA, POS, 15, None, ALU.bitwise_and))
            link(nc.vector.tensor_copy(PAF[:, :, :], PA))
            hk = PAF.rearrange("p h k -> p (h k)").unsqueeze(2).to_broadcast([P, PH * PTOP, PTOP])
            oh = OH.rearrange("p h k j -> p (h k) j")
            link(tt(oh, hk, IOTA.unsqueeze(1).to_broadcast([P, PH * PTOP, PTOP]), ALU.is_equal))
            link(tt(OH, OH, f[:, :, c].unsqueeze(2).to_broadcast(full), ALU.mult))
            link(nc.vector.tensor_reduce(sel.rearrange("p h k -> p (h k)"), oh, AX.X, ALU.add))
        e = EID[:, t].rearrange("p (h k) -> p h k", h=PH)
        nc.vector.scalar_tensor_tensor(out=e, in0=SEL1, scalar=float(PK), in1=SEL2, op0=ALU.mult,
                                       op1=ALU.add).then_inc(s_eid, 1)

    def gates_dve(t, link):
        nc.vector.wait_ge(s_gate, t + 1)
        link(nc.vector.tensor_reduce(GM, GT[:, t], AX.X, ALU.add))
        link(nc.vector.reciprocal(GM, GM))
        link(nc.vector.tensor_tensor(GT[:, t], GT[:, t], GM.unsqueeze(2).to_broadcast([P, PH, PTOP]), ALU.mult))

    NSLOT = PH * PTOP
    ROUNDS = NSLOT // NB

    def gathers_pool():
        g = nc.gpsimd
        for part in range(4):
            t, table = part % 2, a["expert_down"] if part < 2 else a["expert_up"]
            if part < 2:
                g.wait_ge(s_eid, 2 * t + 2)
            for i in range(NSLOT):
                n = NSLOT * part + i
                if n >= NB:
                    g.wait_ge(s_use, n - NB + 1)
                (g.indirect_dma_start(GB_[:, n % NB], None, table,
                                      bass.IndirectOffsetOnAxis(ap=EID[:, t, i:i + 1], axis=0))
                 .then_inc(s_gb[n % NB], 16))

    def down_dve(t):
        base = ROUNDS * t
        with nc.vector.Fori(0, ROUNDS, 1) as it:
            for j in range(NB):
                nc.vector.wait_ge(s_gb[j], 16 * (base + 1) + 16 * it)
                (nc.vector.tensor_tensor_reduce(GB_[:, j], GB_[:, j], XTOK[:, t], 1.0, 0.0, ALU.mult, ALU.add,
                                                ADB[:, j:j + 1]).then_inc(s_use, 1))
            nc.vector.wait_ge(s_use, NB * (base + 1) + NB * it)
            nc.vector.tensor_copy(AD[:, t, bass.ds(NB * it, NB)], ADB).then_inc(s_adc, 1)
            nc.vector.wait_ge(s_adc, base + 1 + it)

    s_adc = sem("s_adc")

    def up_dve(t):
        base = ROUNDS * (2 + t)
        with nc.vector.Fori(0, ROUNDS, 1) as it:
            for j in range(NB):
                acc = (ACC[:, t], ACB)[j % 2]
                nc.vector.wait_ge(s_gb[j], 16 * (base + 1) + 16 * it)
                nc.vector.wait_ge(s_use, NB * base - 1 + j + NB * it)
                (nc.vector.scalar_tensor_tensor(out=acc, in0=GB_[:, j], scalar=COEF[:, t, bass.ds(NB * it + j, 1)],
                                                in1=acc, op0=ALU.mult, op1=ALU.add).then_inc(s_use, 1))

    def residual_dve(y, gain, T, h, link, Z=ZG):
        for k in range(KT):
            ins = nc.vector.scalar_tensor_tensor(out=Z[:, k, 0:T], in0=y[:, k, 0:T], scalar=col(gain, k),
                                                 in1=RT[:, 1, 0:T], op0=ALU.mult, op1=ALU.mult)
        link(ins)
        nc.vector.tensor_tensor(h, h, Z[:, :, 0:T], ALU.add).then_inc(s_h, 1)

    def postnorm_dve(i, y, ready, n, T, gain, h, link):
        nc.vector.wait_ge(ready, n)
        nc.vector.tensor_tensor(SQ[:, 0:4, 0:T], y[:, 0:4], y[:, 0:4], ALU.mult).then_inc(s_sqv, 1)
        nc.vector.wait_ge(s_rt, i + 1)
        link(nc.vector.reciprocal(RT[:, 1, 0:T], RT[:, 0, 0:T]))
        residual_dve(y, gain, T, h, link)

    s_out = sem("s_out")

    def finish(sp):
        for t in range(2):
            sp.wait_ge(s_done, t + 1)
            sp.dma_start(a["out"][t * P:(t + 1) * P], ACC[:, t]).then_inc(s_out, 16)
        sp.wait_ge(s_out, 32)
    s_done = sem("s_done")

    @block.sync
    def _(sp):
        sp.dma_start(H, a["xT"]).then_inc(s_x, 16)
        sp.dma_start(cols[:, :], a["cols"]).then_inc(s_cols, 16)
        w = a["w"]

        def load(j, c):
            sp.dma_start(ring[:, j].rearrange("p k n -> p (k n)"),
                         w[bass.ds(c, 1)].rearrange("a p n -> p (a n)") if not isinstance(c, int) else w[c]
                         ).then_inc(s_w[j], 16)
        for j in range(RING):
            load(j, j)
        with sp.Fori(1, NCHUNK // RING, 1) as it:
            for j in range(RING):
                sp.wait_ge(s_chunk, RING * it + (j + 1 - RING))
                load(j, RING * it + j)
        finish(sp)

    @block.gpsimd
    def _(pool):
        g = nc.gpsimd
        n = [0]

        def link(ins):
            n[0] += 1
            ins.then_inc(s_p, 1)
            pool.wait_ge(s_p, n[0])
        g.memset(ones[:, :], 1.0)
        g.memset(epsc[:, :], EPS)
        g.memset(rmask[:, :], 1.0)
        g.memset(ident[:, :], 0.0)
        link(g.memset(SEL, 0.0))
        rm = rmask[:, :].rearrange("p (h t) -> p h t", h=GH)
        for t in GSTART:
            g.memset(rm[:, :, t:t + 1], 0.0)
        g.affine_select(out=ident[:, :], in_=ident[:, :], compare_op=ALU.not_equal, fill=1.0, base=0,
                        pattern=[[-1, P]], channel_multiplier=1)
        v = SEL[0:ST].rearrange("p q (r c) -> p q r c", r=4)
        g.affine_select(out=v, in_=v, compare_op=ALU.not_equal, fill=1.0, base=0,
                        pattern=[[-4, 8], [-1, 4], [0, 32]], channel_multiplier=1)
        link(g.affine_select(out=cmask[:, :], in_=ones[:, :], compare_op=ALU.is_ge, fill=0.0, base=0,
                             pattern=[[1, P]], channel_multiplier=-1))
        g.memset(cmask[0:GCH, GCH:P], 0.0).then_inc(s_const, 1)
        pool.wait_ge(s_s5c, 32)
        flat2 = lambda v: v.rearrange("p j h -> p (j h)")
        g.tensor_scalar(flat2(CM[1]), flat2(CM[0]), -1.0, None, ALU.mult)
        g.tensor_scalar(flat2(CM[2]), flat2(CM[2]), -1.0, None, ALU.mult).then_inc(s_cn, 1)
        s5_pool()
        pool.wait_ge(s_og, 1)
        pool.wait_ge(s_hrt, 4)
        pool.dma_start(WKV, a["w_akv"]).then_inc(s_kv, 16)
        g.memset(NEGC, 0.0)
        g.memset(SELH, 0.0)
        link(g.memset(MASK3, 0.0))
        g.affine_select(out=NEGC, in_=NEGC, compare_op=ALU.is_ge, fill=NEG, base=0, pattern=[[1, P]],
                        channel_multiplier=-1)
        for b in (0, 2):
            g.affine_select(out=MASK3[:, b], in_=MASK3[:, b], compare_op=ALU.is_ge, fill=NEG, base=0,
                            pattern=[[-1, P]], channel_multiplier=1)
        g.affine_select(out=MASK3[:, 1], in_=MASK3[:, 1], compare_op=ALU.is_ge, fill=NEG, base=-1,
                        pattern=[[1, P]], channel_multiplier=-1)
        g.affine_select(out=SELH[0:MH], in_=SELH[0:MH], compare_op=ALU.not_equal, fill=1.0, base=0,
                        pattern=[[-1, MH], [0, P]], channel_multiplier=1).then_inc(s_c2, 1)
        pool.wait_ge(s_xoc, XH)
        pool.dma_start(SKT[:, 0], a["sub1"]).then_inc(s_sk, 16)
        pool.dma_start(SKT[:, 1], a["sub2"]).then_inc(s_sk, 16)
        pool.dma_start(GFIN, a["g_final"]).then_inc(s_sk, 16)
        g.iota(IOI, pattern=[[1, PTOP]], base=0, channel_multiplier=0).then_inc(s_io, 1)
        pool.wait_ge(s_io, 1)
        g.tensor_copy(IOTA, IOI).then_inc(s_io, 1)
        gathers_pool()

    @block.scalar
    def _(act):
        act.dma_start(AR[0:ST], a["a_re"]).then_inc(s_s5, 16)
        act.dma_start(AI[0:ST], a["a_im"]).then_inc(s_s5, 16)
        act.dma_start(LST[0:ST], a["log_step"]).then_inc(s_s5, 16)
        act.dma_start(walow[:, :, :], a["w_alow"]).then_inc(s_small, 16)
        act.dma_start(wgu[:, :], a["w_gate_up"]).then_inc(s_small, 16)
        act.dma_start(wif[:, :, :], a["w_if"]).then_inc(s_small, 16)
        act.dma_start(BR, a["b_re"]).then_inc(s_s5b, 16)
        act.dma_start(BI, a["b_im"]).then_inc(s_s5b, 16)
        act.dma_start(CM[0], a["c_re"]).then_inc(s_s5c, 16)
        act.dma_start(CM[2], a["c_im"]).then_inc(s_s5c, 16)
        n = [0]

        def link(ins):
            n[0] += 1
            ins.then_inc(s_a, 1)
            act.wait_ge(s_a, n[0])
        act.wait_ge(s_const, 1)
        norm_act(0, H, s_x, 16, T1)
        act.wait_ge(s_cols, 16)
        dense_act(FIRST["u"], 1, T1, evac(UU, ACT.Identity))
        dense_act(FIRST["qk"], 1, T1, evac(QK, ACT.Identity))
        gate_act(link)
        act.wait_ge(s_bd, 2)
        dense_act(FIRST["r"], 1, T1, evac(RR, ACT.Silu))
        dense_act(FIRST["zg"], 1, T1, evac(ZG, ACT.Sigmoid))
        dense_act(FIRST["zs"], 1, T1, evac(ZS, ACT.Sigmoid))
        for j in range(RING):
            v1_act(j)
        act.wait_ge(s_ye, 8)
        act.activation(YS, YS, ACT.Gelu_apprx_tanh).then_inc(s_gs, 1)
        gla_exp_act()
        glu_act(0)
        glu_act(1)
        gla_act_b()
        dense_act(FIRST["w_o_gla"], 1, T1, evac(RR, ACT.Identity))
        dense_act(FIRST["w_out"], 1, T1, evac(YS, ACT.Identity))
        norm_act(1, YS, s_dev, FIRST["w_out"] + 4, T1)
        norm_act(2, H, s_h, 1, T1)
        dense_act(FIRST["w_ff1"], 4, T1, evac(FFH, ACT.Relu))
        act.wait_ge(s_mix, 1)
        act.dma_start(MEM, a["memT"]).then_inc(s_mem, 16)
        norm_act(3, MEM, s_mem, 16, T2)
        ff2_act(ZS, T1)
        norm_act(4, ZS, s_dev, FIRST["w_ff2"] + 16, T1)
        for j in range(2):
            pair_act(FIRST["xk"], j, KX[:, 2 * j:2 * j + 2])
        norm_act(5, H2, s_h, 2, T2)
        for j in range(2, 4):
            pair_act(FIRST["xk"], j, KX[:, 2 * j:2 * j + 2])
        for j in range(4):
            tok_act(FIRST["xv"], j, XV[:, :, j * CW:(j + 1) * CW])
        for j in range(4):
            if j < 2:
                pair_act(FIRST["mqk_mo"], j, MQKP[:, 2 * j:2 * j + 2, 3:3 + T2])
            else:
                pair_act(FIRST["mqk_mo"], j, MO[:, 2 * j - 4:2 * j - 2], ACT.Sigmoid)
        small2_act(link)
        for j in range(2):
            pair_act(FIRST["aq_mv"], j, AQ[:, 2 * j:2 * j + 2])
        for j in range(2):
            tok_act(FIRST["aq_mv"], 2 + j, MVT[:, :, j * CW:(j + 1) * CW])
        act.wait_ge(s_conv, 1)
        act.activation(MQK[:, :, :], MQK[:, :, :], ACT.Silu).then_inc(s_silu, 1)
        mdecay_act()
        wexp_act(link)
        mnorm_act()
        wout_act()
        for j in range(4):
            pair_act(FIRST["w_out_2"], j, DEL[:, 2 * j:2 * j + 2])
        norm_act(6, H2, s_h, 3, T2)
        for j in range(4):
            pair_act(FIRST["xq"], j, QX[:, 2 * j:2 * j + 2])
        cross_act()
        for j in range(4):
            pair_act(FIRST["xo"], j, DEL[:, 2 * j:2 * j + 2])
        norm_act(7, H2, s_h, 4, T2)
        for j in range(8):
            pair_act(FIRST["pq"], j, QH[:, 2 * j:2 * j + 2])
        peer_act(link)

    @block.vector
    def _(dve):
        n = [0]

        def link(ins):
            n[0] += 1
            ins.then_inc(s_v, 1)
            dve.wait_ge(s_v, n[0])
        dve.wait_ge(s_cols, 16)
        norm_dve(0, H, s_x, 16, T1, "g_mix_pre", XN, link)
        s5_param_dve(link)
        dve.wait_ge(s_ltc, 1)
        dve.wait_ge(s_dev, FIRST["u"] + 4)
        s5_dve(link)
        gate_dve(link)
        gla_prep_dve(link)
        gla_dve_a(link)
        gla_dve_norm(link)
        dve.wait_ge(s_dev, FIRST["w_glu"] + 8)
        link(dve.tensor_tensor(UU, UU, EX, ALU.mult))
        link(dve.tensor_tensor(UU, UU, ZS, ALU.mult))
        dve.wait_ge(s_dev, FIRST["w_o_gla"] + 4)
        link(dve.tensor_tensor(RR, RR, ZG, ALU.mult))
        dve.tensor_tensor(RR, RR, UU, ALU.add).then_inc(s_mix, 1)
        postnorm_dve(1, YS, s_dev, FIRST["w_out"] + 4, T1, "g_mix_post", H, link)
        norm_dve(2, H, s_h, 1, T1, "g_ffn_pre", XN, link)

        def square(it):
            for j in range(RING):
                dve.wait_ge(s_dev, FIRST["w_ff1"] + 4 * it + (j + 1))
                v = FFH[:, bass.ds(8 * it + 2 * j, 2)]
                dve.tensor_tensor(v, v, v, ALU.mult).then_inc(s_ffh, 1)
        repeat(dve, 4, square)
        norm_dve(3, MEM, s_mem, 16, T2, "g_mem_2", MEM, link)
        postnorm_dve(4, ZS, s_dev, FIRST["w_ff2"] + 16, T1, "g_ffn_post", H, link)
        norm_dve(5, H2, s_h, 2, T2, "g_mix_2", XN2, link)
        link(dve.memset(MQKP[:, :, 0:3], 0.0))
        dve.wait_ge(s_dev, FIRST["mqk_mo"] + 2)
        conv_dve(link)
        mrows_dve(link)
        mdecay_dve()
        wsoft1_dve(link)
        mprod_dve()
        wsoft2_dve(link)
        mout_dve(link)
        mnorm_dve(link)
        dve.wait_ge(s_dev, FIRST["w_out_2"] + 4)
        dve.tensor_tensor(H2, H2, DEL, ALU.add).then_inc(s_h, 1)
        norm_dve(6, H2, s_h, 3, T2, "g_cross_2", XN2, link)
        cross_dve(link)
        dve.wait_ge(s_dev, FIRST["xo"] + 4)
        dve.tensor_tensor(H2, H2, DEL, ALU.add).then_inc(s_h, 1)
        norm_dve(7, H2, s_h, 4, T2, "g_ffn_2", XN2, link)
        route_dve(0, link)
        dve.wait_ge(s_ttc, 4)
        gates_dve(0, link)
        route_dve(1, link)
        gates_dve(1, link)
        down_dve(0)
        down_dve(1)
        for t in range(2):
            dve.wait_ge(s_gel, t + 1)
            link(dve.tensor_tensor(COEF[:, t], AD[:, t], GT[:, t].rearrange("p h k -> p (h k)"), ALU.mult))
        for t in range(2):
            dve.memset(ACC[:, t], 0.0)
            link(dve.memset(ACB, 0.0))
            up_dve(t)
            dve.wait_ge(s_use, NB * ROUNDS * (3 + t))
            link(dve.tensor_tensor(ACC[:, t], ACC[:, t], ACB, ALU.add))
            dve.tensor_tensor(ACC[:, t], ACC[:, t], HTOK[:, t], ALU.add).then_inc(s_fin, 1)
            dve.wait_ge(s_frt, t + 1)
            link(dve.reciprocal(FS[:, t, 2:3], FS[:, t, 1:2]))
            dve.wait_ge(s_sk, 48)
            dve.scalar_tensor_tensor(out=ACC[:, t], in0=ACC[:, t], scalar=FS[:, t, 2:3], in1=GFIN, op0=ALU.mult,
                                     op1=ALU.mult).then_inc(s_done, 1)

    @block.tensor
    def _(pe):
        pe.wait_ge(s_const, 1)
        norm_pe(0, T1)
        pe.wait_ge(s_xn, 1)
        dense_pe(FIRST["u"], 1, XN, T1)
        dense_pe(FIRST["qk"], 1, XN, T1)
        s5_param_pe()
        pe.wait_ge(s_ltc, 1)
        gate_pe()
        pe.wait_ge(s_gzc, GH)
        for i in range(16):
            if i < 12:
                chunk_pe(FIRST["r"], i, XN, T1)
            else:
                v1_pe(i - 12)
            for j in (2 * i, 2 * i + 1):
                s5_bu(j)
                if j >= 2:
                    s5_y(j - 2)
        s5_y(ST - 2)
        s5_y(ST - 1)
        pe.wait_ge(s_gs, 1)
        dense_pe(FIRST["w_glu"], 1, YS, T1)
        gla_pe_a()
        dense_pe(FIRST["w_glu"] + 4, 1, YS, T1)
        gla_pe_b()
        gla_pe_norm()
        pe.wait_ge(s_og, 1)
        dense_pe(FIRST["w_o_gla"], 1, QK, T1)
        pe.wait_ge(s_mix, 1)
        dense_pe(FIRST["w_out"], 1, RR, T1)
        norm_pe(1, T1)
        norm_pe(2, T1)
        pe.wait_ge(s_xn, 2)
        dense_pe(FIRST["w_ff1"], 4, XN, T1)
        norm_pe(3, T2)
        pe.wait_ge(s_ffh, 16)
        pe.wait_ge(s_xn, 3)
        ff2_pe(FFH, T1)
        for j in range(2):
            chunk_pe(FIRST["xk"], j, MEM, T2)
        norm_pe(4, T1)
        for j in range(2, 4):
            chunk_pe(FIRST["xk"], j, MEM, T2)
        norm_pe(5, T2)
        for j in range(4):
            tok_pe(FIRST["xv"], j, MEM)
        pe.wait_ge(s_xn, 4)
        for j in range(4):
            chunk_pe(FIRST["mqk_mo"], j, XN2, T2)
        small2_pe()
        for j in range(2):
            chunk_pe(FIRST["aq_mv"], j, XN2, T2)
        for j in range(2):
            tok_pe(FIRST["aq_mv"], 2 + j, XN2)
        mrows_pe()
        wscore_pe()
        mscore_pe()
        mnum_pe()
        mnorm_pe()
        wout_pe()
        pe.wait_ge(s_cat, 1)
        pe.wait_ge(s_woc, 4)
        for j in range(4):
            chunk_pe(FIRST["w_out_2"], j, CAT, T2)
        norm_pe(6, T2)
        pe.wait_ge(s_xn, 5)
        for j in range(4):
            chunk_pe(FIRST["xq"], j, XN2, T2)
        cross_pe()
        pe.wait_ge(s_xoc, XH)
        for j in range(4):
            chunk_pe(FIRST["xo"], j, OX, T2)
        norm_pe(7, T2)
        pe.wait_ge(s_xn, 6)
        for j in range(8):
            chunk_pe(FIRST["pq"], j, XN2, T2)
        peer_pe()

    ctx.close()


OUTS = None


def kernel(**inputs):
    import concourse.bacc as bacc
    from concourse.bass_utils import run_bass_kernel_spmd
    ins = layout({k: np.asarray(v) for k, v in inputs.items()})
    nc = bacc.Bacc("TRN2", target_bir_lowering=False, num_devices=1)
    args = {}
    for name, v in ins.items():
        args[name] = nc.dram_tensor("in_" + name, v.shape, mybir.dt.from_np(v.dtype), kind="ExternalInput").ap()
    args["out"] = nc.dram_tensor("out_0", (SEQ, D), F32, kind="ExternalOutput").ap()
    build(nc, args)
    r = run_bass_kernel_spmd(nc, [{"in_" + k: v for k, v in ins.items()}], core_ids=[0])
    return r.results[0]["out_0"].reshape(1, SEQ, D)
```

```python
from contextlib import ExitStack

import numpy as np
import concourse.bass as bass
from concourse import mybir

F32 = mybir.dt.float32
I32 = mybir.dt.int32
U32 = mybir.dt.uint32
ALU = mybir.AluOpType
ACT = mybir.ActivationFunctionType
AX = mybir.AxisListType

P = 128
D = 1024
KT = D // P
EPS = 1e-6
SEQ, META = 256, 16
T1 = META + SEQ
T2 = SEQ
CW = 256
RING = 4
FF = 4 * D
GH, GDK, GDV, GCH = 4, 128, 256, 64
GSTART = [0] + [META + GCH * i for i in range(SEQ // GCH)]
TOK1 = [(0, META), (META, P), (META + P, P)]
SG, SN, SHG = 64, 64, 16
ST = SG * SN // P
SHALF = 8
MH, MQK, MV = 4, 64, 128
AH, AKV, ADH = 8, 2, 64
XH, XD = 4, 256
PH, PK, PTOP, PEXP = 8, 128, 16, 128 * 128

MQK_SCALE = MQK ** -0.5
MAGIC = 1.5 * 2.0 ** 23
NEG = -1.0e30
MAXNEG = -3.0e38

COLS = {}
_n = 0
for _name, _w in [("g_mix_pre", 8), ("g_mix_post", 8), ("g_ffn_pre", 8), ("g_ffn_post", 8), ("b_gate", 4),
                  ("gla_norm_g", 8), ("d_skip", 8), ("b_glu", 16), ("g_mix_2", 8), ("conv_w_2", 16),
                  ("conv_b_2", 4), ("g_mhead_2", 4), ("g_cross_2", 8), ("g_mem_2", 8), ("g_ffn_2", 8),
                  ("b_igate_2", 1), ("b_fgate_2", 1), ("sinks_2", 8)]:
    COLS[_name] = (_n, _w)
    _n += _w
NCOLS = _n

STREAM = [("u", 4), ("qk", 4), ("r", 4), ("zg", 4), ("zs", 4), ("v", 4), ("w_glu", 8), ("w_o_gla", 4),
          ("w_out", 4), ("w_ff1", 16), ("w_ff2", 16),
          ("xk", 4), ("xv", 4), ("mqk_mo", 4), ("aq_mv", 4), ("w_out_2", 4), ("xq", 4), ("xo", 4), ("pq", 8)]
FIRST = {}
_n = 0
for _name, _w in STREAM:
    FIRST[_name] = _n
    _n += _w
NCHUNK = _n


def layout(x):
    c = np.ascontiguousarray
    w1, w2 = x["w_in"][0], x["w_in_2"][0]
    b = np.cumsum([0, 512, 512, 1024, 1024, 16, 1024, 1024, 1024])
    q, k, v, r, al, u, zg, zs = (w1[:, b[i]:b[i + 1]] for i in range(8))
    b2 = np.cumsum([0, 256, 256, 512, 512, 4, 4, 512, 128, 128])
    mq, mk, mv, mo, mi, mf, aq, ak, av = (w2[:, b2[i]:b2[i + 1]] for i in range(9))
    pair = np.arange(AH).reshape(2, 4).T.reshape(-1)
    aqp = aq.reshape(D, AH, ADH)[:, pair].reshape(D, -1)
    wo2 = x["w_out_2"][0]
    wo2 = np.concatenate([wo2[:512], wo2[512:].reshape(AH, ADH, D)[pair].reshape(-1, D)])

    def chunks(m):
        kk, n = m.shape
        return m.reshape(kk // D, KT, P, n // CW, CW).transpose(3, 0, 2, 1, 4).reshape(-1, P, KT * CW)
    g = {"u": u, "qk": np.concatenate([q, k], 1), "r": r, "zg": zg, "zs": zs, "v": v, "w_glu": x["w_glu"][0],
         "w_o_gla": x["w_o_gla"][0], "w_out": x["w_out"][0], "w_ff1": x["w_ff1"][0], "w_ff2": x["w_ff2"][0],
         "xk": x["w_xk_2"][0], "xv": x["w_xv_2"][0], "mqk_mo": np.concatenate([mq, mk, mo], 1),
         "aq_mv": np.concatenate([aqp, mv], 1), "w_out_2": wo2, "xq": x["w_xq_2"][0], "xo": x["w_xo_2"][0],
         "pq": x["w_pq_2"][0]}
    fm = lambda m: m.reshape(-1, KT, P).transpose(2, 1, 0)

    table = np.zeros((P, NCOLS), np.float32)
    for name, (at, n) in COLS.items():
        v0 = x[name].reshape(-1)
        if name == "conv_w_2":
            table[:, at:at + n] = x[name][0].reshape(4, 4, P).transpose(2, 1, 0).reshape(P, 16)
        elif name in ("b_igate_2", "b_fgate_2"):
            table[0:4, at] = v0
        elif name == "sinks_2":
            table[:, at:at + n] = v0[None, pair]
        else:
            table[:, at:at + n] = v0.reshape(n, P).T
    h = np.concatenate([x["meta_tokens"], x["x"][0]], 0)
    cre, cim = (x[n][0].reshape(ST, 2, SHG, SN) for n in ("c_re", "c_im"))

    def cmat(m):
        o = np.zeros((2, SN, ST, 2, SHG), np.float32)
        for i in range(2):
            o[i, :, :, i, :] = m[:, i].transpose(2, 0, 1)
        return o.reshape(P, ST, 2 * SHG)

    def bmat(m):
        m = m.reshape(8, 4, 2, SN, SHG)
        o = np.zeros((4, 2, SHG, 8, 2, SN), np.float32)
        for i in range(2):
            o[:, i, :, :, i, :] = m[:, :, i].transpose(1, 3, 0, 2)
        return o.reshape(P, 8, P)
    out = {
        "xT": fm(h), "w": np.concatenate([chunks(g[n]) for n, _ in STREAM]), "cols": table,
        "a_re": x["a_re"].reshape(ST, P), "a_im": x["a_im"].reshape(ST, P), "log_step": x["log_step"].reshape(ST, 2),
        "w_alow": al.reshape(KT, P, 16).transpose(1, 0, 2), "w_gate_up": x["w_gate_up"][0],
        "b_re": bmat(x["b_re"][0]), "b_im": bmat(x["b_im"][0]), "c_re": cmat(cre), "c_im": cmat(cim),
        "memT": fm(x["mem_2"][0]), "w_if": np.concatenate([mi, mf], 1).reshape(KT, P, 2 * MH).transpose(1, 0, 2),
        "w_akv": np.concatenate([ak, av], 1).reshape(KT, P, CW).transpose(1, 0, 2),
        "sub1": x["sub_keys1_2"][0].T, "sub2": x["sub_keys2_2"][0].T,
        "g_final": np.broadcast_to(x["g_final_2"][None], (P, D)),
        "expert_down": x["expert_down_2"][0], "expert_up": x["expert_up_2"][0],
    }
    return {n: c(v) for n, v in out.items()}


def build(nc, a):
    ctx = ExitStack()

    def sb(name, shape, dt=F32):
        return ctx.enter_context(nc.sbuf_tensor(name, shape, dt))

    def sem(name):
        return ctx.enter_context(nc.semaphore(name))

    ring = sb("ring", [P, RING, KT, CW])
    feat = sb("feat", [P, 10, 8, T1])
    H, XN, SQ, UU, YS, QK, RR, ZG, ZS, EX = (feat[:, i] for i in range(10))
    FFH = feat[:, 3:7].rearrange("p s k t -> p (s k) t")
    VT = sb("VT", [P, 3, D])
    arena = sb("arena", [P, 16384])
    cols = sb("cols", [P, NCOLS])
    ident = sb("ident", [P, P])
    ones = sb("ones", [P, P])
    cmask = sb("cmask", [P, P])
    rmask = sb("rmask", [P, GH * T1])
    epsc = sb("epsc", [P, 1])
    RT = sb("RT", [P, 2, T1])
    walow = sb("walow", [P, KT, 16])
    wgu = sb("wgu", [16, GH * GDK])
    wif = sb("wif", [P, KT, 2 * MH])
    alow = sb("alow", [16, T1])

    at = [0]

    def carve(shape):
        n = int(np.prod(shape))
        v = arena[:, at[0]:at[0] + n]
        at[0] += n
        assert at[0] <= 16384, at[0]
        if len(shape) == 2:
            v = v.rearrange("p (a b) -> p a b", a=shape[0])
        if len(shape) == 3:
            v = v.rearrange("p (a b c) -> p a b c", a=shape[0], b=shape[1])
        return v

    COS = carve([SHALF, T1])
    SIN = carve([SHALF, T1])
    BD = [carve([8, P]) for _ in range(2)]
    CM = [carve([ST, 2 * SHG]) for _ in range(3)]
    P1, P2, WW, ZZ, R1, R2 = ([carve([2, T1]) for _ in range(2)] for _ in range(6))
    s5_end = at[0]
    SEL = VT[:, 0].rearrange("p (q c) -> p q c", q=8)
    LT = carve([3, ST])
    at[0] = 0
    GA, GB, GC, GE, GF, GI, GK = (carve([GH, T1]) for _ in range(7))
    GS = carve([4, GH, GDV])
    KST = carve([3, GH, GDK])
    SCT = carve([3, GH, P])
    prm = RR[0:ST].rearrange("p k t -> p (k t)")

    psD = ctx.enter_context(nc.psum_tensor("psD", [P, 4, 512], F32))
    psB = ctx.enter_context(nc.psum_tensor("psB", [P, 2, 512], F32))
    psY = ctx.enter_context(nc.psum_tensor("psY", [P, 512], F32))
    psN = ctx.enter_context(nc.psum_tensor("psN", [P, 512], F32))

    s_w = [sem(f"s_w{j}") for j in range(RING)]
    s_chunk = sem("s_chunk")
    s_dev = sem("s_dev")
    s_x = sem("s_x")
    s_cols = sem("s_cols")
    s_small = sem("s_small")
    s_s5 = sem("s_s5")
    s_s5b = sem("s_s5b")
    s_s5c = sem("s_s5c")
    s_zero = sem("s_zero")
    s_const = sem("s_const")
    s_vconst = sem("s_vconst")
    s_v = sem("s_v")
    s_p = sem("s_p")
    s_a = sem("s_a")
    s_sqa, s_sqv, s_ms, s_rt, s_xn = (sem(n) for n in ("s_sqa", "s_sqv", "s_ms", "s_rt", "s_xn"))
    s_h = sem("s_h")
    s_prm, s_exp, s_lt, s_ltc, s_bd = (sem(n) for n in ("s_prm", "s_exp", "s_lt", "s_ltc", "s_bd"))
    s_cn = sem("s_cn")
    s_bu, s_p12, s_rot, s_scan, s_r1, s_r2, s_y, s_ye, s_gs, s_tab = (
        sem(n) for n in ("s_bu", "s_p12", "s_rot", "s_scan", "s_r1", "s_r2", "s_y", "s_ye", "s_gs", "s_tab"))
    s_al, s_alc, s_gz, s_gzc, s_ls = (sem(n) for n in ("s_al", "s_alc", "s_gz", "s_gzc", "s_ls"))

    def counter(eng, s):
        n = [0]

        def link(ins):
            n[0] += 1
            ins.then_inc(s, 1)
            eng.wait_ge(s, n[0])
        return link

    def repeat(eng, n, body):
        if n == 1:
            body(0)
        else:
            with eng.Fori(0, n, 1) as it:
                body(it)

    def col(name, k, n=1):
        c = COLS[name][0] + k
        return cols[:, c:c + n]

    block = ctx.enter_context(nc.Block())

    def norm_act(i, x, ready, n, T, width=D):
        nc.scalar.wait_ge(ready, n)
        nc.scalar.activation(SQ[:, 4:8, 0:T], x[:, 4:8], ACT.Square).then_inc(s_sqa, 1)
        nc.scalar.wait_ge(s_ms, i + 1)
        nc.scalar.activation(RT[:, 0, 0:T], psN[:, 0:T], ACT.Sqrt, bias=epsc[:, 0:1],
                             scale=1.0 / width).then_inc(s_rt, 1)

    def norm_pe(i, T):
        nc.tensor.wait_ge(s_sqa, i + 1)
        nc.tensor.wait_ge(s_sqv, i + 1)
        for k in range(KT):
            mm = nc.tensor.matmul(psN[:, 0:T], ones[:, :], SQ[:, k, 0:T], start=(k == 0), stop=(k == KT - 1))
        mm.then_inc(s_ms, 1)

    def norm_dve(i, x, ready, n, T, gain, out, link):
        nc.vector.wait_ge(ready, n)
        nc.vector.tensor_tensor(SQ[:, 0:4, 0:T], x[:, 0:4], x[:, 0:4], ALU.mult).then_inc(s_sqv, 1)
        nc.vector.wait_ge(s_rt, i + 1)
        link(nc.vector.reciprocal(RT[:, 1, 0:T], RT[:, 0, 0:T]))
        for k in range(KT):
            ins = nc.vector.scalar_tensor_tensor(out=out[:, k, 0:T], in0=x[:, k], scalar=col(gain, k),
                                                 in1=RT[:, 1, 0:T], op0=ALU.mult, op1=ALU.mult)
        ins.then_inc(s_xn, 1)

    def dense_pe(first, n, x, T, hook=None):
        def body(it):
            for j in range(RING):
                c = first + RING * it + j
                nc.tensor.wait_ge(s_w[j], (first // RING + it + 1) * 16)
                if first + j >= 2:
                    nc.tensor.wait_ge(s_dev, first + j - 1 + RING * it)
                for m in range(2):
                    for k in range(KT):
                        mm = nc.tensor.matmul(psD[:, 2 * (j % 2) + m, 0:T], ring[:, j, k, m * P:(m + 1) * P],
                                              x[:, k], start=(k == 0), stop=(k == KT - 1))
                mm.then_inc(s_chunk, 1)
                if hook:
                    hook(j)
        repeat(nc.tensor, n, body)

    def dense_act(first, n, T, out):
        def body(it):
            for j in range(RING):
                nc.scalar.wait_ge(s_chunk, first + j + 1 + RING * it)
                out(it, j, psD[:, 2 * (j % 2):2 * (j % 2) + 2, 0:T]).then_inc(s_dev, 1)
        repeat(nc.scalar, n, body)


    def region(i, n=P):
        return prm[:, i * P:i * P + n]

    def poly(out, x, coef, link):
        link(nc.vector.tensor_scalar(out, x, float(coef[-1]), None, ALU.mult))
        for c in coef[-2::-1]:
            link(nc.vector.scalar_tensor_tensor(out=out, in0=out, scalar=float(c), in1=x, op0=ALU.add, op1=ALU.mult))

    def exp_exact(out, x, n, r, q, link):
        link(nc.vector.tensor_scalar(n, x, float(1 / np.log(2)), MAGIC, ALU.mult, ALU.add))
        link(nc.vector.tensor_scalar(n, n, MAGIC, -126.0, ALU.subtract, ALU.max))
        link(nc.vector.tensor_scalar(n, n, 127.0, None, ALU.min))
        link(nc.vector.scalar_tensor_tensor(out=r, in0=n, scalar=-0.693359375, in1=x, op0=ALU.mult, op1=ALU.add))
        link(nc.vector.scalar_tensor_tensor(out=r, in0=n, scalar=2.12194440e-4, in1=r, op0=ALU.mult, op1=ALU.add))
        poly(q, r, [1.0 / float(np.prod(np.arange(1, k + 1))) for k in range(1, 9)], link)
        link(nc.vector.tensor_scalar(n.bitcast(I32), n, 127.0, None, ALU.add))
        link(nc.vector.tensor_scalar(n.bitcast(I32), n.bitcast(I32), 23, None, ALU.logical_shift_left))
        link(nc.vector.scalar_tensor_tensor(out=out, in0=q, scalar=1.0, in1=n, op0=ALU.add, op1=ALU.mult))

    AR, AI, X, NN, RE, Q, TH, S2, C2, MAG, LRE, LIM, TT, DEN = (region(i) for i in range(14))
    FRI = prm[:, 14 * P:16 * P]
    FR, FI = FRI[:, 0:P], FRI[:, P:2 * P]
    LST, DT, D1, D2, D3 = (prm[:, 16 * P + 2 * i:16 * P + 2 * i + 2] for i in range(5))
    BR, BI = (s[:, 0:4].rearrange("p k t -> p (k t)")[:, 0:8 * P].rearrange("p (q n) -> p q n", q=8) for s in (ZG, ZS))

    def s5_param_dve(link):
        tt = nc.vector.tensor_tensor
        nc.vector.wait_ge(s_s5, 48)
        exp_exact(DT, LST, D1, D2, D3, link)
        dtb = DT.unsqueeze(2).to_broadcast([ST, 2, SN])
        three = lambda v: v.rearrange("p (g n) -> p g n", g=2)
        link(tt(three(X), three(AR), dtb, ALU.mult))
        link(tt(three(TH), three(AI), dtb, ALU.mult))
        exp_exact(MAG, X, NN, RE, Q, link)
        c1 = 6.28125
        c2 = float(np.float32(np.round((2 * np.pi - c1) * 2 ** 22) / 2 ** 22))
        c3 = float(2 * np.pi - c1 - c2)
        link(nc.vector.tensor_scalar(NN, TH, float(1 / (2 * np.pi)), MAGIC, ALU.mult, ALU.add))
        link(nc.vector.tensor_scalar(NN, NN, MAGIC, None, ALU.subtract))
        link(nc.vector.scalar_tensor_tensor(out=RE, in0=NN, scalar=-c1, in1=TH, op0=ALU.mult, op1=ALU.add))
        link(nc.vector.scalar_tensor_tensor(out=RE, in0=NN, scalar=-c2, in1=RE, op0=ALU.mult, op1=ALU.add))
        link(nc.vector.scalar_tensor_tensor(out=RE, in0=NN, scalar=-c3, in1=RE, op0=ALU.mult, op1=ALU.add))
        link(nc.vector.tensor_scalar(RE, RE, 0.5, None, ALU.mult))
        link(tt(X, RE, RE, ALU.mult))
        fact = lambda k: float(np.prod(np.arange(1.0, k + 1)))
        poly(Q, X, [(-1) ** k / fact(2 * k + 1) for k in range(1, 8)], link)
        link(nc.vector.scalar_tensor_tensor(out=S2, in0=Q, scalar=1.0, in1=RE, op0=ALU.add, op1=ALU.mult))
        poly(Q, X, [(-1) ** k / fact(2 * k) for k in range(1, 8)], link)
        link(nc.vector.scalar_tensor_tensor(out=C2, in0=Q, scalar=1.0, in1=S2, op0=ALU.add, op1=ALU.mult))
        link(nc.vector.tensor_scalar(C2, C2, 2.0, None, ALU.mult))
        link(tt(S2, S2, S2, ALU.mult))
        link(nc.vector.tensor_scalar(S2, S2, -2.0, 1.0, ALU.mult, ALU.add))
        link(tt(LRE, MAG, S2, ALU.mult))
        link(tt(LIM, MAG, C2, ALU.mult))
        link(nc.vector.tensor_scalar(LRE, LRE, -1.0, None, ALU.add))
        link(tt(DEN, AR, AR, ALU.mult))
        link(tt(TT, AI, AI, ALU.mult))
        link(tt(DEN, DEN, TT, ALU.add))
        link(nc.vector.reciprocal(DEN, DEN))
        link(tt(FR, LRE, AR, ALU.mult))
        link(tt(TT, LIM, AI, ALU.mult))
        link(tt(FR, FR, TT, ALU.add))
        link(tt(FI, LIM, AR, ALU.mult))
        link(tt(TT, LRE, AI, ALU.mult))
        link(tt(FI, FI, TT, ALU.subtract))
        link(tt(FR, FR, DEN, ALU.mult))
        tt(FI, FI, DEN, ALU.mult).then_inc(s_prm, 1)
        nc.vector.wait_ge(s_lt, 1)
        nc.vector.tensor_copy(LT[:, :, :].rearrange("p a j -> p (a j)"), psN[:, 0:3 * ST]).then_inc(s_ltc, 1)
        nc.vector.wait_ge(s_s5b, 32)
        for half in range(2):
            nc.vector.wait_ge(s_exp, half + 1)
            f = psB[:, :, :].rearrange("p b (q c n) -> p (b q) c n", q=2, c=2)
            qs = slice(4 * half, 4 * half + 4)
            fr, fi = f[:, :, 0], f[:, :, 1]
            ta, tb = (WW[i][:, :, :].rearrange("p a t -> p (a t)")[:, 0:4 * P].rearrange("p (q n) -> p q n", q=4)
                      for i in range(2))
            for dst, (x1, x2), op in ((BD[0], (BR, BI), ALU.subtract), (BD[1], (BI, BR), ALU.add)):
                link(tt(ta, fr, x1[:, qs], ALU.mult))
                link(tt(tb, fi, x2[:, qs], ALU.mult))
                ins = tt(dst[:, qs], ta, tb, op)
                if dst is BD[0]:
                    link(ins)
            ins.then_inc(s_bd, 1)
            nc.vector.wait_ge(s_bd, half + 1)

    def s5_param_pe():
        nc.tensor.wait_ge(s_prm, 1)
        nc.tensor.wait_ge(s_const, 1)
        for i, v in enumerate((MAG, S2, C2)):
            mm = nc.tensor.transpose(psN[:, i * ST:(i + 1) * ST], v, ident[0:ST, 0:ST])
        mm.then_inc(s_lt, 1)
        for half in range(2):
            if half:
                nc.tensor.wait_ge(s_bd, half)
            for i in range(4):
                mm = nc.tensor.matmul(psB[:, i // 2, (i % 2) * 256:(i % 2) * 256 + 256],
                                      SEL[0:ST, 4 * half + i, :], FRI, start=True, stop=True)
            mm.then_inc(s_exp, 1)

    def s5_tables(g, link):
        tt = nc.vector.tensor_tensor
        js = slice(g * SHALF, (g + 1) * SHALF)
        ta, tb = (SQ[:, 4 * i:4 * i + 4].rearrange("p k t -> p (k t)")[:, 0:SHALF * P]
                  .rearrange("p (j t) -> p j t", j=SHALF) for i in range(2))
        if g:
            nc.vector.wait_ge(s_r2, g * SHALF)
            nc.vector.wait_ge(s_r1, g * SHALF)
        nc.vector.memset(COS[:, :, 0:1], 1.0)
        nc.vector.memset(SIN[:, :, 0:1], 0.0)
        nc.vector.tensor_copy(COS[:, :, 1:2], LT[:, 1, js].unsqueeze(2))
        link(nc.vector.tensor_copy(SIN[:, :, 1:2], LT[:, 2, js].unsqueeze(2)))
        known = 1
        while known < T1 - 1:
            n = min(known, T1 - 1 - known)
            c, s = COS[:, :, 1:1 + n], SIN[:, :, 1:1 + n]
            ck = COS[:, :, known:known + 1].to_broadcast([P, SHALF, n])
            sk = SIN[:, :, known:known + 1].to_broadcast([P, SHALF, n])
            new = slice(known + 1, known + 1 + n)
            tt(ta[:, :, 0:n], c, ck, ALU.mult)
            link(tt(tb[:, :, 0:n], s, sk, ALU.mult))
            link(tt(COS[:, :, new], ta[:, :, 0:n], tb[:, :, 0:n], ALU.subtract))
            tt(ta[:, :, 0:n], c, sk, ALU.mult)
            link(tt(tb[:, :, 0:n], s, ck, ALU.mult))
            link(tt(SIN[:, :, new], ta[:, :, 0:n], tb[:, :, 0:n], ALU.add))
            known += n

    def s5_bu(j):
        q, r = j // 4, j % 4
        if j == 0:
            nc.tensor.wait_ge(s_bd, 2)
            nc.tensor.wait_ge(s_dev, FIRST["u"] + 4)
        if j >= 1:
            nc.tensor.wait_ge(s_p12, j)
        for c in range(2):
            mm = nc.tensor.matmul(psB[:, c, 0:T1], BD[c][32 * r:32 * r + 32, q, :], UU[32 * r:32 * r + 32, q],
                                  start=True, stop=True, tile_position=(32 * r, 0))
        mm.then_inc(s_bu, 1)

    def s5_y(j):
        q, r = j // 4, j % 4
        if j == 0:
            nc.tensor.wait_ge(s_cn, 1)
        if r == 0 and q:
            nc.tensor.wait_ge(s_ye, q)
        nc.tensor.wait_ge(s_r1, j + 1)
        nc.tensor.wait_ge(s_r2, j + 1)
        b = j % 2
        terms = [(CM[0], R1[b][:, 0]), (CM[1], R2[b][:, 1]), (CM[2], R2[b][:, 0]), (CM[2], R1[b][:, 1])]
        for i, (c, x) in enumerate(terms):
            mm = nc.tensor.matmul(psY[32 * r:32 * r + 32, 0:T1], c[:, j, :], x, start=(i == 0), stop=(i == 3),
                                  tile_position=(0, 32 * r))
        mm.then_inc(s_y, 1)

    def bc(tab, j):
        return tab[:, j % SHALF].unsqueeze(1).to_broadcast([P, 2, T1])

    def s5_dve(link):
        def rotate_in(j):
            if j % SHALF == 0:
                s5_tables(j // SHALF, link)
            nc.vector.wait_ge(s_bu, j + 1)
            if j >= 2:
                nc.vector.wait_ge(s_rot, j - 1)
            nc.vector.tensor_tensor(P1[j % 2], psB[:, :, 0:T1], bc(COS, j), ALU.mult)
            nc.vector.tensor_tensor(P2[j % 2], psB[:, :, 0:T1], bc(SIN, j), ALU.mult).then_inc(s_p12, 1)

        def scan(j):
            b = j % 2
            nc.vector.wait_ge(s_rot, j + 1)
            if j >= 2:
                nc.vector.wait_ge(s_r2, j - 1)
            for c in range(2):
                m = LT[:, 0, j:j + 1].to_broadcast([P, T1])
                ins = nc.vector.tensor_tensor_scan(ZZ[b][:, c], m, WW[b][:, c], 0.0, ALU.mult, ALU.add)
            ins.then_inc(s_scan, 1)
            nc.vector.wait_ge(s_scan, j + 1)
            if j >= 2:
                nc.vector.wait_ge(s_y, j - 1)
            nc.vector.tensor_tensor(R1[b], ZZ[b], bc(COS, j), ALU.mult).then_inc(s_r1, 1)

        def skip(q):
            nc.vector.wait_ge(s_y, 4 * q + 4)
            nc.vector.scalar_tensor_tensor(out=YS[:, q], in0=UU[:, q], scalar=col("d_skip", q), in1=psY[:, 0:T1],
                                           op0=ALU.mult, op1=ALU.add).then_inc(s_ye, 1)

        for j in range(ST + 1):
            if j < ST:
                if j % SHALF == 0 and j:
                    scan(j - 1)
                    rotate_in(j)
                else:
                    rotate_in(j)
                    if j:
                        scan(j - 1)
            else:
                scan(j - 1)
            if j >= 6 and (j - 6) % 4 == 0:
                skip((j - 6) // 4)
        skip(ST // 4 - 1)

    def s5_pool():
        def back(j):
            b = j % 2
            nc.gpsimd.wait_ge(s_scan, j + 1)
            if j >= 2:
                nc.gpsimd.wait_ge(s_y, j - 1)
            nc.gpsimd.tensor_tensor(R2[b], ZZ[b], bc(SIN, j), ALU.mult).then_inc(s_r2, 1)

        for j in range(ST):
            b = j % 2
            if j % SHALF == 0 and j:
                back(j - 1)
            nc.gpsimd.wait_ge(s_p12, j + 1)
            if j >= 2:
                nc.gpsimd.wait_ge(s_scan, j - 1)
            nc.gpsimd.tensor_tensor(WW[b][:, 0], P1[b][:, 0], P2[b][:, 1], ALU.add)
            nc.gpsimd.tensor_tensor(WW[b][:, 1], P1[b][:, 1], P2[b][:, 0], ALU.subtract).then_inc(s_rot, 1)
            if j % SHALF:
                back(j - 1)
        back(ST - 1)

    LZ, LB = EX[:, 0:4], EX[:, 4:8]
    flat = lambda v: v.rearrange("p h t -> p (h t)")

    def gate_pe():
        nc.tensor.wait_ge(s_small, 48)
        for k in range(KT):
            mm = nc.tensor.matmul(psY[0:16, 0:T1], walow[:, k, :], XN[:, k], start=(k == 0), stop=(k == KT - 1))
        mm.then_inc(s_al, 1)
        nc.tensor.wait_ge(s_alc, 1)
        for h in range(GH):
            if h >= 2:
                nc.tensor.wait_ge(s_gzc, h - 1)
            (nc.tensor.matmul((psY, psN)[h % 2][:, 0:T1], wgu[:, h * P:(h + 1) * P], alow[:, :], start=True, stop=True)
             .then_inc(s_gz, 1))

    def gate_act(link):
        nc.scalar.wait_ge(s_al, 1)
        nc.scalar.activation(alow[:, :], psY[0:16, 0:T1], ACT.Identity).then_inc(s_alc, 1)
        for h in range(GH):
            nc.scalar.wait_ge(s_gz, h + 1)
            (nc.scalar.activation(LZ[:, h], (psY, psN)[h % 2][:, 0:T1], ACT.Identity, bias=col("b_gate", h))
             .then_inc(s_gzc, 1))
        nc.scalar.wait_ge(s_gzc, GH)
        link(nc.scalar.activation(LB, LZ, ACT.Abs))
        link(nc.scalar.activation(LB, LB, ACT.Exp, scale=-1.0))
        nc.scalar.activation(LB, LB, ACT.Ln, bias=1.0).then_inc(s_ls, 1)

    def gate_dve(link):
        nc.vector.wait_ge(s_ls, 1)
        link(nc.vector.scalar_tensor_tensor(out=LZ, in0=LZ, scalar=0.0, in1=LB, op0=ALU.min, op1=ALU.subtract))
        link(nc.vector.tensor_tensor_scan(flat(LB), rmask[:, :], flat(LZ), 0.0, ALU.mult, ALU.add))

    s_gd, s_ge, s_gq, s_kt, s_ktc, s_sc, s_scc, s_u, s_st, s_o, s_oc, s_hms, s_hrt, s_og = (sem(n) for n in (
        "s_gd", "s_ge", "s_gq", "s_kt", "s_ktc", "s_sc", "s_scc", "s_u", "s_st", "s_o", "s_oc", "s_hms", "s_hrt",
        "s_og"))
    inv = 1.0 / 16.0

    def gla_prep_dve(link):
        tt = nc.vector.tensor_tensor
        nc.vector.wait_ge(s_y, ST)
        nc.vector.wait_ge(s_r2, ST)
        body = lambda v: v[:, :, META:T1].rearrange("p h (c t) -> p h c t", t=GCH)
        wide = [P, GH, 4, GCH]
        nc.vector.memset(SCT[:, :, :, :], 0.0)
        for h in range(GH):
            tt(body(GA)[:, h], body(LB)[:, h], body(LB)[:, h, :, 32:33].to_broadcast([P, 4, GCH]), ALU.subtract)
            tt(body(GB)[:, h], body(LB)[:, h, :, 63:64].to_broadcast([P, 4, GCH]), body(LB)[:, h], ALU.subtract)
        nc.vector.tensor_copy(GA[:, :, 0:META], LB[:, :, 0:META])
        tt(GB[:, :, 0:META], LB[:, :, META - 1:META].to_broadcast([P, GH, META]), LB[:, :, 0:META],
           ALU.subtract).then_inc(s_gd, 1)
        nc.vector.wait_ge(s_ge, 1)
        nc.vector.wait_ge(s_dev, FIRST["qk"] + 4)
        sc = float(GDK) ** -0.5
        stt = nc.vector.scalar_tensor_tensor
        tt(GK, QK[:, 4:8], GB, ALU.mult).then_inc(s_gq, 1)
        tt(GI, QK[:, 4:8], GA, ALU.mult)
        link(stt(out=GF, in0=QK[:, 0:4], scalar=sc, in1=GC, op0=ALU.mult, op1=ALU.mult))
        stt(out=GC, in0=QK[:, 0:4], scalar=sc, in1=GE, op0=ALU.mult, op1=ALU.mult).then_inc(s_gq, 1)

    def gla_exp_act():
        nc.scalar.wait_ge(s_gd, 1)
        nc.scalar.activation(GC, GA, ACT.Exp, scale=inv)
        nc.scalar.activation(GE, LB, ACT.Exp, scale=inv)
        nc.scalar.activation(GB, GB, ACT.Exp, scale=inv)
        nc.scalar.activation(GA, GA, ACT.Exp, scale=-inv).then_inc(s_ge, 1)

    KTB = [psB[:, 0], psB[:, 1], psY]
    SCB = [psN, psB[:, 0], psB[:, 1]]

    def gla_pe_a():
        nc.tensor.wait_ge(s_gq, 1)
        nc.tensor.wait_ge(s_ye, 8)
        for g, (t0, n) in enumerate(TOK1):
            for h in range(GH):
                mm = nc.tensor.transpose(KTB[g][0:n, h * P:(h + 1) * P], GK[:, h, t0:t0 + n], ident[:, :])
            mm.then_inc(s_kt, 1)
        nc.tensor.wait_ge(s_gq, 2)
        for g, (t0, n) in enumerate(TOK1):
            if g:
                nc.tensor.wait_ge(s_ktc, g)
            for h in range(GH):
                mm = nc.tensor.matmul(SCB[g][0:n, h * P:h * P + n], GI[:, h, t0:t0 + n], GF[:, h, t0:t0 + n],
                                      start=True, stop=True)
            mm.then_inc(s_sc, 1)
        nc.tensor.wait_ge(s_dev, FIRST["v"] + 4)
        nc.tensor.wait_ge(s_ktc, 3)
        nc.tensor.wait_ge(s_scc, 3)
        rows = [(0, 0, META), (1, 0, 64), (1, 64, 64), (2, 0, 64)]
        for c, (g, r, n) in enumerate(rows):
            if c:
                nc.tensor.wait_ge(s_st, c)
            for h in range(GH):
                mm = nc.tensor.matmul(psB[:, h // 2, (h % 2) * GDV:(h % 2) * GDV + GDV],
                                      KST[r:r + n, g, h, :], VT[r:r + n, g, h * GDV:(h + 1) * GDV],
                                      start=True, stop=True, tile_position=(r, 0))
            mm.then_inc(s_u, 1)

    def gla_dve_a(link):
        for g, (t0, n) in enumerate(TOK1):
            nc.vector.wait_ge(s_kt, g + 1)
            (nc.vector.tensor_copy(KST[0:n, g].rearrange("p h d -> p (h d)"), KTB[g][0:n, :])
             .then_inc(s_ktc, 1))
        for g, (t0, n) in enumerate(TOK1):
            nc.vector.wait_ge(s_sc, g + 1)
            src = SCB[g][0:n, :].rearrange("p (h i) -> p h i", h=GH)[:, :, 0:n]
            mask = cmask[0:n, 0:n].bitcast(U32).unsqueeze(1).to_broadcast([n, GH, n])
            nc.vector.copy_predicated(SCT[0:n, g, :, 0:n], mask, src).then_inc(s_scc, 1)
        ends = [META - 1 + GCH * c for c in range(4)]
        for c in range(4):
            nc.vector.wait_ge(s_u, c + 1)
            if c == 0:
                ins = nc.vector.tensor_copy(GS[:, 0].rearrange("p (b h) v -> p b (h v)", b=2), psB[:, :, :])
            else:
                nc.vector.wait_ge(s_st, c)
                for h in range(GH):
                    ins = nc.vector.scalar_tensor_tensor(
                        out=GS[:, c, h], in0=GS[:, c - 1, h], scalar=GE[:, h, ends[c]:ends[c] + 1],
                        in1=psB[:, h // 2, (h % 2) * GDV:(h % 2) * GDV + GDV], op0=ALU.mult, op1=ALU.add)
            ins.then_inc(s_st, 1)

    def gla_pe_b():
        for g, (t0, n) in enumerate(TOK1):
            nc.tensor.wait_ge(s_st, 4)
            if g:
                nc.tensor.wait_ge(s_oc, g)
            for h in range(GH):
                for m in range(2):
                    i = 2 * h + m
                    o = psB[:, i // 4, (i % 4) * P:(i % 4) * P + n]
                    vcol = h * GDV + m * P
                    mm = nc.tensor.matmul(o, VT[0:n, g, vcol:vcol + P], SCT[0:n, g, h, 0:n], start=True,
                                          stop=(g == 0), skip_group_check=True)
                    for half in range(2 if g else 0):
                        c = 2 * g - 1 + half
                        q = GC[:, h, GSTART[c]:GSTART[c] + GCH]
                        mm = nc.tensor.matmul(o[:, half * GCH:half * GCH + GCH], GS[:, c - 1, h, m * P:(m + 1) * P], q,
                                              start=False, stop=True, skip_group_check=True)
            mm.then_inc(s_o, 1)

    def gla_act_b():
        for g, (t0, n) in enumerate(TOK1):
            nc.scalar.wait_ge(s_o, g + 1)
            src = psB[:, :, :].rearrange("p b (i t) -> p (b i) t", t=P)[:, :, 0:n]
            nc.scalar.activation(QK[:, :, t0:t0 + n], src, ACT.Identity).then_inc(s_oc, 1)
        nc.scalar.wait_ge(s_oc, 3)
        nc.scalar.activation(SQ[:, :, :], QK[:, :, :], ACT.Square).then_inc(s_oc, 1)
        for h in range(GH):
            nc.scalar.wait_ge(s_hms, h + 1)
            (nc.scalar.activation(GA[:, h], (psB[:, 0], psB[:, 1], psY, psN)[h][:, 0:T1], ACT.Sqrt,
                                  bias=epsc[:, 0:1], scale=1.0 / GDV).then_inc(s_hrt, 1))

    def gla_pe_norm():
        nc.tensor.wait_ge(s_oc, 4)
        for h in range(GH):
            for m in range(2):
                mm = nc.tensor.matmul((psB[:, 0], psB[:, 1], psY, psN)[h][:, 0:T1], ones[:, :], SQ[:, 2 * h + m],
                                      start=(m == 0), stop=(m == 1))
            mm.then_inc(s_hms, 1)

    def gla_dve_norm(link):
        nc.vector.wait_ge(s_hrt, 4)
        link(nc.vector.reciprocal(GB, GA))
        for k in range(8):
            ins = nc.vector.scalar_tensor_tensor(out=QK[:, k], in0=QK[:, k], scalar=col("gla_norm_g", k),
                                                 in1=GB[:, k // 2], op0=ALU.mult, op1=ALU.mult)
        link(ins)
        nc.vector.tensor_tensor(QK, QK, RR, ALU.mult).then_inc(s_og, 1)

    def v1_pe(j):
        c = FIRST["v"] + j
        nc.tensor.wait_ge(s_w[j], (c // RING + 1) * 16)
        nc.tensor.wait_ge(s_dev, c - 1)
        for g, (t0, n) in ((1, TOK1[1]), (2, TOK1[2]), (0, TOK1[0])):
            o = psD[0:n, 2 * (j % 2) + (g == 0), (g == 2) * CW:(g == 2) * CW + CW]
            for k in range(KT):
                mm = nc.tensor.matmul(o, XN[:, k, t0:t0 + n], ring[:, j, k, :], start=(k == 0), stop=(k == KT - 1))
        mm.then_inc(s_chunk, 1)

    def v1_act(j):
        nc.scalar.wait_ge(s_chunk, FIRST["v"] + j + 1)
        b = 2 * (j % 2)
        nc.scalar.activation(VT[:, 1:3, j * CW:(j + 1) * CW],
                             psD[:, b, :].rearrange("p (g n) -> p g n", g=2), ACT.Identity)
        nc.scalar.activation(VT[0:META, 0, j * CW:(j + 1) * CW], psD[0:META, b + 1, 0:CW],
                             ACT.Identity).then_inc(s_dev, 1)

    def chunk_pe(first, j, x, T):
        c = first + j
        nc.tensor.wait_ge(s_w[j % RING], (c // RING + 1) * 16)
        if c >= 2:
            nc.tensor.wait_ge(s_dev, c - 1)
        for m in range(2):
            for k in range(KT):
                mm = nc.tensor.matmul(psD[:, 2 * (c % 2) + m, 0:T], ring[:, j % RING, k, m * P:(m + 1) * P],
                                      x[:, k], start=(k == 0), stop=(k == KT - 1))
        mm.then_inc(s_chunk, 1)

    def evac(dst, func, base=0, T=T1):
        return lambda it, j, ps: nc.scalar.activation(dst[:, bass.ds(2 * j + 8 * it, 2), 0:T] if not isinstance(it, int)
                                                      else dst[:, 2 * j + 8 * it:2 * j + 8 * it + 2, 0:T], ps, func)

    s_mix, s_ffh, s_t, s_glu = sem("s_mix"), sem("s_ffh"), sem("s_t"), sem("s_glu")

    def glu_act(part):
        for j in range(RING):
            c = FIRST["w_glu"] + 4 * part + j
            nc.scalar.wait_ge(s_chunk, c + 1)
            for m in range(2):
                i = 2 * j + m
                dst = (UU, EX)[part][:, i]
                ins = nc.scalar.activation(dst, psD[:, 2 * (j % 2) + m, 0:T1], (ACT.Identity, ACT.Sigmoid)[part],
                                           bias=col("b_glu", 8 * part + i))
            ins.then_inc(s_dev, 1)

    def ff2_pe(x, T):
        first = FIRST["w_ff2"]

        def body(it):
            for half in range(2):
                for kg in range(RING):
                    nc.tensor.wait_ge(s_w[kg], (first // RING + 1 + half + 2 * it) * 16)
                    if kg == 0:
                        nc.tensor.wait_ge(s_dev, first + (4 * (2 * it + half) - 4) if not isinstance(it, int)
                                          else first + max(4 * (2 * it + half) - 4, half - 1))
                    for m in range(2):
                        for k in range(KT):
                            mm = nc.tensor.matmul(psD[:, 2 * half + m, 0:T], ring[:, kg, k, m * P:(m + 1) * P],
                                                  x[:, KT * kg + k], start=(kg == 0 and k == 0),
                                                  stop=(kg == RING - 1 and k == KT - 1))
                    mm.then_inc(s_chunk, 1)
        body(0)
        body(1)

    def ff2_act(dst, T):
        for mg in range(4):
            nc.scalar.wait_ge(s_chunk, FIRST["w_ff2"] + 4 * mg + 4)
            (nc.scalar.activation(dst[:, 2 * mg:2 * mg + 2, 0:T], psD[:, 2 * (mg % 2):2 * (mg % 2) + 2, 0:T],
                                  ACT.Identity).then_inc(s_dev, 4))

    H2 = H[:, :, META:T1]
    XN2 = XN[:, :, 0:T2]
    MEM = EX[:, :, 0:T2]
    KX = UU[:, :, 0:T2]
    XV = YS.rearrange("p k t -> p (k t)")[:, 0:2 * D].rearrange("p (s n) -> p s n", s=2)
    MQKP = QK[:, 0:4, :]
    MO = QK[:, 4:8, 0:T2]
    AQ = RR[:, 0:4, 0:T2]
    MVT = RR[:, 4:8].rearrange("p k t -> p (k t)")[:, 0:2 * 512].rearrange("p (s n) -> p s n", s=2)
    CAT = ZS[:, :, 0:T2]
    QX = EX[:, :, 0:T2]
    OX = QK[:, :, 0:T2]
    DEL = ZG[:, :, 0:T2]
    at[0] = 0
    WKV = carve([KT, CW])
    AK = carve([T2])
    AV = carve([2, P])
    MQK = carve([4, T2])
    NEGC = carve([P])
    MASK3 = carve([3, P])
    ROWS = carve([5, T2])
    SELH = carve([MH, P])
    ACOL = carve([2, MH])
    EXPM = carve([MH, T2])
    DTE = carve([MH, 3 * P])
    PTM = carve([MH, 3 * P])
    HM = carve([MH, T2])
    RH = carve([MH, T2])
    SB = carve([AH, 3 * P])
    at_swa = at[0]
    MX, NMX, SUM, ESK = (carve([2, AH]) for _ in range(4))
    at[0] = 0
    XP = carve([XH, 2, T2])
    XPT = carve([XH, 2, T2])
    XMX, XNM, XSM, XRC = (carve([XH, 2]) for _ in range(4))
    at[0] = 0
    QH = feat[:, 3:5].rearrange("p s k t -> p (s k) t")[:, :, 0:T2]
    SCO = feat[:, 5:7].rearrange("p s k t -> p (s k t)")[:, 0:4096].rearrange("p (t x n) -> p t x n", t=2, x=16)
    XTOK, ACC = (feat[:, i].rearrange("p k t -> p (k t)")[:, 0:2 * D].rearrange("p (t d) -> p t d", t=2)
                       for i in (7, 9))
    SKT = carve([2, PK])
    VAL = carve([2, PTOP])
    IDX = carve([2, PTOP]).bitcast(U32)
    IDF = carve([2, PTOP])
    CS = carve([PTOP, PTOP])
    OH = carve([2, PTOP, PTOP])
    TV = carve([2, PH, PTOP])
    POS = carve([1, PTOP]).bitcast(U32)
    PA = carve([2, PTOP]).bitcast(U32)
    PAF = carve([2, PTOP])
    SELK = carve([2, PTOP])
    EID = carve([2, PH * PTOP]).bitcast(U32)
    IOTA = carve([PTOP])
    IOI = carve([PTOP]).bitcast(I32)
    GT = carve([2, PH, PTOP])
    GM = carve([2 * PH])
    AD = carve([2, PH * PTOP])
    DIAG = carve([PTOP // 2, P])
    COEF = carve([2, PH * PTOP])
    ACB = carve([D])
    GFIN = carve([D])
    FS = carve([2, 4])
    GROW = [carve([D]) for _ in range(9)] + [VT[:, i] for i in range(3)]
    GROW += [feat[:, s].rearrange("p k t -> p (k t)")[:, i * D:(i + 1) * D] for s in (2, 8) for i in range(2)]
    NB = len(GROW)

    (s_mem, s_kv, s_c2, s_if, s_ifl, s_conv, s_silu, s_mrow, s_acol, s_acs, s_rb, s_em, s_dt, s_de, s_ms2, s_pt,
     s_num, s_hm, s_hsq, s_hs, s_hr, s_cat, s_akv, s_aks, s_ws, s_wsb, s_wmx, s_wex, s_wpn, s_wt, s_wtc, s_wo_,
     s_woc) = (sem(n) for n in (
         "s_mem", "s_kv", "s_c2", "s_if", "s_ifl", "s_conv", "s_silu", "s_mrow", "s_acol", "s_acs", "s_rb", "s_em",
         "s_dt", "s_de", "s_ms2", "s_pt", "s_num", "s_hm", "s_hsq", "s_hs", "s_hr", "s_cat", "s_akv", "s_aks",
         "s_ws", "s_wsb", "s_wmx", "s_wex", "s_wpn", "s_wt", "s_wtc", "s_wo_", "s_woc"))

    def tok_pe(first, j, x):
        c = first + j
        nc.tensor.wait_ge(s_w[c % RING], (c // RING + 1) * 16)
        nc.tensor.wait_ge(s_dev, c - 1)
        for g in range(2):
            for k in range(KT):
                mm = nc.tensor.matmul(psD[:, 2 * (c % 2) + g, 0:CW], x[:, k, g * P:(g + 1) * P], ring[:, c % RING, k, :],
                                      start=(k == 0), stop=(k == KT - 1))
        mm.then_inc(s_chunk, 1)

    def tok_act(first, j, dst):
        c = first + j
        nc.scalar.wait_ge(s_chunk, c + 1)
        (nc.scalar.activation(dst, psD[:, 2 * (c % 2):2 * (c % 2) + 2, 0:CW], ACT.Identity).then_inc(s_dev, 1))

    def pair_act(first, j, dst, func=ACT.Identity):
        c = first + j
        nc.scalar.wait_ge(s_chunk, c + 1)
        (nc.scalar.activation(dst, psD[:, 2 * (c % 2):2 * (c % 2) + 2, 0:T2], func).then_inc(s_dev, 1))

    def small2_pe():
        nc.tensor.wait_ge(s_kv, 16)
        for i in range(2):
            for k in range(KT):
                mm = nc.tensor.matmul(psY[0:MH, i * T2:(i + 1) * T2], wif[:, k, MH * i:MH * i + MH], XN2[:, k],
                                      start=(k == 0), stop=(k == KT - 1))
        mm.then_inc(s_if, 1)
        for k in range(KT):
            mm = nc.tensor.matmul(psB[:, 0, 0:T2], WKV[:, k, 0:P], XN2[:, k], start=(k == 0), stop=(k == KT - 1))
        for g in range(2):
            for k in range(KT):
                mm = nc.tensor.matmul(psB[:, 1, g * P:(g + 1) * P], XN2[:, k, g * P:(g + 1) * P], WKV[:, k, P:2 * P],
                                      start=(k == 0), stop=(k == KT - 1))
        mm.then_inc(s_akv, 1)

    def small2_act(link):
        nc.scalar.wait_ge(s_if, 1)
        r = ROWS[0:MH]
        nc.scalar.activation(r[:, 3], psY[0:MH, 0:T2], ACT.Identity, bias=col("b_igate_2", 0)[0:MH])
        link(nc.scalar.activation(r[:, 4], psY[0:MH, T2:2 * T2], ACT.Identity, bias=col("b_fgate_2", 0)[0:MH]))
        link(nc.scalar.activation(r[:, 0], r[:, 4], ACT.Abs))
        link(nc.scalar.activation(r[:, 0], r[:, 0], ACT.Exp, scale=-1.0))
        nc.scalar.activation(r[:, 0], r[:, 0], ACT.Ln, bias=1.0).then_inc(s_ifl, 1)
        nc.scalar.wait_ge(s_akv, 1)
        nc.scalar.activation(AK, psB[:, 0, 0:T2], ACT.Identity)
        nc.scalar.activation(AV[:, :, :], psB[:, 1, 0:2 * P].rearrange("p (g n) -> p g n", g=2),
                             ACT.Identity).then_inc(s_aks, 1)

    def conv_dve(link):
        for i in range(4):
            for k in range(4):
                x = MQKP[:, k, i:i + T2]
                if i == 0:
                    ins = nc.vector.tensor_scalar(MQK[:, k], x, col("conv_w_2", 4 * k), col("conv_b_2", k),
                                                  ALU.mult, ALU.add)
                else:
                    ins = nc.vector.scalar_tensor_tensor(out=MQK[:, k], in0=x, scalar=col("conv_w_2", 4 * k + i),
                                                         in1=MQK[:, k], op0=ALU.mult, op1=ALU.add)
            if i < 3:
                link(ins)
        ins.then_inc(s_conv, 1)

    def mrows_dve(link):
        r = ROWS[0:MH]
        nc.vector.wait_ge(s_ifl, 1)
        link(nc.vector.scalar_tensor_tensor(out=r[:, 4], in0=r[:, 4], scalar=0.0, in1=r[:, 0], op0=ALU.min,
                                            op1=ALU.subtract))
        nc.vector.tensor_tensor_scan(r[:, 2], r[:, 4], r[:, 3], 0.0, ALU.add, ALU.max)
        one = ones[0:MH, 0:1].to_broadcast([MH, T2])
        link(nc.vector.tensor_tensor_scan(r[:, 1], one, r[:, 4], 0.0, ALU.mult, ALU.add))
        link(nc.vector.tensor_tensor(r[:, 0], r[:, 3], r[:, 1], ALU.subtract))
        nc.vector.tensor_tensor(r[:, 1], r[:, 1], r[:, 2], ALU.subtract).then_inc(s_mrow, 1)
        nc.vector.wait_ge(s_acol, 1)
        (nc.vector.tensor_copy(ACOL.rearrange("p s h -> p (s h)"), psY[:, 0:2 * MH]).then_inc(s_acs, 1))

    RB = [psB[:, 0], psB[:, 1], psY[:, :], psN[:, :]]

    def mrows_pe():
        nc.tensor.wait_ge(s_mrow, 1)
        nc.tensor.wait_ge(s_ifl, 1)
        for s in range(2):
            mm = nc.tensor.transpose(psY[:, s * MH:(s + 1) * MH], ROWS[0:MH, 0, s * P:(s + 1) * P], ident[0:MH, 0:MH])
        mm.then_inc(s_acol, 1)
        nc.tensor.wait_ge(s_c2, 1)
        nc.tensor.wait_ge(s_aks, 1)
        nc.tensor.wait_ge(s_acs, 1)
        for h in range(MH):
            (nc.tensor.matmul(RB[h][:, :], SELH[0:MH, h, :], ROWS[0:MH, 1:3].rearrange("p a t -> p (a t)"),
                              start=True, stop=True).then_inc(s_rb, 1))

    def mdecay_act():
        for h in range(MH):
            nc.scalar.wait_ge(s_dt, h + 1)
            nc.scalar.activation(EXPM[:, h], RB[h][:, T2:2 * T2], ACT.Exp, scale=-1.0)
            nc.scalar.activation(DTE[:, h, P:2 * P], RB[h][:, P:2 * P], ACT.Exp, bias=ACOL[:, 0, h:h + 1])
            v = DTE[:, h].rearrange("p (a t) -> p a t", a=3)[:, 0:3:2]
            nc.scalar.activation(v, v, ACT.Exp).then_inc(s_de, 1)

    def mdecay_dve():
        nc.vector.wait_ge(s_c2, 1)
        for h in range(MH):
            nc.vector.wait_ge(s_rb, h + 1)
            for s in range(2):
                ins = nc.vector.scalar_tensor_tensor(out=DTE[:, h, 2 * s * P:2 * s * P + P], in0=RB[h][:, s * P:(s + 1) * P],
                                                     scalar=ACOL[:, s, h:h + 1], in1=NEGC, op0=ALU.add, op1=ALU.add)
            ins.then_inc(s_dt, 1)

    def mscore_pe():
        nc.tensor.wait_ge(s_silu, 1)
        nc.tensor.wait_ge(s_de, MH)
        for h in range(MH):
            r = 64 * (h % 2)
            q, k = MQK[r:r + 64, h // 2], MQK[r:r + 64, 2 + h // 2]
            nc.tensor.matmul(RB[h][:, 0:T2], k[:, 0:P], q, start=True, stop=True, tile_position=(r, 0))
            (nc.tensor.matmul(RB[h][:, T2:T2 + P], k[:, P:T2], q[:, P:T2], start=True, stop=True, tile_position=(r, 0))
             .then_inc(s_ms2, 1))

    def mprod_dve():
        for h in range(MH):
            nc.vector.wait_ge(s_ms2, h + 1)
            nc.vector.wait_ge(s_de, h + 1)
            (nc.vector.scalar_tensor_tensor(out=PTM[:, h], in0=RB[h][:, 0:3 * P], scalar=float(MQK_SCALE), in1=DTE[:, h],
                                            op0=ALU.mult, op1=ALU.mult).then_inc(s_pt, 1))

    def mnum_pe():
        nc.tensor.wait_ge(s_dev, FIRST["aq_mv"] + 4)
        for h in range(MH):
            nc.tensor.wait_ge(s_pt, h + 1)
            for i in range(2):
                w = [MVT[:, s, h * P:(h + 1) * P] if i == 0 else ones[:, :] for s in range(2)]
                o = i * T2
                nc.tensor.matmul(RB[h][:, o:o + T2], w[0], PTM[:, h, 0:T2], start=True, stop=False,
                                 skip_group_check=True)
                mm = nc.tensor.matmul(RB[h][:, o + P:o + T2], w[1], PTM[:, h, T2:T2 + P], start=False, stop=True,
                                      skip_group_check=True)
            mm.then_inc(s_num, 1)

    def mout_dve(link):
        for h in range(MH):
            nc.vector.wait_ge(s_num, h + 1)
            link(nc.vector.scalar_tensor_tensor(out=RH[:, h], in0=RB[h][:, T2:2 * T2], scalar=-1.0, in1=EXPM[:, h],
                                                op0=ALU.mult, op1=ALU.max))
            link(nc.vector.tensor_tensor(RH[:, h], RB[h][:, T2:2 * T2], RH[:, h], ALU.max))
            link(nc.vector.reciprocal(RH[:, h], RH[:, h]))
            nc.vector.tensor_tensor(HM[:, h], RB[h][:, 0:T2], RH[:, h], ALU.mult).then_inc(s_hm, 1)

    def mnorm_act():
        nc.scalar.wait_ge(s_hm, MH)
        nc.scalar.activation(SQ[:, 0:MH, 0:T2], HM[:, :, :], ACT.Square).then_inc(s_hsq, 1)
        nc.scalar.wait_ge(s_hs, 1)
        (nc.scalar.activation(RH[:, :, :], psB[:, :, :].rearrange("p b (h t) -> p (b h) t", h=2), ACT.Sqrt,
                              bias=epsc[:, 0:1], scale=1.0 / MV).then_inc(s_hr, 1))

    def mnorm_pe():
        nc.tensor.wait_ge(s_hsq, 1)
        for h in range(MH):
            mm = nc.tensor.matmul(psB[:, h // 2, (h % 2) * T2:(h % 2) * T2 + T2], ones[:, :], SQ[:, h, 0:T2],
                                  start=True, stop=True)
        mm.then_inc(s_hs, 1)

    def mnorm_dve(link):
        nc.vector.wait_ge(s_hr, 1)
        link(nc.vector.reciprocal(RH[:, :, :], RH[:, :, :]))
        for h in range(MH):
            ins = nc.vector.scalar_tensor_tensor(out=HM[:, h], in0=HM[:, h], scalar=col("g_mhead_2", h), in1=RH[:, h],
                                                 op0=ALU.mult, op1=ALU.mult)
        link(ins)
        nc.vector.tensor_tensor(CAT[:, 0:4], HM[:, :, :], MO, ALU.mult).then_inc(s_cat, 1)

    WB = [psD[:, i] for i in range(4)]

    def wscore_pe():
        nc.tensor.wait_ge(s_dev, FIRST["aq_mv"] + 4)
        nc.tensor.wait_ge(s_aks, 1)
        for i in range(AH):
            if i >= 4:
                nc.tensor.wait_ge(s_wsb, i - 3)
            r = 64 * (i % 2)
            q, k, o = AQ[r:r + 64, i // 2], AK[r:r + 64], WB[i % 4]
            nc.tensor.matmul(o[:, 0:P], q[:, 0:P], k[:, 0:P], start=True, stop=True, tile_position=(r, 0))
            (nc.tensor.matmul(o[:, P:3 * P], q[:, P:T2], k[:, 0:T2], start=True, stop=True, tile_position=(r, 0))
             .then_inc(s_ws, 1))

    def wsoft1_dve(link):
        nc.vector.wait_ge(s_c2, 1)
        for i in range(AH):
            nc.vector.wait_ge(s_ws, i + 1)
            (nc.vector.scalar_tensor_tensor(out=SB[:, i], in0=WB[i % 4][:, 0:3 * P], scalar=float(ADH) ** -0.5,
                                            in1=MASK3.rearrange("p a s -> p (a s)"), op0=ALU.mult, op1=ALU.add)
             .then_inc(s_wsb, 1))
        nc.vector.wait_ge(s_wsb, AH)
        nc.vector.tensor_reduce(MX[:, 0], SB[:, :, 0:P], AX.X, ALU.max)
        link(nc.vector.tensor_reduce(MX[:, 1], SB[:, :, P:3 * P], AX.X, ALU.max))
        sk = col("sinks_2", 0, AH).unsqueeze(1).to_broadcast([P, 2, AH])
        link(nc.vector.tensor_tensor(MX[:, :, :], MX[:, :, :], sk, ALU.max))
        nc.vector.tensor_scalar(NMX[:, :, :], MX[:, :, :], -1.0, None, ALU.mult).then_inc(s_wmx, 1)
        nc.vector.tensor_tensor(ESK[:, :, :], sk, MX[:, :, :], ALU.subtract).then_inc(s_wmx, 1)

    def wsoft2_dve(link):
        nc.vector.wait_ge(s_wex, 1)
        link(nc.vector.tensor_tensor(SUM[:, :, :], SUM[:, :, :], ESK[:, :, :], ALU.add))
        link(nc.vector.reciprocal(SUM[:, :, :], SUM[:, :, :]))
        nc.vector.tensor_tensor(SB[:, :, 0:P], SB[:, :, 0:P], SUM[:, 0].unsqueeze(2).to_broadcast([P, AH, P]), ALU.mult)
        (nc.vector.tensor_tensor(SB[:, :, P:3 * P], SB[:, :, P:3 * P], SUM[:, 1].unsqueeze(2).to_broadcast([P, AH, 2 * P]),
                                 ALU.mult).then_inc(s_wpn, 1))

    def wexp_act(link):
        nc.scalar.wait_ge(s_wmx, 1)
        for i in range(AH):
            nc.scalar.activation(SB[:, i, 0:P], SB[:, i, 0:P], ACT.Exp, bias=NMX[:, 0, i:i + 1],
                                 accum_out=SUM[:, 0, i:i + 1])
            nc.scalar.activation(SB[:, i, P:3 * P], SB[:, i, P:3 * P], ACT.Exp, bias=NMX[:, 1, i:i + 1],
                                 accum_out=SUM[:, 1, i:i + 1])
        nc.scalar.wait_ge(s_wmx, 2)
        nc.scalar.activation(ESK[:, :, :], ESK[:, :, :], ACT.Exp).then_inc(s_wex, 1)

    WPT = [DTE, PTM]

    def wout_pe():
        def turn(i):
            if i >= 4:
                nc.tensor.wait_ge(s_wtc, i - 3)
            for b, x in enumerate((0, 1, 2)):
                mm = nc.tensor.transpose(WB[i % 4][:, b * P:(b + 1) * P], SB[:, i, x * P:(x + 1) * P], ident[:, :])
            mm.then_inc(s_wt, 1)

        def product(i):
            r, p = 64 * (i % 2), WPT[i // 4][:, i % 4]
            o = RB[i // 2][r:r + 64]
            nc.tensor.wait_ge(s_wtc, i + 1)
            kv = slice(64 * (i % 2), 64 * (i % 2) + 64)
            nc.tensor.matmul(o[:, 0:T2], AV[:, 0, kv], p[:, 0:T2], start=True, stop=False, tile_position=(0, r),
                             skip_group_check=True)
            mm = nc.tensor.matmul(o[:, P:T2], AV[:, 1, kv], p[:, T2:3 * P], start=False, stop=True,
                                  tile_position=(0, r), skip_group_check=True)
            if i % 2:
                mm.then_inc(s_wo_, 1)
        nc.tensor.wait_ge(s_wpn, 1)
        nc.tensor.wait_ge(s_hr, 1)
        nc.tensor.wait_ge(s_hm, MH)
        for i in range(AH):
            turn(i)
            if i >= 2:
                product(i - 2)
        product(AH - 2)
        product(AH - 1)

    def wout_act():
        for i in range(AH):
            nc.scalar.wait_ge(s_wt, i + 1)
            nc.scalar.activation(WPT[i // 4][:, i % 4], WB[i % 4][:, 0:3 * P], ACT.Identity).then_inc(s_wtc, 1)
        for p in range(4):
            nc.scalar.wait_ge(s_wo_, p + 1)
            nc.scalar.activation(CAT[:, 4 + p], RB[p][:, 0:T2], ACT.Identity).then_inc(s_woc, 1)

    s_xs, s_xmx, s_xex, s_xpn, s_xt, s_xtc, s_xo, s_xoc = (sem(n) for n in (
        "s_xs", "s_xmx", "s_xex", "s_xpn", "s_xt", "s_xtc", "s_xo", "s_xoc"))

    def cross_pe():
        nc.tensor.wait_ge(s_dev, FIRST["xq"] + 4)
        for h in range(XH):
            for t in range(2):
                for m in range(2):
                    mm = nc.tensor.matmul(RB[h][:, t * T2:(t + 1) * T2], QX[:, 2 * h + m, t * P:(t + 1) * P],
                                          KX[:, 2 * h + m], start=(m == 0), stop=(m == 1))
            mm.then_inc(s_xs, 1)
        for h in range(XH):
            nc.tensor.wait_ge(s_xpn, h + 1)
            for t in range(2):
                for s in range(2):
                    mm = nc.tensor.transpose(WB[h][:, s * T2 + t * P:s * T2 + t * P + P],
                                             XP[:, h, t, s * P:(s + 1) * P], ident[:, :])
            mm.then_inc(s_xt, 1)
        for h in range(XH):
            nc.tensor.wait_ge(s_xtc, h + 1)
            for m in range(2):
                for s in range(2):
                    mm = nc.tensor.matmul(RB[h][:, m * T2:(m + 1) * T2], XV[:, s, h * XD + m * P:h * XD + (m + 1) * P],
                                          XPT[:, h, s], start=(s == 0), stop=(s == 1))
            mm.then_inc(s_xo, 1)

    def cross_dve(link):
        sc = float(XD) ** -0.5
        for h in range(XH):
            nc.vector.wait_ge(s_xs, h + 1)
            link(nc.vector.tensor_reduce(XMX[:, h], RB[h][:, :].rearrange("p (t s) -> p t s", t=2), AX.X, ALU.max))
            nc.vector.tensor_scalar(XNM[:, h], XMX[:, h], -sc, None, ALU.mult).then_inc(s_xmx, 1)
        for h in range(XH):
            nc.vector.wait_ge(s_xex, h + 1)
            link(nc.vector.reciprocal(XRC[:, h], XSM[:, h]))
            for t in range(2):
                ins = nc.vector.tensor_scalar(XP[:, h, t], XP[:, h, t], XRC[:, h, t:t + 1], None, ALU.mult)
            ins.then_inc(s_xpn, 1)
        for h in range(XH):
            nc.vector.wait_ge(s_xt, h + 1)
            nc.vector.tensor_copy(XPT[:, h].rearrange("p s t -> p (s t)"), WB[h]).then_inc(s_xtc, 1)

    def cross_act():
        sc = float(XD) ** -0.5
        for h in range(XH):
            nc.scalar.wait_ge(s_xmx, h + 1)
            for t in range(2):
                ins = nc.scalar.activation(XP[:, h, t], RB[h][:, t * T2:(t + 1) * T2], ACT.Exp, bias=XNM[:, h, t:t + 1],
                                           scale=sc, accum_out=XSM[:, h, t:t + 1])
            ins.then_inc(s_xex, 1)
        for h in range(XH):
            nc.scalar.wait_ge(s_xo, h + 1)
            (nc.scalar.activation(OX[:, 2 * h:2 * h + 2], RB[h][:, :].rearrange("p (m t) -> p m t", m=2), ACT.Identity)
             .then_inc(s_xoc, 1))

    (s_sk, s_ps, s_psc, s_tt, s_ttc, s_eid, s_gate, s_io, s_gel, s_coef, s_usev, s_uset, s_diag, s_fin, s_fsq, s_frt) = (
        sem(n) for n in (
            "s_sk", "s_ps", "s_psc", "s_tt", "s_ttc", "s_eid", "s_gate", "s_io", "s_gel", "s_coef", "s_usev",
            "s_uset", "s_diag", "s_fin", "s_fsq", "s_frt"))
    s_gb = [sem(f"s_gb{j}") for j in range(NB)]

    HALF = PTOP // 2
    PERV = PTOP + HALF
    ROWS_ = 2 * PTOP
    FILLS = ROWS_ // NB
    FREE = HALF

    def used(g, i):
        if i < PTOP:
            return s_usev, PERV * g + i + 1
        if i % 2 == 0:
            return s_usev, PERV * g + PTOP + (i - PTOP) // 2 + 1
        return s_uset, FREE + HALF * g + (i - PTOP) // 2 + 1

    def peer_pe():
        sums = ((psY, psN), (psB[:, 0], psB[:, 1]))

        def queries(h):
            chunk_pe(FIRST["pq"], h, XN2, T2)
            if h < 2:
                for half in range(2):
                    if h:
                        nc.tensor.wait_ge(s_ttc, half + 1)
                    for k in range(4):
                        mm = nc.tensor.transpose((psY, psN)[half][:, k * P:(k + 1) * P],
                                                 XN2[:, 4 * half + k, h * P:(h + 1) * P], ident[:, :])
                    mm.then_inc(s_tt, 1)
            if h >= 2:
                nc.tensor.wait_ge(s_psc, h - 1)
            nc.tensor.wait_ge(s_dev, FIRST["pq"] + h + 1)
            for t in range(2):
                for x in range(2):
                    mm = nc.tensor.matmul(psB[:, h % 2, (2 * t + x) * PK:(2 * t + x + 1) * PK],
                                          QH[:, 2 * h + x, t * P:(t + 1) * P], SKT[:, x], start=True, stop=True)
            mm.then_inc(s_ps, 1)

        def residual(t):
            for half in range(2):
                for k in range(4):
                    nc.tensor.matmul(sums[t][half][:, k * P:(k + 1) * P], H2[:, 4 * half + k, t * P:(t + 1) * P],
                                     ident[:, :], start=False, stop=True, skip_group_check=True)

        def weigh(t, g, first=False):
            for k in range(HALF):
                row = (PTOP + 2 * k + 1) % NB
                nc.tensor.wait_ge(s_gb[row], 16 * FILLS * g + 16 * ((PTOP + 2 * k + 1) // NB + 1))
                nc.tensor.wait_ge(s_diag, HALF * g + (k + 1))
                for half in range(2):
                    mm = nc.tensor.matmul(sums[t][half][:, 0:512], DIAG[:, k], GROW[row][:, 512 * half:512 * half + 512],
                                          start=(first and k == 0), stop=True, skip_group_check=True)
                mm.then_inc(s_uset, 1)
        nc.tensor.wait_ge(s_sk, 48)
        for h in range(6):
            queries(h)
            if h == 0:
                nc.tensor.sem_inc(s_uset, FREE)
        nc.tensor.wait_ge(s_ttc, 4)
        weigh(0, 0, first=True)
        residual(0)
        queries(6)
        queries(7)
        with nc.tensor.Fori(1, PH, 1) as g:
            weigh(0, g)
        nc.tensor.wait_ge(s_psc, PH)
        weigh(1, PH, first=True)
        residual(1)
        with nc.tensor.Fori(PH + 1, 2 * PH, 1) as g:
            weigh(1, g)

    def peer_act(link):
        for h in range(PH):
            pair_act(FIRST["pq"], h, QH[:, 2 * h:2 * h + 2])
            if h < 2:
                for half in range(2):
                    nc.scalar.wait_ge(s_tt, 2 * h + half + 1)
                    (nc.scalar.activation(XTOK[:, h, 512 * half:512 * half + 512], (psY, psN)[half][:, :], ACT.Identity)
                     .then_inc(s_ttc, 1))
            nc.scalar.wait_ge(s_ps, h + 1)
            (nc.scalar.activation(SCO[:, :, 2 * h:2 * h + 2], psB[:, h % 2].rearrange("p (t x n) -> p t x n", t=2, x=2),
                                  ACT.Identity).then_inc(s_psc, 1))
            if h == 5:
                coefficients(0)
        for g in range(1, 2 * PH):
            if g == PH:
                root(0)
            coefficients(g)
        root(1)

    def coefficients(g):
        t, h = g // PH, g % PH
        nc.scalar.wait_ge(s_eid, g + 1)
        nc.scalar.activation(GT[:, t, h], GT[:, t, h], ACT.Exp, accum_out=GM[:, g:g + 1])
        nc.scalar.wait_ge(s_usev, PERV * g + PTOP)
        v = AD[:, t, PTOP * h:PTOP * (h + 1)]
        nc.scalar.activation(v, v, ACT.Gelu).then_inc(s_gel, 1)
        nc.scalar.wait_ge(s_coef, g + 1)
        for k in range(HALF):
            c = PTOP * h + 2 * k + 1
            nc.scalar.wait_ge(s_uset, HALF * g + k + 1)
            nc.scalar.activation(DIAG[:, k], ident[:, :], ACT.Identity, scale=COEF[:, t, c:c + 1]).then_inc(s_diag, 1)

    def root(t):
        nc.scalar.wait_ge(s_fin, t + 1)
        nc.scalar.activation(XTOK[:, t], ACC[:, t], ACT.Square, accum_out=FS[:, t, 0:1]).then_inc(s_fsq, 1)
        nc.scalar.wait_ge(s_fsq, t + 1)
        (nc.scalar.activation(FS[:, t, 1:2], FS[:, t, 0:1], ACT.Sqrt, bias=epsc[:, 0:1], scale=1.0 / D)
         .then_inc(s_frt, 1))

    def top16(vals, idx, src, n, link):
        v = nc.vector
        for r in range(n):
            ins = v.max(vals[:, r, 0:8], src[:, r])
        link(ins)
        for r in range(n):
            v.max_index(idx[:, r, 0:8], vals[:, r, 0:8], src[:, r])
        for r in range(n):
            ins = v.match_replace(src[:, r], vals[:, r, 0:8], src[:, r], MAXNEG)
        link(ins)
        for r in range(n):
            ins = v.max(vals[:, r, 8:16], src[:, r])
        link(ins)
        for r in range(n):
            ins = v.max_index(idx[:, r, 8:16], vals[:, r, 8:16], src[:, r])
        link(ins)

    def route_dve(t, h, link):
        tt = nc.vector.tensor_tensor
        if t == 0:
            nc.vector.wait_ge(s_psc, h + 1)
        top16(VAL, IDX, SCO[:, t, 2 * h:2 * h + 2], 2, link)
        nc.vector.tensor_copy(IDF[:, :, :], IDX)
        link(tt(CS, VAL[:, 0].unsqueeze(2).to_broadcast([P, PTOP, PTOP]),
                VAL[:, 1].unsqueeze(1).to_broadcast([P, PTOP, PTOP]), ALU.add))
        tv = TV[:, t, h:h + 1]
        top16(tv, POS, CS.rearrange("p a b -> p (a b)").unsqueeze(1), 1, link)
        tt(GT[:, t, h], tv[:, 0], tv[:, 0, 0:1].to_broadcast([P, PTOP]), ALU.subtract)
        nc.vector.tensor_scalar(PA[:, 0], POS[:, 0], 4, None, ALU.logical_shift_right)
        link(nc.vector.tensor_scalar(PA[:, 1], POS[:, 0], 15, None, ALU.bitwise_and))
        link(nc.vector.tensor_copy(PAF[:, :, :], PA))
        oh = OH.rearrange("p c k j -> p (c k) j")
        wide = [P, 2 * PTOP, PTOP]
        if t == 0 and h == 0:
            nc.vector.wait_ge(s_io, 2)
        link(tt(oh, PAF.rearrange("p c k -> p (c k)").unsqueeze(2).to_broadcast(wide),
                IOTA.unsqueeze(1).to_broadcast(wide), ALU.is_equal))
        link(tt(OH, OH, IDF.unsqueeze(2).to_broadcast([P, 2, PTOP, PTOP]), ALU.mult))
        link(nc.vector.tensor_reduce(SELK.rearrange("p c k -> p (c k)"), oh, AX.X, ALU.add))
        (nc.vector.scalar_tensor_tensor(out=EID[:, t, h * PTOP:(h + 1) * PTOP], in0=SELK[:, 0], scalar=float(PK),
                                        in1=SELK[:, 1], op0=ALU.mult, op1=ALU.add).then_inc(s_eid, 1))

    def gathers_pool():
        for g in range(2 * PH):
            t, h = g // PH, g % PH
            nc.gpsimd.wait_ge(s_eid, g + 1)
            for i in range(ROWS_):
                table = a["expert_down"] if i < PTOP else a["expert_up"]
                if g or i >= NB:
                    nc.gpsimd.wait_ge(*(used(g, i - NB) if i >= NB else used(g - 1, i - NB + ROWS_)))
                c = h * PTOP + i % PTOP
                (nc.gpsimd.indirect_dma_start(GROW[i % NB], None, table,
                                              bass.IndirectOffsetOnAxis(ap=EID[:, t, c:c + 1], axis=0))
                 .then_inc(s_gb[i % NB], 16))

    def down_dve(g):
        t, h = g // PH, g % PH
        for i in range(PTOP):
            row = GROW[i % NB]
            c = PTOP * h + i
            nc.vector.wait_ge(s_gb[i % NB], 16 * (FILLS * g + i // NB + 1))
            (nc.vector.tensor_tensor_reduce(row, row, XTOK[:, t], 1.0, 0.0, ALU.mult, ALU.add, AD[:, t, c:c + 1])
             .then_inc(s_usev, 1))

    def coef_dve(g, link):
        t, h = g // PH, g % PH
        nc.vector.wait_ge(s_gel, g + 1)
        link(nc.vector.reciprocal(GM[:, g:g + 1], GM[:, g:g + 1]))
        c = slice(PTOP * h, PTOP * (h + 1))
        ins = nc.vector.scalar_tensor_tensor(out=COEF[:, t, c], in0=AD[:, t, c], scalar=GM[:, g:g + 1], in1=GT[:, t, h],
                                             op0=ALU.mult, op1=ALU.mult)
        ins.then_inc(s_coef, 1)
        nc.vector.wait_ge(s_coef, g + 1)

    def up_dve(g):
        t, h = g // PH, g % PH
        for k in range(HALF):
            i = PTOP + 2 * k
            acc = (ACC[:, t], ACB)[k % 2]
            c = PTOP * h + 2 * k
            nc.vector.wait_ge(s_gb[i % NB], 16 * (FILLS * g + i // NB + 1))
            if k >= 2:
                nc.vector.wait_ge(s_usev, PERV * g + PTOP + k - 1)
            (nc.vector.scalar_tensor_tensor(out=acc, in0=GROW[i % NB], scalar=COEF[:, t, c:c + 1], in1=acc,
                                            op0=ALU.mult, op1=ALU.add).then_inc(s_usev, 1))

    def peer_dve(link):
        dve = nc.vector

        def last(t):
            dve.wait_ge(s_usev, PERV * PH * (t + 1))
            link(dve.tensor_tensor(ACC[:, t], ACC[:, t], ACB, ALU.add))
            dve.wait_ge(s_uset, FREE + HALF * PH * (t + 1))
            for half, ps in enumerate((psY[:, :], psN[:, :]) if t == 0 else (psB[:, 0], psB[:, 1])):
                v = ACC[:, t, 512 * half:512 * half + 512]
                ins = dve.tensor_tensor(v, v, ps, ALU.add)
            ins.then_inc(s_fin, 1)
            dve.wait_ge(s_frt, t + 1)
            link(dve.reciprocal(FS[:, t, 2:3], FS[:, t, 1:2]))
            dve.wait_ge(s_sk, 48)
            dve.scalar_tensor_tensor(out=ACC[:, t], in0=ACC[:, t], scalar=FS[:, t, 2:3], in1=GFIN, op0=ALU.mult,
                                     op1=ALU.mult).then_inc(s_done, 1)
        for t in range(2):
            dve.memset(ACC[:, t], 0.0)
        route_dve(0, 0, link)
        for g in range(2 * PH):
            if g % PH == 0:
                link(dve.memset(ACB, 0.0))
                dve.wait_ge(s_ttc, 2 * (g // PH) + 2)
            down_dve(g)
            if g + 1 < 2 * PH:
                route_dve((g + 1) // PH, (g + 1) % PH, link)
            coef_dve(g, link)
            up_dve(g)
            if g % PH == PH - 1:
                last(g // PH)

    def residual_dve(y, gain, T, h, link, Z=ZG):
        for k in range(KT):
            ins = nc.vector.scalar_tensor_tensor(out=Z[:, k, 0:T], in0=y[:, k, 0:T], scalar=col(gain, k),
                                                 in1=RT[:, 1, 0:T], op0=ALU.mult, op1=ALU.mult)
        link(ins)
        nc.vector.tensor_tensor(h, h, Z[:, :, 0:T], ALU.add).then_inc(s_h, 1)

    def postnorm_dve(i, y, ready, n, T, gain, h, link):
        nc.vector.wait_ge(ready, n)
        nc.vector.tensor_tensor(SQ[:, 0:4, 0:T], y[:, 0:4], y[:, 0:4], ALU.mult).then_inc(s_sqv, 1)
        nc.vector.wait_ge(s_rt, i + 1)
        link(nc.vector.reciprocal(RT[:, 1, 0:T], RT[:, 0, 0:T]))
        residual_dve(y, gain, T, h, link)

    s_out = sem("s_out")

    def finish(sp):
        for t in range(2):
            sp.wait_ge(s_done, t + 1)
            sp.dma_start(a["out"][t * P:(t + 1) * P], ACC[:, t]).then_inc(s_out, 16)
        sp.wait_ge(s_out, 32)
    s_done = sem("s_done")

    @block.sync
    def _(sp):
        sp.dma_start(H, a["xT"]).then_inc(s_x, 16)
        sp.dma_start(cols[:, :], a["cols"]).then_inc(s_cols, 16)
        w = a["w"]

        def load(j, c):
            sp.dma_start(ring[:, j].rearrange("p k n -> p (k n)"),
                         w[bass.ds(c, 1)].rearrange("a p n -> p (a n)") if not isinstance(c, int) else w[c]
                         ).then_inc(s_w[j], 16)
        for j in range(RING):
            load(j, j)
        with sp.Fori(1, NCHUNK // RING, 1) as it:
            for j in range(RING):
                sp.wait_ge(s_chunk, RING * it + (j + 1 - RING))
                load(j, RING * it + j)
        finish(sp)

    @block.gpsimd
    def _(pool):
        g = nc.gpsimd
        n = [0]

        def link(ins):
            n[0] += 1
            ins.then_inc(s_p, 1)
            pool.wait_ge(s_p, n[0])
        g.memset(ones[:, :], 1.0)
        g.memset(epsc[:, :], EPS)
        g.memset(rmask[:, :], 1.0)
        g.memset(ident[:, :], 0.0)
        link(g.memset(SEL, 0.0))
        rm = rmask[:, :].rearrange("p (h t) -> p h t", h=GH)
        for t in GSTART:
            g.memset(rm[:, :, t:t + 1], 0.0)
        g.affine_select(out=ident[:, :], in_=ident[:, :], compare_op=ALU.not_equal, fill=1.0, base=0,
                        pattern=[[-1, P]], channel_multiplier=1)
        v = SEL[0:ST].rearrange("p q (r c) -> p q r c", r=4)
        g.affine_select(out=v, in_=v, compare_op=ALU.not_equal, fill=1.0, base=0,
                        pattern=[[-4, 8], [-1, 4], [0, 32]], channel_multiplier=1)
        link(g.affine_select(out=cmask[:, :], in_=ones[:, :], compare_op=ALU.is_ge, fill=0.0, base=0,
                             pattern=[[1, P]], channel_multiplier=-1))
        g.memset(cmask[0:GCH, GCH:P], 0.0).then_inc(s_const, 1)
        pool.wait_ge(s_s5c, 32)
        flat2 = lambda v: v.rearrange("p j h -> p (j h)")
        g.tensor_scalar(flat2(CM[1]), flat2(CM[0]), -1.0, None, ALU.mult)
        g.tensor_scalar(flat2(CM[2]), flat2(CM[2]), -1.0, None, ALU.mult).then_inc(s_cn, 1)
        s5_pool()
        pool.wait_ge(s_og, 1)
        pool.wait_ge(s_hrt, 4)
        pool.dma_start(WKV, a["w_akv"]).then_inc(s_kv, 16)
        g.memset(NEGC, 0.0)
        g.memset(SELH, 0.0)
        link(g.memset(MASK3, 0.0))
        g.affine_select(out=NEGC, in_=NEGC, compare_op=ALU.is_ge, fill=NEG, base=0, pattern=[[1, P]],
                        channel_multiplier=-1)
        for b in (0, 2):
            g.affine_select(out=MASK3[:, b], in_=MASK3[:, b], compare_op=ALU.is_ge, fill=NEG, base=0,
                            pattern=[[-1, P]], channel_multiplier=1)
        g.affine_select(out=MASK3[:, 1], in_=MASK3[:, 1], compare_op=ALU.is_ge, fill=NEG, base=-1,
                        pattern=[[1, P]], channel_multiplier=-1)
        g.affine_select(out=SELH[0:MH], in_=SELH[0:MH], compare_op=ALU.not_equal, fill=1.0, base=0,
                        pattern=[[-1, MH], [0, P]], channel_multiplier=1).then_inc(s_c2, 1)
        pool.wait_ge(s_xoc, XH)
        pool.dma_start(SKT[:, 0], a["sub1"]).then_inc(s_sk, 16)
        pool.dma_start(SKT[:, 1], a["sub2"]).then_inc(s_sk, 16)
        pool.dma_start(GFIN, a["g_final"]).then_inc(s_sk, 16)
        g.iota(IOI, pattern=[[1, PTOP]], base=0, channel_multiplier=0).then_inc(s_io, 1)
        pool.wait_ge(s_io, 1)
        g.tensor_copy(IOTA, IOI).then_inc(s_io, 1)
        gathers_pool()

    @block.scalar
    def _(act):
        act.dma_start(AR[0:ST], a["a_re"]).then_inc(s_s5, 16)
        act.dma_start(AI[0:ST], a["a_im"]).then_inc(s_s5, 16)
        act.dma_start(LST[0:ST], a["log_step"]).then_inc(s_s5, 16)
        act.dma_start(walow[:, :, :], a["w_alow"]).then_inc(s_small, 16)
        act.dma_start(wgu[:, :], a["w_gate_up"]).then_inc(s_small, 16)
        act.dma_start(wif[:, :, :], a["w_if"]).then_inc(s_small, 16)
        act.dma_start(BR, a["b_re"]).then_inc(s_s5b, 16)
        act.dma_start(BI, a["b_im"]).then_inc(s_s5b, 16)
        act.dma_start(CM[0], a["c_re"]).then_inc(s_s5c, 16)
        act.dma_start(CM[2], a["c_im"]).then_inc(s_s5c, 16)
        n = [0]

        def link(ins):
            n[0] += 1
            ins.then_inc(s_a, 1)
            act.wait_ge(s_a, n[0])
        act.wait_ge(s_const, 1)
        norm_act(0, H, s_x, 16, T1)
        act.wait_ge(s_cols, 16)
        dense_act(FIRST["u"], 1, T1, evac(UU, ACT.Identity))
        dense_act(FIRST["qk"], 1, T1, evac(QK, ACT.Identity))
        gate_act(link)
        act.wait_ge(s_bd, 2)
        dense_act(FIRST["r"], 1, T1, evac(RR, ACT.Silu))
        dense_act(FIRST["zg"], 1, T1, evac(ZG, ACT.Sigmoid))
        dense_act(FIRST["zs"], 1, T1, evac(ZS, ACT.Sigmoid))
        for j in range(RING):
            v1_act(j)
        act.wait_ge(s_ye, 8)
        act.activation(YS, YS, ACT.Gelu_apprx_tanh).then_inc(s_gs, 1)
        gla_exp_act()
        glu_act(0)
        glu_act(1)
        gla_act_b()
        dense_act(FIRST["w_o_gla"], 1, T1, evac(RR, ACT.Identity))
        dense_act(FIRST["w_out"], 1, T1, evac(YS, ACT.Identity))
        norm_act(1, YS, s_dev, FIRST["w_out"] + 4, T1)
        norm_act(2, H, s_h, 1, T1)
        dense_act(FIRST["w_ff1"], 4, T1, evac(FFH, ACT.Relu))
        act.wait_ge(s_mix, 1)
        act.dma_start(MEM, a["memT"]).then_inc(s_mem, 16)
        norm_act(3, MEM, s_mem, 16, T2)
        ff2_act(ZS, T1)
        norm_act(4, ZS, s_dev, FIRST["w_ff2"] + 16, T1)
        for j in range(2):
            pair_act(FIRST["xk"], j, KX[:, 2 * j:2 * j + 2])
        norm_act(5, H2, s_h, 2, T2)
        for j in range(2, 4):
            pair_act(FIRST["xk"], j, KX[:, 2 * j:2 * j + 2])
        for j in range(4):
            tok_act(FIRST["xv"], j, XV[:, :, j * CW:(j + 1) * CW])
        for j in range(4):
            if j < 2:
                pair_act(FIRST["mqk_mo"], j, MQKP[:, 2 * j:2 * j + 2, 3:3 + T2])
            else:
                pair_act(FIRST["mqk_mo"], j, MO[:, 2 * j - 4:2 * j - 2], ACT.Sigmoid)
        small2_act(link)
        for j in range(2):
            pair_act(FIRST["aq_mv"], j, AQ[:, 2 * j:2 * j + 2])
        for j in range(2):
            tok_act(FIRST["aq_mv"], 2 + j, MVT[:, :, j * CW:(j + 1) * CW])
        act.wait_ge(s_conv, 1)
        act.activation(MQK[:, :, :], MQK[:, :, :], ACT.Silu).then_inc(s_silu, 1)
        mdecay_act()
        wexp_act(link)
        mnorm_act()
        wout_act()
        for j in range(4):
            pair_act(FIRST["w_out_2"], j, DEL[:, 2 * j:2 * j + 2])
        norm_act(6, H2, s_h, 3, T2)
        for j in range(4):
            pair_act(FIRST["xq"], j, QX[:, 2 * j:2 * j + 2])
        cross_act()
        for j in range(4):
            pair_act(FIRST["xo"], j, DEL[:, 2 * j:2 * j + 2])
        norm_act(7, H2, s_h, 4, T2)
        peer_act(link)

    @block.vector
    def _(dve):
        n = [0]

        def link(ins):
            n[0] += 1
            ins.then_inc(s_v, 1)
            dve.wait_ge(s_v, n[0])
        dve.wait_ge(s_cols, 16)
        norm_dve(0, H, s_x, 16, T1, "g_mix_pre", XN, link)
        s5_param_dve(link)
        dve.wait_ge(s_ltc, 1)
        dve.wait_ge(s_dev, FIRST["u"] + 4)
        s5_dve(link)
        gate_dve(link)
        gla_prep_dve(link)
        gla_dve_a(link)
        gla_dve_norm(link)
        dve.wait_ge(s_dev, FIRST["w_glu"] + 8)
        link(dve.tensor_tensor(UU, UU, EX, ALU.mult))
        link(dve.tensor_tensor(UU, UU, ZS, ALU.mult))
        dve.wait_ge(s_dev, FIRST["w_o_gla"] + 4)
        link(dve.tensor_tensor(RR, RR, ZG, ALU.mult))
        dve.tensor_tensor(RR, RR, UU, ALU.add).then_inc(s_mix, 1)
        postnorm_dve(1, YS, s_dev, FIRST["w_out"] + 4, T1, "g_mix_post", H, link)
        norm_dve(2, H, s_h, 1, T1, "g_ffn_pre", XN, link)

        def square(it):
            for j in range(RING):
                dve.wait_ge(s_dev, FIRST["w_ff1"] + 4 * it + (j + 1))
                v = FFH[:, bass.ds(8 * it + 2 * j, 2)]
                dve.tensor_tensor(v, v, v, ALU.mult).then_inc(s_ffh, 1)
        repeat(dve, 4, square)
        norm_dve(3, MEM, s_mem, 16, T2, "g_mem_2", MEM, link)
        postnorm_dve(4, ZS, s_dev, FIRST["w_ff2"] + 16, T1, "g_ffn_post", H, link)
        norm_dve(5, H2, s_h, 2, T2, "g_mix_2", XN2, link)
        link(dve.memset(MQKP[:, :, 0:3], 0.0))
        dve.wait_ge(s_dev, FIRST["mqk_mo"] + 2)
        conv_dve(link)
        mrows_dve(link)
        mdecay_dve()
        wsoft1_dve(link)
        mprod_dve()
        wsoft2_dve(link)
        mout_dve(link)
        mnorm_dve(link)
        dve.wait_ge(s_dev, FIRST["w_out_2"] + 4)
        dve.tensor_tensor(H2, H2, DEL, ALU.add).then_inc(s_h, 1)
        norm_dve(6, H2, s_h, 3, T2, "g_cross_2", XN2, link)
        cross_dve(link)
        dve.wait_ge(s_dev, FIRST["xo"] + 4)
        dve.tensor_tensor(H2, H2, DEL, ALU.add).then_inc(s_h, 1)
        norm_dve(7, H2, s_h, 4, T2, "g_ffn_2", XN2, link)
        peer_dve(link)

    @block.tensor
    def _(pe):
        pe.wait_ge(s_const, 1)
        norm_pe(0, T1)
        pe.wait_ge(s_xn, 1)
        dense_pe(FIRST["u"], 1, XN, T1)
        dense_pe(FIRST["qk"], 1, XN, T1)
        s5_param_pe()
        pe.wait_ge(s_ltc, 1)
        gate_pe()
        pe.wait_ge(s_gzc, GH)
        for i in range(16):
            if i < 12:
                chunk_pe(FIRST["r"], i, XN, T1)
            else:
                v1_pe(i - 12)
            for j in (2 * i, 2 * i + 1):
                s5_bu(j)
                if j >= 2:
                    s5_y(j - 2)
        s5_y(ST - 2)
        s5_y(ST - 1)
        pe.wait_ge(s_gs, 1)
        dense_pe(FIRST["w_glu"], 1, YS, T1)
        gla_pe_a()
        dense_pe(FIRST["w_glu"] + 4, 1, YS, T1)
        gla_pe_b()
        gla_pe_norm()
        pe.wait_ge(s_og, 1)
        dense_pe(FIRST["w_o_gla"], 1, QK, T1)
        pe.wait_ge(s_mix, 1)
        dense_pe(FIRST["w_out"], 1, RR, T1)
        norm_pe(1, T1)
        norm_pe(2, T1)
        pe.wait_ge(s_xn, 2)
        dense_pe(FIRST["w_ff1"], 4, XN, T1)
        norm_pe(3, T2)
        pe.wait_ge(s_ffh, 16)
        pe.wait_ge(s_xn, 3)
        ff2_pe(FFH, T1)
        for j in range(2):
            chunk_pe(FIRST["xk"], j, MEM, T2)
        norm_pe(4, T1)
        for j in range(2, 4):
            chunk_pe(FIRST["xk"], j, MEM, T2)
        norm_pe(5, T2)
        for j in range(4):
            tok_pe(FIRST["xv"], j, MEM)
        pe.wait_ge(s_xn, 4)
        for j in range(4):
            chunk_pe(FIRST["mqk_mo"], j, XN2, T2)
        small2_pe()
        for j in range(2):
            chunk_pe(FIRST["aq_mv"], j, XN2, T2)
        for j in range(2):
            tok_pe(FIRST["aq_mv"], 2 + j, XN2)
        mrows_pe()
        wscore_pe()
        mscore_pe()
        mnum_pe()
        mnorm_pe()
        wout_pe()
        pe.wait_ge(s_cat, 1)
        pe.wait_ge(s_woc, 4)
        for j in range(4):
            chunk_pe(FIRST["w_out_2"], j, CAT, T2)
        norm_pe(6, T2)
        pe.wait_ge(s_xn, 5)
        for j in range(4):
            chunk_pe(FIRST["xq"], j, XN2, T2)
        cross_pe()
        pe.wait_ge(s_xoc, XH)
        for j in range(4):
            chunk_pe(FIRST["xo"], j, OX, T2)
        norm_pe(7, T2)
        pe.wait_ge(s_xn, 6)
        peer_pe()

    ctx.close()


OUTS = None


def kernel(**inputs):
    import concourse.bacc as bacc
    from concourse.bass_utils import run_bass_kernel_spmd
    ins = layout({k: np.asarray(v) for k, v in inputs.items()})
    nc = bacc.Bacc("TRN2", target_bir_lowering=False, num_devices=1)
    args = {}
    for name, v in ins.items():
        args[name] = nc.dram_tensor("in_" + name, v.shape, mybir.dt.from_np(v.dtype), kind="ExternalInput").ap()
    args["out"] = nc.dram_tensor("out_0", (SEQ, D), F32, kind="ExternalOutput").ap()
    build(nc, args)
    r = run_bass_kernel_spmd(nc, [{"in_" + k: v for k, v in ins.items()}], core_ids=[0])
    return r.results[0]["out_0"].reshape(1, SEQ, D)
```
